# Optimizing a Trainium2 kernel written in Bass

```python
import math
import jax, jax.numpy as jnp
from jax import lax
import numpy as np

D_MODEL = 2048
BATCH = 1
SEQ = 512
DEPTH = 1

HEAD_DIM = 128
D_MIX = D_MODEL
D_CONV = D_MIX // 4
D_FOX = (3 * D_MIX) // 8
D_NSA = D_MIX - D_CONV - D_FOX
H_FOX = D_FOX // HEAD_DIM
H_NSA = D_NSA // HEAD_DIM
NSA_KV_HEADS = 2
NSA_GROUP = H_NSA // NSA_KV_HEADS
NSA_KV_DIM = NSA_KV_HEADS * HEAD_DIM
CONV_WIDTH = 3
Q_BLOCK = 128
CMP_LEN = 32
CMP_STRIDE = 16
CMP_HIDDEN = 256
SEL_LEN = 64
SEL_TOPK = 16
WINDOW = 512
REL_BUCKETS = 32
REL_MAX_DIST = 128
NORM_EPS = 1e-6
NEG_BIG = -1e30
FORCED_SCORE = 1e4
N_IN = 4 * D_CONV + 4 * D_FOX + H_FOX + 2 * D_NSA + 6 * NSA_KV_DIM + 3 * H_NSA

kernel_name = "hybrid_conv_fox_nsa_trunk"

def _split_sizes():
    return ([D_CONV] * 4
            + [D_FOX] * 3 + [H_FOX, D_FOX]
            + [D_NSA] + [NSA_KV_DIM] * 6
            + [3 * H_NSA, D_NSA])

def _split_columns(proj):
    pts, acc = [], 0
    for w in _split_sizes()[:-1]:
        acc += w
        pts.append(acc)
    return jnp.split(proj, pts, axis=-1)

def _rms_norm(x, g):
    xf = x.astype(jnp.float32)
    y = xf * lax.rsqrt(jnp.mean(xf * xf, axis=-1, keepdims=True) + NORM_EPS)
    return (y * g.astype(jnp.float32)).astype(x.dtype)

def _t5_bucket(dist):
    max_exact = REL_BUCKETS // 2
    n = jnp.maximum(dist, 0)
    nf = jnp.maximum(n, max_exact).astype(jnp.float32)
    large = max_exact + (jnp.log(nf / max_exact) / math.log(REL_MAX_DIST / max_exact)
                         * (REL_BUCKETS - max_exact)).astype(jnp.int32)
    return jnp.where(n < max_exact, n, jnp.minimum(large, REL_BUCKETS - 1))

def _short_conv(u, gate_b, gate_c, conv_w):
    y = gate_c * u
    s = y.shape[1]
    yp = jnp.pad(y, ((0, 0), (CONV_WIDTH - 1, 0), (0, 0)))
    z = sum(conv_w[j] * yp[:, j:j + s] for j in range(CONV_WIDTH))
    return gate_b * z

def _forgetting_attention(q, k, v, f_logit, b_f):
    b, s, h, _ = q.shape
    scale = HEAD_DIM ** -0.5
    log_f = jax.nn.log_sigmoid(f_logit.astype(jnp.float32) + b_f.astype(jnp.float32))
    cum = lax.cumsum(log_f, axis=1).swapaxes(1, 2)
    nb = s // Q_BLOCK
    qb = q.reshape(b, nb, Q_BLOCK, h, HEAD_DIM).swapaxes(0, 1)
    cq = cum.reshape(b, h, nb, Q_BLOCK).transpose(2, 0, 1, 3)
    kpos = jnp.arange(s)

    def block(args):
        i, qi, ci = args
        qpos = i * Q_BLOCK + jnp.arange(Q_BLOCK)
        sc = jnp.einsum('bqhd,bkhd->bhqk', qi, k, preferred_element_type=jnp.float32) * scale
        sc = sc + ci[..., :, None] - cum[:, :, None, :]
        sc = jnp.where(kpos[None, :] <= qpos[:, None], sc, -jnp.inf)
        p = jax.nn.softmax(sc, axis=-1)
        return jnp.einsum('bhqk,bkhd->bqhd', p.astype(v.dtype), v)

    out = lax.map(block, (jnp.arange(nb), qb, cq))
    return out.swapaxes(0, 1).reshape(b, s, h * HEAD_DIM)

def _compress(kv, pe, w1, w2, blk_idx):
    b, _, g, _ = kv.shape
    n = blk_idx.shape[0]
    blocks = kv[:, blk_idx] + pe[:, None, :]
    flat = blocks.transpose(0, 1, 3, 2, 4).reshape(b, n, g, CMP_LEN * HEAD_DIM)
    return jax.nn.silu(flat @ w1) @ w2

def _native_sparse_attention(q, kc, vc, ks, vs, kw, vw, g_logit,
                             pe_k, w1_k, w2_k, pe_v, w1_v, w2_v, rel_bias):
    b, s = q.shape[:2]
    g_, r_ = NSA_KV_HEADS, NSA_GROUP
    scale = HEAD_DIM ** -0.5
    q = q.reshape(b, s, g_, r_, HEAD_DIM)
    kc, vc, ks, vs, kw, vw = [t.reshape(b, s, g_, HEAD_DIM) for t in (kc, vc, ks, vs, kw, vw)]

    n_cmp = (s - CMP_LEN) // CMP_STRIDE + 1
    blk_idx = np.arange(n_cmp)[:, None] * CMP_STRIDE + np.arange(CMP_LEN)[None, :]
    cmp_end = jnp.asarray(blk_idx[:, -1], dtype=jnp.int32)
    k_cmp = _compress(kc, pe_k, w1_k, w2_k, blk_idx)
    v_cmp = _compress(vc, pe_v, w1_v, w2_v, blk_idx)

    n_sel = s // SEL_LEN
    k_top = min(SEL_TOPK, n_sel)
    sel_start = np.arange(n_sel) * SEL_LEN
    c_lo = np.arange(n_cmp)[:, None] * CMP_STRIDE
    overlap = (c_lo < sel_start[None, :] + SEL_LEN) & (c_lo + CMP_LEN > sel_start[None, :])
    cmp_to_sel = jnp.asarray(overlap, dtype=jnp.float32)
    ks_blk = ks.reshape(b, n_sel, SEL_LEN, g_, HEAD_DIM).transpose(0, 3, 1, 2, 4)
    vs_blk = vs.reshape(b, n_sel, SEL_LEN, g_, HEAD_DIM).transpose(0, 3, 1, 2, 4)

    kw_pad = jnp.pad(kw, ((0, 0), (WINDOW, 0), (0, 0), (0, 0)))
    vw_pad = jnp.pad(vw, ((0, 0), (WINDOW, 0), (0, 0), (0, 0)))

    bias_tab = rel_bias.reshape(REL_BUCKETS, g_, r_).transpose(1, 2, 0)
    gates = jax.nn.sigmoid(g_logit.astype(jnp.float32)).reshape(b, s, g_, r_, 3)
    nb = s // Q_BLOCK
    qb = q.reshape(b, nb, Q_BLOCK, g_, r_, HEAD_DIM).swapaxes(0, 1)
    gb = gates.reshape(b, nb, Q_BLOCK, g_, r_, 3).swapaxes(0, 1)
    bidx = jnp.arange(b)[:, None, None, None]
    gidx = jnp.arange(g_)[None, :, None, None]
    g6 = jnp.arange(g_)[None, :, None, None, None, None]
    r6 = jnp.arange(r_)[None, None, :, None, None, None]
    sel_j = jnp.arange(n_sel)

    def block(args):
        i, qi, gi = args
        qpos = i * Q_BLOCK + jnp.arange(Q_BLOCK)

        s_c = jnp.einsum('bqgrd,bngd->bgrqn', qi, k_cmp, preferred_element_type=jnp.float32) * scale
        s_c = s_c + bias_tab[:, :, _t5_bucket(qpos[:, None] - cmp_end[None, :])]
        mask_c = cmp_end[None, :] <= qpos[:, None]
        p_c = jax.nn.softmax(jnp.where(mask_c, s_c, NEG_BIG), axis=-1)
        p_c = jnp.where(jnp.any(mask_c, axis=-1)[:, None], p_c, 0.0)
        o_c = jnp.einsum('bgrqn,bngd->bqgrd', p_c.astype(v_cmp.dtype), v_cmp)

        imp = jnp.einsum('bgrqn,nm->bgqm', p_c, cmp_to_sel)
        own = qpos // SEL_LEN
        eligible = sel_j[None, :] * SEL_LEN <= qpos[:, None]
        forced = ((sel_j[None, :] == 0) | (sel_j[None, :] == own[:, None])
                  | (sel_j[None, :] == own[:, None] - 1))
        score = jnp.where(eligible, jnp.where(forced, FORCED_SCORE, imp), -1.0)
        top_val, top_idx = lax.top_k(score, k_top)
        k_sel = ks_blk[bidx, gidx, top_idx]
        v_sel = vs_blk[bidx, gidx, top_idx]
        pos_sel = top_idx[..., None] * SEL_LEN + jnp.arange(SEL_LEN)
        dist_s = qpos[None, None, :, None, None] - pos_sel
        mask_s = (dist_s >= 0) & (top_val >= 0.0)[..., None]
        s_s = jnp.einsum('bqgrd,bgqkld->bgrqkl', qi, k_sel, preferred_element_type=jnp.float32) * scale
        s_s = s_s + bias_tab[g6, r6, _t5_bucket(dist_s)[:, :, None]]
        s_s = jnp.where(mask_s[:, :, None], s_s, NEG_BIG).reshape(b, g_, r_, Q_BLOCK, k_top * SEL_LEN)
        p_s = jax.nn.softmax(s_s, axis=-1).reshape(b, g_, r_, Q_BLOCK, k_top, SEL_LEN)
        o_s = jnp.einsum('bgrqkl,bgqkld->bqgrd', p_s.astype(v_sel.dtype), v_sel)

        k_win = lax.dynamic_slice_in_dim(kw_pad, i * Q_BLOCK, WINDOW + Q_BLOCK, axis=1)
        v_win = lax.dynamic_slice_in_dim(vw_pad, i * Q_BLOCK, WINDOW + Q_BLOCK, axis=1)
        kpos = i * Q_BLOCK - WINDOW + jnp.arange(WINDOW + Q_BLOCK)
        dist_w = qpos[:, None] - kpos[None, :]
        mask_w = (dist_w >= 0) & (dist_w < WINDOW) & (kpos[None, :] >= 0)
        s_w = jnp.einsum('bqgrd,bkgd->bgrqk', qi, k_win, preferred_element_type=jnp.float32) * scale
        s_w = s_w + bias_tab[:, :, _t5_bucket(dist_w)]
        p_w = jax.nn.softmax(jnp.where(mask_w, s_w, NEG_BIG), axis=-1)
        o_w = jnp.einsum('bgrqk,bkgd->bqgrd', p_w.astype(v_win.dtype), v_win)

        out = gi[..., 0:1] * o_c + gi[..., 1:2] * o_s + gi[..., 2:3] * o_w
        return out.astype(qi.dtype)

    out = lax.map(block, (jnp.arange(nb), qb, gb))
    return out.swapaxes(0, 1).reshape(b, s, H_NSA * HEAD_DIM)

def setup_inputs(seed: int = 0) -> dict:
    key = jax.random.key(seed)
    ks = jax.random.split(key, 18)
    f32 = jnp.float32

    def nrm(k, shape, sc):
        return jax.random.normal(k, shape, f32) * sc

    flat_cmp = CMP_LEN * HEAD_DIM
    return {
        'x': nrm(ks[0], (BATCH, SEQ, D_MODEL), 1.0),
        'c': nrm(ks[1], (BATCH, D_MODEL), 1.0),
        'w_ada': nrm(ks[2], (DEPTH, D_MODEL, 3 * D_MODEL), 0.5 * D_MODEL ** -0.5),
        'b_ada': nrm(ks[3], (DEPTH, 3 * D_MODEL), 0.02),
        'pre_norm': 1.0 + nrm(ks[4], (DEPTH, D_MODEL), 0.05),
        'post_norm': 1.0 + nrm(ks[5], (DEPTH, D_MODEL), 0.05),
        'w_in': nrm(ks[6], (DEPTH, D_MODEL, N_IN), D_MODEL ** -0.5),
        'b_forget': jax.random.uniform(ks[7], (DEPTH, H_FOX), f32, 1.0, 4.0),
        'conv_w': nrm(ks[8], (DEPTH, CONV_WIDTH, D_CONV), CONV_WIDTH ** -0.5),
        'cmp_pe_k': nrm(ks[9], (DEPTH, CMP_LEN, HEAD_DIM), 0.5),
        'cmp_w1_k': nrm(ks[10], (DEPTH, flat_cmp, CMP_HIDDEN), flat_cmp ** -0.5),
        'cmp_w2_k': nrm(ks[11], (DEPTH, CMP_HIDDEN, HEAD_DIM), 2.0 * CMP_HIDDEN ** -0.5),
        'cmp_pe_v': nrm(ks[12], (DEPTH, CMP_LEN, HEAD_DIM), 0.5),
        'cmp_w1_v': nrm(ks[13], (DEPTH, flat_cmp, CMP_HIDDEN), flat_cmp ** -0.5),
        'cmp_w2_v': nrm(ks[14], (DEPTH, CMP_HIDDEN, HEAD_DIM), 2.0 * CMP_HIDDEN ** -0.5),
        'w_out': nrm(ks[15], (DEPTH, D_MIX, D_MODEL), D_MIX ** -0.5),
        'rel_bias': nrm(ks[16], (REL_BUCKETS, H_NSA), 0.5),
    }

def reference(x, c, w_ada, b_ada, pre_norm, post_norm, w_in, b_forget, conv_w,
              cmp_pe_k, cmp_w1_k, cmp_w2_k, cmp_pe_v, cmp_w1_v, cmp_w2_v, w_out, rel_bias):
    b, s, _ = x.shape
    c_act = jax.nn.silu(c)
    for l in range(DEPTH):
        mod = c_act @ w_ada[l] + b_ada[l]
        shift, scale, gate = jnp.split(mod, 3, axis=-1)
        h = _rms_norm(x, pre_norm[l]) * (1.0 + scale[:, None]) + shift[:, None]

        proj = h @ w_in[l]
        (u_a, gb_a, gc_a, z_a,
         q_f, k_f, v_f, f_f, z_f,
         q_n, kc_n, vc_n, ks_n, vs_n, kw_n, vw_n, g_n, z_n) = _split_columns(proj)

        y_a = _short_conv(u_a, gb_a, gc_a, conv_w[l])
        y_f = _forgetting_attention(q_f.reshape(b, s, H_FOX, HEAD_DIM),
                                    k_f.reshape(b, s, H_FOX, HEAD_DIM),
                                    v_f.reshape(b, s, H_FOX, HEAD_DIM),
                                    f_f, b_forget[l])
        y_n = _native_sparse_attention(q_n, kc_n, vc_n, ks_n, vs_n, kw_n, vw_n, g_n,
                                       cmp_pe_k[l], cmp_w1_k[l], cmp_w2_k[l],
                                       cmp_pe_v[l], cmp_w1_v[l], cmp_w2_v[l], rel_bias)

        y = jnp.concatenate([y_a * jax.nn.silu(z_a),
                             y_f * jax.nn.silu(z_f),
                             y_n * jax.nn.silu(z_n)], axis=-1) @ w_out[l]
        x = x + gate[:, None] * _rms_norm(y, post_norm[l])
    return x


_drawn_inputs = setup_inputs


def setup_inputs(seed=0):
    import zlib

    import numpy as np

    out = dict(_drawn_inputs(seed))
    spreads = {}
    factors = {'post_norm': 3.658, 'cmp_pe_k': 3.112}
    for name, (base, spread) in spreads.items():
        noise = np.random.default_rng([zlib.crc32(name.encode()), seed]).standard_normal(out[name].shape)
        drawn = base * np.exp(spread * noise) if base else spread * noise
        out[name] = __import__('jax').numpy.asarray(drawn.astype(out[name].dtype))
    for name, factor in factors.items():
        out[name] = (out[name] * factor).astype(out[name].dtype)
    return out
```

```python
from contextlib import ExitStack

import numpy as np

import concourse.bass as bass
from concourse import mybir

F32 = mybir.dt.float32
F32R = mybir.dt.float32r
ALU = mybir.AluOpType
ACT = mybir.ActivationFunctionType
AX = mybir.AxisListType

P = 128
D = 2048
S = 512
KT = D // P
ST = S // P
HD = 128
D_CONV = D // 4
D_FOX = 3 * D // 8
D_NSA = D - D_CONV - D_FOX
HF = D_FOX // HD
HN = D_NSA // HD
KVG = 2
CT = D_CONV // P
CW = 3
CMP_LEN, CMP_STRIDE, CMP_HID = 32, 16, 256
NC = (S - CMP_LEN) // CMP_STRIDE + 1
BUCKETS, MAX_DIST = 32, 128
EPS = 1e-6
NEG = -1e30
SCALE = HD ** -0.5

U_A = 0
GB_A, GC_A, Z_A = D_CONV, 2 * D_CONV, 3 * D_CONV
Q_F = 4 * D_CONV
K_F, V_F = Q_F + D_FOX, Q_F + 2 * D_FOX
F_F = Q_F + 3 * D_FOX
Z_F = F_F + HF
Q_N = Z_F + D_FOX
KV = KVG * HD
KC, VC, KS, VS, KW, VW = (Q_N + D_NSA + i * KV for i in range(6))
G_N = VW + KV
Z_N = G_N + 3 * HN
N_IN = Z_N + D_NSA

R_C, R_PRE, R_ADA, R_CONV, R_POST = 0, KT, 2 * KT, 5 * KT, 5 * KT + CW * CT
R_ALL = R_POST + KT

PANEL = [(V_F, 512, 0), (V_F + 512, D_FOX + HF - 512, 512), (VS, KV, D_FOX + HF),
         (VW, KV + 3 * HN, D_FOX + HF + KV)]
PW = sum(n for _, n, _ in PANEL)
PF, PVS, PVW, PG = D_FOX, D_FOX + HF, D_FOX + HF + KV, D_FOX + HF + 2 * KV

SLOT = 1120
NRAW, NSPLIT, NADA = 4, 4, 4
VEC = S + P

SW = [(b + 1) * P for b in range(ST)]
SO = [sum(SW[:b]) for b in range(ST)]
SALL = sum(SW)
TW = [S - k * P for k in range(ST)]
TO = [sum(TW[:k]) for k in range(ST)]


def tiles_and_jobs():
    conv = [(kind, i) for i in range(CT) for kind in ("u", "gc", "gb", "za")]
    tiles = [("kw", 0), ("kw", 1), conv.pop(0), conv.pop(0)]
    jobs = []
    for g in range(HN):
        b = len(tiles)
        tiles += [("qn", g), ("zn", g), ("qf", g), ("kf", g), ("zf", g), conv.pop(0), conv.pop(0)]
        jobs += [("sel", g, b + 1), ("win", g, b + 3), ("fox", g, b + 5)]
    return tiles + conv, jobs


TILES, JOBS = tiles_and_jobs()
NT = len(TILES)
CMP_TILES, CMP_PER = 4, 4
LATE = 8
OUT_ORDER = [k for k in range(KT) if k != CT - 1] + [CT - 1]
COL0 = {"kw": KW, "qn": Q_N, "zn": Z_N, "qf": Q_F, "kf": K_F, "zf": Z_F,
        "u": U_A, "gc": GC_A, "gb": GB_A, "za": Z_A}


def weight_units():
    units = [("first", (k,), KV * 3) for k in range(KT)]
    for b, (_, n, _) in enumerate(PANEL):
        step = 2 if n > 280 else 4
        units += [("panel", (b, k, step), step * n) for k in range(0, KT, step)]
    at, half_at, cmp_at = [], {}, {}
    for t in range(NT):
        at.append(len(units))
        for h in range(2):
            half_at[t, h] = len(units)
            units.append(("tile", (t, h), KT // 2 * P))
            if t < CMP_TILES:
                for i in range(CMP_PER // 2):
                    q = CMP_PER * t + CMP_PER // 2 * h + i
                    cmp_at[q] = len(units)
                    units.append(("cmp", (q,), 4 * CMP_HID))
    at.append(len(units))
    units += [("out", (n, k), D // 2) for n in range(2) for k in OUT_ORDER]
    return units, at, half_at, cmp_at


UNITS, AT, HALF_AT, CMP_AT = weight_units()
NU = len(UNITS)
FIRST_LATE = NU - LATE
N_FIRST = KT
N_PANEL = AT[0] - N_FIRST


def layer_program(nc, x, c, w_ada, b_ada, pre_norm, post_norm, w_in, b_forget, conv_w,
                  pe_k, w1_k, w2_k, pe_v, w1_v, w2_v, w_out, rel_bias, consts, onehot, out):
    ctx = ExitStack()
    with ctx:
        top = [ctx.enter_context(nc.sbuf_tensor("arena", [P, 56960], F32))]
        base = 1152
        place = {}

        def at(name, shape, dt, offset):
            place[name] = offset + 4 * int(np.prod(shape[1:]))
            assert place[name] <= base + 4 * 56960, (name, place[name])
            return nc.alloc_sbuf_tensor_at(name, shape, dt, offset=offset)

        def row(names, offset):
            made = []
            for name, shape, dt in names:
                made.append(at(name, shape, dt, offset))
                offset = -(-place[name] // 32) * 32
            return made, offset

        (h_hi, h_lo), o = row([("h_hi", [P, KT, S], F32R), ("h_lo", [P, KT, S], F32R)], base)
        xT = at("xT", [P, KT, S], F32, base + 4 * KT * S)
        (w_raw, w_hi, w_lo), o2 = row([("w_raw", [P, NRAW, SLOT], F32),
                                       ("w_hi", [P, NSPLIT, SLOT], F32R),
                                       ("w_lo", [P, NSPLIT, SLOT], F32R)], o)
        x_again = at("x_again", [P, 2, D], F32, o)
        fin = at("fin", [P, 2, D], F32, o + 4 * NRAW * SLOT)
        shared = o2
        (yT, vals, prob, probT, dbias), o3 = row(
            [("yT", [P, KT, S], F32), ("vals", [P, ST, PW], F32), ("prob", [P, SALL], F32),
             ("probT", [P, SALL], F32), ("dbias", [P, SALL], F32)], shared)
        ada = at("ada", [P, NADA, 4, S], F32, shared)
        x_sb = at("x_sb", [P, ST, D], F32, shared + 4 * KT * S)
        o_prob = shared + 4 * KT * S + 4 * ST * PW
        o_prob = -(-o_prob // 32) * 32
        (kvc, blk, blk_hi, blk_lo, hidT), oc = row(
            [("kvc", [P, 4, S], F32), ("blk", [P, 4, 2 * NC], F32),
             ("blk_hi", [P, 2, 4, 66], F32R), ("blk_lo", [P, 2, 4, 66], F32R),
             ("hidT", [P, 2, 2, 2 * NC], F32)], o_prob)
        assert oc <= o3
        late_hi = at("late_hi", [P, LATE, D // 2], F32R, shared)
        late_lo = at("late_lo", [P, LATE, D // 2], F32R, shared + 4 * LATE * D // 2)
        assert shared + 8 * LATE * D // 2 <= o3
        mid = o3
        (ks, kw, qn, qf, kf, bias_t, u_sb, conv_y, conv_z, e_sb, pcT, sq_out), o4 = row(
            [("ks", [P, KVG, S], F32), ("kw", [P, KVG, S], F32), ("qn", [P, S], F32),
             ("qf", [P, S], F32), ("kf", [P, S], F32), ("bias_t", [P, 2, S], F32),
             ("u_sb", [P, S], F32), ("conv_y", [P, CW - 1 + S], F32), ("conv_z", [P, S], F32),
             ("e_sb", [P, S], F32), ("pcT", [NC, S], F32), ("sq_out", [P, S], F32)], mid)
        (g_bc, y_half), o5 = row([("g_bc", [P, D], F32), ("y_half", [P, ST, D // 2], F32)], mid)
        assert o5 <= o4
        acc = at("acc", [P, 2, S], F32, mid + 4 * 2 * KVG * S)
        hid = at("hid", [2 * NC, 2, CMP_HID], F32, -(-place["pcT"] // 32) * 32)
        oneh = at("oneh", [BUCKETS, S], F32, place["qf"] + 4 * S + 2 * 4 * S)
        (vec, rows_a, rows_b), _ = row([("vec", [HN, VEC], F32), ("rows_a", [R_ALL, P], F32),
                                        ("rows_b", [2 * CMP_LEN, P], F32)], -(-place["conv_y"] // 32) * 32)
        assert place["rows_b"] <= place["pcT"]
        xmix = at("xmix", [P, 2, S], F32, -(-place["qf"] // 32) * 32)
        (cst, rel, cols_a, pe_cols, c_act, c_tmp, gate_col, mod_sc, mod_sh,
         stat, rstd, w2, eps_c, one_c, cum, fl, fe, gate, bf, ssum, nmx, mx, rr, bias_c, pc,
         kcmp, vcmp, sq, tot, rs2, rs3, b1), o6 = row(
            [("cst", [P, 3 * P + 1], F32), ("rel", [BUCKETS, HN], F32),
             ("cols_a", [P, R_ALL], F32), ("pe_cols", [P, 2, CMP_LEN], F32),
             ("c_act", [P, KT], F32), ("c_tmp", [P, KT], F32), ("gate_col", [P, KT], F32),
             ("mod_sc", [P, KT], F32), ("mod_sh", [P, KT], F32), ("stat", [P, ST], F32),
             ("rstd", [P, ST], F32), ("w2", [P, 2, 2, HD], F32),
             ("eps_c", [P, 1], F32), ("one_c", [P, 1], F32), ("cum", [P, ST, HF], F32),
             ("fl", [P, ST, HF], F32), ("fe", [P, ST, HF], F32), ("gate", [P, ST, 3 * HN], F32),
             ("bf", [P, HF], F32), ("ssum", [P, ST], F32), ("nmx", [P, ST], F32),
             ("mx", [P, ST], F32), ("rr", [P, ST], F32), ("bias_c", [P, ST, NC], F32),
             ("pc", [P, ST, NC], F32), ("kcmp", [P, 2 * NC], F32),
             ("vcmp", [NC, KVG, HD], F32), ("sq", [P, ST, 3], F32), ("tot", [P, ST], F32),
             ("rs2", [P, ST], F32), ("rs3", [P, ST], F32), ("b1", [P, KT], F32)], o4)
        ident, tri, ones, anym = (cst[:, 0:P], cst[:, P:2 * P], cst[:, 2 * P:3 * P],
                                  cst[:, 3 * P:3 * P + 1])
        t5_dram = nc.dram_tensor("t5_rows", [HN, VEC], F32, kind="Internal").ap()
        t5_wide = nc.dram_tensor("t5_wide", [HN, P, VEC], F32, kind="Internal").ap()

        bank = [ctx.enter_context(nc.psum_tensor(f"bank{i}", [P, S], F32)) for i in range(8)]
        ACC = [bank[2], bank[3]]
        SB = [bank[6], bank[6], bank[5], bank[4]]
        SBO = [0, SW[0], 0, 0]
        SC = bank[6][:, SW[0] + SW[1]:SW[0] + SW[1] + ST * NC]
        T0, T1, OB = bank[0], bank[1], bank[7]
        YB = [bank[i] for i in (1, 2, 7, 3, 4, 5, 6, 0)]

        def sem(name):
            return ctx.enter_context(nc.semaphore(name))

        rows_in, const_in, misc_in, t5_out = (sem(n) for n in ("rows_in", "const_in", "misc_in", "t5_out"))
        x_in = [sem(f"x_in{i}") for i in range(ST)]
        raw_in = [sem(f"raw_in{i}") for i in range(NRAW)]
        ada_in = [sem(f"ada_in{i}") for i in range(NADA)]
        bias_in = [sem(f"bias_in{i}") for i in range(2)]
        xa_in = [sem(f"xa_in{i}") for i in range(2)]
        stored = [sem(f"stored{i}") for i in range(2)]
        rows_T, t5_mm, xT_mm, mod_mm, unit_used = (
            sem(n) for n in ("rows_T", "t5_mm", "xT_mm", "mod_mm", "unit_used"))
        cum_mm, cumb_mm, s_mm, t_mm, o_mm = (
            sem(n) for n in ("cum_mm", "cumb_mm", "s_mm", "t_mm", "o_mm"))
        hidT_mm, kvcmp_mm, gb_mm, y_mm = (sem(n) for n in ("hidT_mm", "kvcmp_mm", "gb_mm", "y_mm"))
        act_seq, hi_done, xT_act, first_act, val_act, tile_act = (
            sem(n) for n in ("act_seq", "hi_done", "xT_act", "first_act", "val_act", "tile_act"))
        c_exp, x_sq, x_std, gate_exp, f_exp, f_ln, z_exp, hid_exp = (
            sem(n) for n in ("c_exp", "x_sq", "x_std", "gate_exp", "f_exp", "f_ln", "z_exp", "hid_exp"))
        p_exp, pc_exp, pT_act, d_act, yh_hi, y_act, y_sq, y_std, gb_act, kc_act = (
            sem(n) for n in ("p_exp", "pc_exp", "pT_act", "d_act", "yh_hi", "y_act", "y_sq", "y_std",
                             "gb_act", "kc_act"))
        dve_seq, lo_done, ada_used, acc_done, xn_done, xT_dve, first_dve, val_dve, tile_dve = (
            sem(n) for n in ("dve_seq", "lo_done", "ada_used", "acc_done", "xn_done", "xT_dve",
                             "first_dve", "val_dve", "tile_dve"))
        cols_done, c_done, vec_done, mod_read, h_ready, stat_v, f_abs, logf_done, cum_done = (
            sem(n) for n in ("cols_done", "c_done", "vec_done", "mod_read", "h_ready", "stat_v",
                             "f_abs", "logf_done", "cum_done"))
        nmx_done, sc_sub, p_done, pc_done, pT_dve, pcT_dve, o_done = (
            sem(n) for n in ("nmx_done", "sc_sub", "p_done", "pc_done", "pT_dve", "pcT_dve", "o_done"))
        hid_done, hidT_done, kvcmp_done, y_ready, y_dve, y_tot, gb_done, fin_done = (
            sem(n) for n in ("hid_done", "hidT_done", "kvcmp_done", "y_ready", "y_dve", "y_tot",
                             "gb_done", "fin_done"))
        mod_done, h_full, h_rounded, yh_sq = (sem(n) for n in ("mod_done", "h_full", "h_rounded", "yh_sq"))
        first_lo, yg_done = sem("first_lo"), sem("yg_done")
        pool_seq, blk_done, d_done, bias_c_done = (
            sem(n) for n in ("pool_seq", "blk_done", "d_done", "bias_c_done"))

        block = ctx.enter_context(nc.Block())

        ON_ACT = ("kw", "qn", "qf", "kf", "u")
        taken, n_act, n_dve = [], 0, 0
        for kind, _ in TILES:
            if kind in ON_ACT:
                n_act += 1
                taken.append((tile_act, n_act))
            else:
                n_dve += 1
                taken.append((tile_dve, n_dve))
        index = {name: t for t, name in enumerate(TILES)}
        z_order = [t for t, (kind, _) in enumerate(TILES) if kind in ("zn", "zf", "za")]

        def y_of(kind, i):
            return {"za": i, "zf": CT + i, "zn": CT + HF + i}[kind]

        def lo_of(u):
            return (first_lo, u + 1) if u < N_FIRST else (lo_done, u + 1 - N_FIRST)

        def split(u):
            n = UNITS[u][2]
            if u >= FIRST_LATE:
                return late_hi[:, u - FIRST_LATE, :], late_lo[:, u - FIRST_LATE, :]
            return w_hi[:, u % NSPLIT, 0:n], w_lo[:, u % NSPLIT, 0:n]

        @block.sync
        def _(sp):
            sp.dma_start(rows_a[R_C:R_C + KT, :], c.rearrange("o (k p) -> (o k) p", p=P)).then_inc(rows_in, 16)
            sp.dma_start(rows_a[R_PRE:R_PRE + KT, :], pre_norm.rearrange("o (k p) -> (o k) p", p=P)).then_inc(rows_in, 16)
            sp.dma_start(rows_a[R_ADA:R_ADA + 3 * KT, :], b_ada.rearrange("o (k p) -> (o k) p", p=P)).then_inc(rows_in, 16)
            sp.dma_start(rows_a[R_CONV:R_CONV + CW * CT, :], conv_w.rearrange("o j (k p) -> (o j k) p", p=P)).then_inc(rows_in, 16)
            sp.dma_start(rows_a[R_POST:R_POST + KT, :], post_norm.rearrange("o (k p) -> (o k) p", p=P)).then_inc(rows_in, 16)
            sp.dma_start(rows_b[0:CMP_LEN, :], pe_k[0]).then_inc(rows_in, 16)
            sp.dma_start(rows_b[CMP_LEN:2 * CMP_LEN, :], pe_v[0]).then_inc(rows_in, 16)
            sp.dma_start(cst[:, :], consts).then_inc(const_in, 16)

            def ada_unit(n):
                chunk, q = n // 4, n % 4
                if n >= NADA:
                    sp.wait_ge(ada_used, n - NADA + 1)
                rows = w_ada[0, q * S:(q + 1) * S, :].rearrange("(k p) n -> p k n", p=P)
                if chunk < D // 256:
                    for half in range(2):
                        sp.dma_start(ada[:, n % NADA, :, half * 256:(half + 1) * 256],
                                     rows[:, :, half * D + chunk * 256:half * D + (chunk + 1) * 256]
                                     ).then_inc(ada_in[n % NADA], 16)
                else:
                    c0 = 2 * D + (chunk - D // 256) * S
                    sp.dma_start(ada[:, n % NADA, :, :], rows[:, :, c0:c0 + S]).then_inc(ada_in[n % NADA], 32)

            def weight_unit(u):
                kind, where, n = UNITS[u]
                if u >= NRAW:
                    sp.wait_ge(*lo_of(u - NRAW))
                dst = w_raw[:, u % NRAW, 0:n]
                if kind == "first":
                    src = w_in[0, where[0] * P:(where[0] + 1) * P, KC:KC + 3 * KV]
                elif kind == "panel":
                    b, k, step = where
                    c0, w, _ = PANEL[b]
                    dst = dst.rearrange("p (k n) -> p k n", k=step)
                    src = w_in[0, k * P:(k + step) * P, c0:c0 + w].rearrange("(k p) n -> p k n", p=P)
                elif kind == "tile":
                    (name, i), half = TILES[where[0]], where[1]
                    c0, n_k = COL0[name] + i * P, KT // 2
                    dst = dst.rearrange("p (k n) -> p k n", k=n_k)
                    src = w_in[0, half * n_k * P:(half + 1) * n_k * P, c0:c0 + P].rearrange(
                        "(k p) n -> p k n", p=P)
                elif kind == "cmp":
                    w1, q = (w1_k, w1_v)[where[0] // 8], where[0] % 8
                    dst = dst.rearrange("p (k n) -> p k n", k=4)
                    src = w1[0, q * S:(q + 1) * S, :].rearrange("(k p) n -> p k n", p=P)
                else:
                    half, k = where
                    src = w_out[0, k * P:(k + 1) * P, half * D // 2:(half + 1) * D // 2]
                sp.dma_start(dst, src).then_inc(raw_in[u % NRAW], 16)

            for chunk in range(D // 256):
                for q in range(4):
                    ada_unit(4 * chunk + q)
                if chunk == 0:
                    for s in range(ST):
                        sp.dma_start(x_sb[:, s, :], x[0, s * P:(s + 1) * P, :]).then_inc(x_in[s], 16)
                    sp.dma_start(oneh[:, :], onehot).then_inc(misc_in, 16)
                    sp.dma_start(rel[:, :], rel_bias).then_inc(misc_in, 16)
                    sp.dma_start(bf[:, :], b_forget.broadcast_to([P, HF])).then_inc(misc_in, 16)
                    sp.dma_start(w2[:, 0, :, :], w2_k[0].rearrange("(k p) n -> p k n", p=P)).then_inc(misc_in, 16)
                    sp.dma_start(w2[:, 1, :, :], w2_v[0].rearrange("(k p) n -> p k n", p=P)).then_inc(misc_in, 16)
                weight_unit(2 * chunk)
                weight_unit(2 * chunk + 1)
            sp.wait_ge(vec_done, 1)
            sp.dma_start(t5_dram, vec[:, :]).then_inc(t5_out, 16)
            for i in range(N_PANEL):
                weight_unit(N_FIRST + i)
                if i < 16:
                    ada_unit(4 * (D // 256) + i)
                if i == 2:
                    sp.wait_ge(t5_out, 16)
                    sp.dma_start(t5_wide, bass.AP(tensor=t5_dram.tensor, offset=0,
                                                  ap=[[VEC, HN], [0, P], [1, VEC]])).then_inc(t5_out, 16)
            sp.wait_ge(t5_out, 32)

            def bias_load(h):
                if h >= 2:
                    sp.wait_ge(nmx_done, 3 * (h - 2) + 2)
                    sp.wait_ge(bias_c_done, h - 1)
                src = bass.AP(tensor=t5_wide.tensor, offset=h * P * VEC + P - 1, ap=[[VEC - 1, P], [1, S]])
                sp.dma_start(bias_t[:, h % 2, :], src).then_inc(bias_in[h % 2], 16)

            bias_load(0)
            for t in range(NT):
                if (t + 2) % 7 == 0 and (t + 2) // 7 < HN:
                    bias_load((t + 2) // 7)
                for u in range(AT[t], AT[t + 1]):
                    weight_unit(u)
            for u in range(AT[NT], NU):
                weight_unit(u)
            sp.wait_ge(*lo_of(NU - 1))
            for s in range(2):
                sp.dma_start(x_again[:, s, :], x[0, s * P:(s + 1) * P, :]).then_inc(xa_in[s], 16)
            for s in range(ST):
                for half in range(2):
                    cs = slice(half * D // 2, (half + 1) * D // 2)
                    sp.wait_ge(fin_done, 2 * s + half + 1)
                    sp.dma_start(out[0, s * P:(s + 1) * P, cs], fin[:, s % 2, cs]).then_inc(stored[s % 2], 16)
                if s + 2 < ST:
                    sp.dma_start(x_again[:, s % 2, :], x[0, (s + 2) * P:(s + 3) * P, :]).then_inc(xa_in[s % 2], 16)
            for i in range(2):
                sp.wait_ge(stored[i], 32 * (ST // 2))

        @block.tensor
        def _(pe):
            def exact(dst, a_hi, a_lo, b_hi, b_lo, first, last):
                pe.matmul(dst, a_hi, b_hi, start=first, stop=False)
                pe.matmul(dst, a_hi, b_lo, start=False, stop=False)
                return pe.matmul(dst, a_lo, b_hi, start=False, stop=last)

            pe.wait_ge(const_in, 16)
            pe.wait_ge(rows_in, 112)
            pe.transpose(bank[7][:, 0:R_ALL], rows_a[:, :], ident[0:R_ALL, 0:R_ALL])
            pe.transpose(bank[7][:, P:P + 2 * CMP_LEN], rows_b[:, :],
                         ident[0:2 * CMP_LEN, 0:2 * CMP_LEN]).then_inc(rows_T, 1)
            def modulation(chunk):
                pe.wait_ge(acc_done, chunk + 1)
                pe.wait_ge(cols_done, 1)
                if chunk >= 1:
                    pe.wait_ge(mod_read, chunk)
                for j in range(4):
                    mm = pe.matmul(bank[7][:, 4 * chunk + j:4 * chunk + j + 1],
                                   acc[:, chunk % 2, j * P:(j + 1) * P], ones[:, 0:1], start=True, stop=True)
                mm.then_inc(mod_mm, 1)

            modulation(0)
            for s in range(ST):
                pe.wait_ge(xn_done, s + 1)
            for k in range(KT):
                if k >= 6:
                    if k % 2 == 0:
                        pe.wait_ge(xT_act, (k - 6) // 2 + 1)
                    else:
                        pe.wait_ge(xT_dve, (k - 6) // 2 + 1)
                for s in range(ST):
                    mm = pe.transpose(bank[k % 6][:, s * P:(s + 1) * P], x_sb[:, s, k * P:(k + 1) * P], ident)
                mm.then_inc(xT_mm, 1)
            pe.wait_ge(misc_in, 80)
            pe.matmul(bank[6][0:HN, 0:S], rel[:, :], oneh[:, :], start=True, stop=True).then_inc(t5_mm, 1)

            for k in range(KT):
                pe.wait_ge(h_ready, k + 1)
                pe.wait_ge(*lo_of(k))
                if k == 0:
                    pe.wait_ge(xT_act, KT // 2)
                    pe.wait_ge(xT_dve, KT // 2)
                hi, lo = split(k)
                for m in range(6):
                    cs = slice(m * P, (m + 1) * P)
                    mm = exact(bank[m][:, :], hi[:, cs], lo[:, cs], h_hi[:, k, :], h_lo[:, k, :],
                               k == 0, k == KT - 1)
                mm.then_inc(unit_used, 1)
                if k % 2 == 0 and k // 2 + 1 < D // 256:
                    modulation(k // 2 + 1)
            u = N_FIRST
            gate_chunk = D // 256
            for b, (_, n, _) in enumerate(PANEL):
                step = 2 if n > 280 else 4
                for k0 in range(0, KT, step):
                    pe.wait_ge(*lo_of(u))
                    hi, lo = split(u)
                    for k in range(k0, k0 + step):
                        ws = slice((k - k0) * n, (k - k0 + 1) * n)
                        for s in range(ST):
                            a = ST * b + s
                            if k == 0:
                                if a < 6:
                                    if a % 2 == 0:
                                        pe.wait_ge(first_act, a // 2 + 1)
                                    else:
                                        pe.wait_ge(first_dve, a // 2 + 1)
                                elif a == 6:
                                    pe.wait_ge(vec_done, 1)
                                elif (a - 7) % 2 == 0:
                                    pe.wait_ge(val_act, (a - 7) // 2 + 1)
                                else:
                                    pe.wait_ge(val_dve, (a - 7) // 2 + 1)
                            ps = slice(s * P, (s + 1) * P)
                            mm = exact(bank[a % 7][:, 0:n], h_hi[:, k, ps], h_lo[:, k, ps], hi[:, ws], lo[:, ws],
                                       k == 0, k == KT - 1)
                    mm.then_inc(unit_used, 1)
                    u += 1
                    if (u - N_FIRST) % 4 == 1 and u - N_FIRST > 4 and gate_chunk < D // 256 + 4:
                        modulation(gate_chunk)
                        gate_chunk += 1

            def compress(q):
                u = CMP_AT[q]
                pe.wait_ge(*lo_of(u))
                pe.wait_ge(blk_done, q + 1)
                hi, lo = split(u)
                for i in range(4):
                    cs = slice(i * CMP_HID, (i + 1) * CMP_HID)
                    mm = exact(bank[4 + q // 8][0:66, 0:CMP_HID], blk_hi[:, q % 2, i, :], blk_lo[:, q % 2, i, :],
                               hi[:, cs], lo[:, cs], q % 8 == 0 and i == 0, q % 8 == 7 and i == 3)
                mm.then_inc(unit_used, 1)

            def hidden_T():
                pe.wait_ge(hid_done, 1)
                for w in range(2):
                    for j in range(2):
                        mm = pe.transpose((T0, T1)[w][:, j * P:j * P + 2 * NC], hid[:, w, j * P:(j + 1) * P],
                                          ident[0:2 * NC, 0:2 * NC])
                mm.then_inc(hidT_mm, 1)

            def compressed_kv():
                pe.wait_ge(hidT_done, 1)
                for j in range(2):
                    pe.matmul(bank[4][:, 0:2 * NC], w2[:, 0, j, :], hidT[:, 0, j, :], start=(j == 0), stop=(j == 1))
                for g in range(KVG):
                    for j in range(2):
                        mm = pe.matmul(bank[4][0:NC, P + g * HD:P + (g + 1) * HD],
                                       hidT[:, 1, j, g * NC:(g + 1) * NC], w2[:, 1, j, :],
                                       start=(j == 0), stop=(j == 1))
                mm.then_inc(kvcmp_mm, 1)

            def cum_rows(g):
                pe.wait_ge(nmx_done, 3 * g + 1)
                pe.wait_ge(cum_done, 1)
                for s in range(ST):
                    mm = pe.matmul(bank[4][:, s * P:(s + 1) * P], cum[:, s, g:g + 1].to_broadcast([P, P]), ident,
                                   start=True, stop=True)
                mm.then_inc(cumb_mm, 1)

            def scores(j):
                kind, h, _ = JOBS[j]
                if j >= 1:
                    pe.wait_ge(nmx_done, j)
                if kind == "sel":
                    pe.wait_ge(*taken[index["qn", h]])
                    q, key = qn, ks[:, h // 3, :]
                    pe.wait_ge(kvcmp_done, 1)
                    pe.wait_ge(kc_act, 1)
                elif kind == "win":
                    pe.wait_ge(d_act, h + 1)
                    q, key = qn, kw[:, h // 3, :]
                else:
                    pe.wait_ge(*taken[index["kf", h]])
                    q, key = qf, kf[:, :]
                for b in range(ST):
                    mm = pe.matmul(SB[b][:, SBO[b]:SBO[b] + SW[b]], q[:, b * P:(b + 1) * P], key[:, 0:SW[b]],
                                   start=True, stop=True)
                if kind == "sel":
                    for b in range(ST):
                        mm = pe.matmul(SC[:, b * NC:(b + 1) * NC], q[:, b * P:(b + 1) * P],
                                       kcmp[:, (h // 3) * NC:(h // 3 + 1) * NC], start=True, stop=True)
                mm.then_inc(s_mm, 1)

            def transposes(j, part):
                kind = JOBS[j][0]
                if part == 0:
                    pe.wait_ge(p_done, j + 1)
                    pe.wait_ge(hidT_done, 1)
                    if j >= 1:
                        pe.wait_ge(pT_act, 2 * j)
                        pe.wait_ge(pT_dve, j)
                        pe.wait_ge(pcT_dve, (j + 2) // 3)
                    for k in range(2):
                        for b in range(k, ST):
                            mm = pe.transpose((T0, T1)[k][:, (b - k) * P:(b - k + 1) * P],
                                              prob[:, SO[b] + k * P:SO[b] + (k + 1) * P], ident)
                else:
                    pe.wait_ge(pT_act, 2 * j + 1)
                    for k in range(2, ST):
                        for b in range(k, ST):
                            o = TO[k] - TO[2] + (b - k) * P
                            mm = pe.transpose(T0[:, o:o + P], prob[:, SO[b] + k * P:SO[b] + (k + 1) * P], ident)
                    if kind == "sel":
                        pe.wait_ge(pT_dve, j + 1)
                        pe.wait_ge(pc_done, j // 3 + 1)
                        for b in range(ST):
                            mm = pe.transpose(T1[0:NC, b * P:(b + 1) * P], pc[:, b, :], ident)
                mm.then_inc(t_mm, 1)

            def weighted_values(j):
                kind, h, _ = JOBS[j]
                if kind != "win" and (j // 3) * 2 + (kind == "fox") >= 1:
                    pe.wait_ge(o_done, (j // 3) * 2 + (kind == "fox"))
                pe.wait_ge(pT_act, 2 * j + 2)
                pe.wait_ge(pT_dve, j + 1)
                v0 = {"sel": PVS + (h // 3) * HD, "win": PVW + (h // 3) * HD, "fox": h * HD}[kind]
                for k in range(ST):
                    mm = pe.matmul(OB[:, k * P:], vals[:, k, v0:v0 + HD], probT[:, TO[k]:TO[k] + TW[k]],
                                   start=(k == 0 and kind != "win"), stop=(k == ST - 1 and kind != "sel"))
                if kind == "sel":
                    pe.wait_ge(pcT_dve, j // 3 + 1)
                    pe.matmul(OB[:, :], vcmp[:, h // 3, :], pcT[:, :], start=False, stop=False)
                else:
                    mm.then_inc(o_mm, 1)

            def cumulative():
                pe.wait_ge(logf_done, 1)
                for s in range(ST):
                    pe.matmul(bank[7][:, 64 + s * HF:64 + (s + 1) * HF], tri, fl[:, s, :], start=True, stop=(s == 0))
                    for r in range(s):
                        mm = pe.matmul(bank[7][:, 64 + s * HF:64 + (s + 1) * HF], ones, fl[:, r, :],
                                       start=False, stop=(r == s - 1))
                mm.then_inc(cum_mm, 1)

            for t in range(NT):
                if t == 0:
                    pe.wait_ge(val_dve, 5)
                    pe.wait_ge(val_act, 6)
                elif t >= 2:
                    pe.wait_ge(*taken[t - 2])
                for half in range(2):
                    u = HALF_AT[t, half]
                    pe.wait_ge(*lo_of(u))
                    hi, lo = split(u)
                    for i in range(KT // 2):
                        k, cs = half * KT // 2 + i, slice(i * P, (i + 1) * P)
                        mm = exact(ACC[t % 2][:, :], hi[:, cs], lo[:, cs], h_hi[:, k, :], h_lo[:, k, :],
                                   k == 0, k == KT - 1)
                    mm.then_inc(unit_used, 1)
                    if t < CMP_TILES:
                        if t == 0 and half == 0:
                            pe.wait_ge(val_act, 8)
                            pe.wait_ge(val_dve, 8)
                        for i in range(CMP_PER // 2):
                            compress(CMP_PER * t + CMP_PER // 2 * half + i)
                    if half == 0:
                        if t == CMP_TILES:
                            hidden_T()
                        for j, (_, _, at_t) in enumerate(JOBS):
                            if t == at_t + 2:
                                transposes(j, 1)
                if t == 1:
                    cumulative()
                if t == CMP_TILES:
                    compressed_kv()
                for j, (_, g, at_t) in enumerate(JOBS):
                    if t == at_t + 2:
                        weighted_values(j)
                for j, (kind, g, at_t) in enumerate(JOBS):
                    if t == at_t + 1:
                        transposes(j, 0)
                        if kind == "sel":
                            cum_rows(g)
                for j, (_, g, at_t) in enumerate(JOBS):
                    if t == at_t:
                        scores(j)

            pe.wait_ge(mod_read, D // 256 + 4)
            pe.wait_ge(nmx_done, len(JOBS))
            pe.wait_ge(pT_act, 2 * len(JOBS))
            for k in range(KT):
                mm = pe.matmul((bank[4], bank[5], bank[6], bank[0])[k // 4][:, k % 4 * P:(k % 4 + 1) * P],
                               gate_col[:, k:k + 1].to_broadcast([P, P]), ident, start=True, stop=True)
                if k % 4 == 3:
                    mm.then_inc(gb_mm, 1)
            pe.wait_ge(pT_dve, len(JOBS))
            pe.wait_ge(*taken[NT - 2])
            pe.wait_ge(o_done, 2 * HN)

            def out_step(half, i, s, u):
                hi, lo = split(u)
                k = OUT_ORDER[i]
                ps = slice(s * P, (s + 1) * P)
                for n in range(2):
                    ws = slice(n * S, (n + 1) * S)
                    if half == 0 and i == 0 and YB[2 * s + n] is ACC[(NT - 1) % 2]:
                        pe.wait_ge(*taken[NT - 1])
                    if half == 0 and i == 0 and 2 * s + n >= 4:
                        pe.wait_ge(gb_done, 2 * s + n - 3)
                    if half == 1 and i == 0:
                        pe.wait_ge((y_act, y_dve)[n], s + 1)
                    mm = exact(YB[2 * s + n][:, :], h_hi[:, k, ps], h_lo[:, k, ps], hi[:, ws], lo[:, ws],
                               i == 0, i == KT - 1)
                    if half == 0 and i == KT - 1 and (s, n) != (ST - 1, 1):
                        mm.then_inc(y_mm, 1)
                return mm

            for half in range(2):
                for i in range(KT if half == 0 else KT - LATE):
                    u = AT[NT] + half * KT + i
                    pe.wait_ge(*lo_of(u))
                    pe.wait_ge(y_ready, i + 1)
                    for s in range(ST):
                        mm = out_step(half, i, s, u)
                    mm.then_inc(unit_used, 1)
            for s in range(ST):
                for i in range(KT - LATE, KT):
                    pe.wait_ge(*lo_of(AT[NT] + KT + i))
                    mm = out_step(1, i, s, AT[NT] + KT + i)
                mm.then_inc(y_mm, 1)

        @block.scalar
        def _(act):
            seq = [0]

            def fence(ins):
                seq[0] += 1
                ins.then_inc(act_seq, 1)
                act.wait_ge(act_seq, seq[0])

            def hi_half(u):
                act.wait_ge(raw_in[u % NRAW], 16 * (u // NRAW + 1))
                if NSPLIT <= u < FIRST_LATE:
                    act.wait_ge(unit_used, u - NSPLIT + 1)
                act.activation(split(u)[0], w_raw[:, u % NRAW, 0:UNITS[u][2]], ACT.Copy).then_inc(hi_done, 1)

            act.wait_ge(cols_done, 1)
            act.activation(c_tmp[:, :], cols_a[:, R_C:R_C + KT], ACT.Exp, scale=-1.0).then_inc(c_exp, 1)
            act.wait_ge(c_exp, 1)
            act.preload_act_table(ACT.Sqrt)
            act.wait_ge(stat_v, 1)
            for s in range(ST):
                act.wait_ge(x_in[s], 16)
                act.activation(xT[:, 4 * s:4 * s + 4, :].rearrange("p k n -> p (k n)"), x_sb[:, s, :], ACT.Square,
                               accum_out=stat[:, s:s + 1]).then_inc(x_sq, 1)
            act.wait_ge(x_sq, ST)
            act.activation(rstd[:, :], stat[:, :], ACT.Sqrt, scale=1.0 / D, bias=eps_c[:, :]).then_inc(x_std, 1)
            for k in range(0, KT, 2):
                act.wait_ge(xT_mm, k + 1)
                act.activation(xT[:, k, :], bank[k % 6][:, :], ACT.Copy).then_inc(xT_act, 1)
            for k in range(KT):
                hi_half(k)
                act.wait_ge(mod_done, k // 2 + 1)
                if k == 0:
                    act.wait_ge(xT_dve, KT // 2)
                if k >= 2:
                    act.wait_ge(h_ready, k - 1)
                act.activation(xmix[:, k % 2, :], xT[:, k, :], ACT.Identity, scale=mod_sc[:, k:k + 1],
                               bias=mod_sh[:, k:k + 1]).then_inc(h_full, 1)
                act.wait_ge(h_full, k + 1)
                act.activation(h_hi[:, k, :], xmix[:, k % 2, :], ACT.Copy).then_inc(h_rounded, 1)
            hi_half(N_FIRST)
            act.wait_ge(unit_used, N_FIRST)
            for m in range(0, 6, 2):
                dst = kvc[:, m, :] if m < 4 else ks[:, m - 4, :]
                act.activation(dst, bank[m][:, :], ACT.Copy).then_inc(first_act, 1)

            def panel_out(a):
                b, s = a // ST, a % ST
                act.activation(vals[:, s, PANEL[b][2]:PANEL[b][2] + PANEL[b][1]], bank[a % 7][:, 0:PANEL[b][1]],
                               ACT.Copy).then_inc(val_act, 1)

            u, done = N_FIRST + 1, N_FIRST
            for b, (_, n, _) in enumerate(PANEL):
                done += 8 if n > 280 else 4
                while u < done + 2:
                    hi_half(u)
                    u += 1
                act.wait_ge(unit_used, done)
                for s in range(0, ST, 2):
                    panel_out(ST * b + s)
            act.wait_ge(val_act, 2 * len(PANEL))
            act.wait_ge(val_dve, 2 * len(PANEL))
            act.activation(gate[:, :, :], vals[:, :, PG:PG + 3 * HN], ACT.Exp, scale=-1.0).then_inc(gate_exp, 1)
            act.wait_ge(f_abs, 1)
            act.activation(fe[:, :, :], fe[:, :, :], ACT.Exp, scale=-1.0).then_inc(f_exp, 1)
            act.wait_ge(f_exp, 1)
            act.activation(fe[:, :, :], fe[:, :, :], ACT.Ln, bias=one_c[:, :]).then_inc(f_ln, 1)

            def tile_out(t):
                kind, i = TILES[t]
                act.wait_ge(unit_used, HALF_AT[t, 1] + 1)
                src = ACC[t % 2][:, :]
                if kind == "kw":
                    ins = act.activation(kw[:, i, :], src, ACT.Copy)
                elif kind == "qn":
                    if i >= 1:
                        act.wait_ge(s_mm, 3 * (i - 1) + 2)
                    ins = act.activation(qn[:, :], src, ACT.Copy, scale=SCALE)
                elif kind == "qf":
                    if i >= 1:
                        act.wait_ge(s_mm, 3 * i)
                    ins = act.activation(qf[:, :], src, ACT.Copy, scale=SCALE)
                elif kind == "kf":
                    if i >= 1:
                        act.wait_ge(s_mm, 3 * i)
                    ins = act.activation(kf[:, :], src, ACT.Copy)
                elif kind == "u":
                    if i >= 1:
                        act.wait_ge(*taken[index["gc", i - 1]])
                    ins = act.activation(u_sb[:, :], src, ACT.Copy)
                elif kind in ("zn", "zf", "za"):
                    z = z_order.index(t)
                    if z >= 1:
                        act.wait_ge(*taken[z_order[z - 1]])
                    act.activation(e_sb[:, :], src, ACT.Exp, scale=-1.0).then_inc(z_exp, 1)
                    return
                else:
                    return
                ins.then_inc(tile_act, 1)

            for t in range(NT + 1):
                if t < NT:
                    lead = list(range(AT[t] + 2, min(AT[t + 1] + 2, NU)))
                    for u in lead[:len(lead) // 2]:
                        hi_half(u)
                if t >= 1:
                    tile_out(t - 1)
                if t == CMP_TILES:
                    act.wait_ge(unit_used, AT[CMP_TILES])
                    for w in range(2):
                        ins = act.activation(hid[:, w, :], bank[4 + w][0:2 * NC, 0:CMP_HID], ACT.Exp, scale=-1.0)
                    ins.then_inc(hid_exp, 1)
                if t == CMP_TILES + 1:
                    act.wait_ge(kvcmp_mm, 1)
                    act.activation(kcmp[:, :], bank[4][:, 0:2 * NC], ACT.Copy).then_inc(kc_act, 1)
                for j, (kind, g, at_t) in enumerate(JOBS):
                    if t == at_t + 2:
                        act.wait_ge(t_mm, 2 * j + 1)
                        if j >= 1:
                            act.wait_ge(o_mm, (j // 3) * 2 + (kind == "fox")) if kind != "win" else act.wait_ge(
                                t_mm, 2 * j + 1)
                        act.activation(probT[:, TO[0]:TO[1]], T0[:, :], ACT.Copy).then_inc(pT_act, 1)
                        if kind == "sel":
                            act.wait_ge(cumb_mm, g + 1)
                            if g >= 1:
                                act.wait_ge(nmx_done, 3 * g)
                            for b in range(ST):
                                ins = act.activation(dbias[:, SO[b]:SO[b] + SW[b]], bank[4][:, 0:SW[b]], ACT.Identity,
                                                     scale=-1.0, bias=cum[:, b, g:g + 1])
                            ins.then_inc(d_act, 1)
                    if t == at_t + 1:
                        act.wait_ge(nmx_done, j + 1)
                        for b in range(ST):
                            cs = slice(SO[b], SO[b] + SW[b])
                            ins = act.activation(prob[:, cs], prob[:, cs], ACT.Exp, bias=nmx[:, b:b + 1],
                                                 accum_out=ssum[:, b:b + 1])
                        ins.then_inc(p_exp, 1)
                        if kind == "sel":
                            act.wait_ge(sc_sub, g + 1)
                            act.activation(pc[:, :, :], pc[:, :, :], ACT.Exp).then_inc(pc_exp, 1)
                if t < NT:
                    for u in lead[len(lead) // 2:]:
                        hi_half(u)
                for j, (_, g, at_t) in enumerate(JOBS):
                    if t == at_t + 2:
                        act.wait_ge(t_mm, 2 * j + 2)
                        act.activation(probT[:, TO[2]:SALL], T0[:, 0:SALL - TO[2]], ACT.Copy).then_inc(pT_act, 1)
            u = AT[NT] + 2
            act.wait_ge(unit_used, AT[NT])
            act.wait_ge(o_done, 2 * HN)
            for k, c_k in enumerate(OUT_ORDER):
                if c_k == CT - 1:
                    act.wait_ge(*taken[index["za", CT - 1]])
                act.activation(h_hi[:, c_k, :], yT[:, c_k, :], ACT.Copy).then_inc(yh_hi, 1)
                if k in (1, 2, 3, 5):
                    n = (1, 2, 3, 5).index(k)
                    act.wait_ge(gb_mm, n + 1)
                    act.activation(g_bc[:, n * S:(n + 1) * S], (bank[4], bank[5], bank[6], bank[0])[n][:, :],
                                   ACT.Copy).then_inc(gb_done, 1)
                if k % 3 == 2 and u < AT[NT] + NSPLIT:
                    hi_half(u)
                    u += 1
            while u < AT[NT] + KT + 2:
                hi_half(u)
                u += 1
            for s in range(ST):
                act.wait_ge(y_mm, 2 * s + 1)
                act.activation(y_half[:, s, 0:S], YB[2 * s][:, :], ACT.Copy).then_inc(y_act, 1)
            while u < FIRST_LATE:
                hi_half(u)
                u += 1
            act.wait_ge(y_ready, KT)
            while u < NU:
                hi_half(u)
                u += 1
            act.wait_ge(unit_used, FIRST_LATE)
            act.wait_ge(*lo_of(NU - 1))
            for s in range(ST):
                act.wait_ge(y_dve, s + 1)
                act.wait_ge(y_act, s + 1)
                act.activation(fin[:, 1, 0:D // 2], y_half[:, s, :], ACT.Square,
                               accum_out=sq[:, s, 0:1]).then_inc(yh_sq, 1)
                act.wait_ge(yh_sq, s + 1)
            act.preload_act_table(ACT.Sqrt)
            for s in range(ST):
                act.wait_ge(y_mm, 2 * ST - 1 + s + 1)
                fence(act.activation(sq_out[:, :], YB[2 * s][:, :], ACT.Square, accum_out=sq[:, s, 1:2]))
                act.activation(sq_out[:, :], YB[2 * s + 1][:, :], ACT.Square, accum_out=sq[:, s, 2:3]).then_inc(y_sq, 1)
                act.wait_ge(y_tot, s + 1)
                act.activation(rs2[:, s:s + 1], tot[:, s:s + 1], ACT.Sqrt, scale=1.0 / D, bias=eps_c[:, :]).then_inc(y_std, 1)

        @block.vector
        def _(dve):
            seq = [0]

            def fence(ins):
                seq[0] += 1
                ins.then_inc(dve_seq, 1)
                dve.wait_ge(dve_seq, seq[0])

            def lo_half(u):
                n = UNITS[u][2]
                hi, lo = split(u)
                dve.wait_ge(hi_done, u + 1)
                dve.tensor_tensor(lo, w_raw[:, u % NRAW, 0:n], hi.bitcast(F32), ALU.subtract).then_inc(lo_done, 1)

            def reciprocal_of_one_plus(dst, src):
                fence(dve.tensor_scalar(dst, src, 1.0, None, ALU.add))
                fence(dve.reciprocal(dst, dst))

            dve.memset(eps_c[:, :], EPS)
            dve.memset(conv_y[:, 0:CW - 1], 0.0)
            dve.memset(one_c[:, :], 1.0).then_inc(stat_v, 1)
            dve.wait_ge(rows_T, 1)
            fence(dve.tensor_copy(cols_a[:, :], bank[7][:, 0:R_ALL]))
            dve.tensor_copy(pe_cols[:, :, :], bank[7][:, P:P + 2 * CMP_LEN].rearrange("p (w l) -> p w l", w=2)) \
               .then_inc(cols_done, 1)
            dve.wait_ge(c_exp, 1)
            reciprocal_of_one_plus(c_tmp[:, :], c_tmp[:, :])
            fence(dve.tensor_tensor(c_act[:, :], cols_a[:, R_C:R_C + KT], c_tmp[:, :], ALU.mult))
            fence(dve.tensor_scalar(b1[:, :], cols_a[:, R_ADA + KT:R_ADA + 2 * KT], 1.0, None, ALU.add))

            def modulate(chunk):
                if chunk >= 2:
                    dve.wait_ge(mod_mm, chunk - 1)
                dst = acc[:, chunk % 2, :]
                for k in range(KT):
                    n = 4 * chunk + k // 4
                    if k % 4 == 0:
                        dve.wait_ge(ada_in[n % NADA], 32 * (n // NADA + 1))
                    src = ada[:, n % NADA, k % 4, :]
                    if k == 0:
                        ins = dve.tensor_scalar(dst, src, c_act[:, 0:1], None, ALU.mult)
                    else:
                        ins = dve.scalar_tensor_tensor(out=dst, in0=src, scalar=c_act[:, k:k + 1], in1=dst,
                                                       op0=ALU.mult, op1=ALU.add)
                    if k == KT - 1:
                        ins.then_inc(acc_done, 1)
                        dve.wait_ge(acc_done, chunk + 1)
                        dve.sem_inc(ada_used, 1)
                    elif k % 4 == 3:
                        ins.then_inc(ada_used, 1)
                        dve.wait_ge(ada_used, n + 1)
                    else:
                        fence(ins)

            def make_h(chunk):
                dve.wait_ge(mod_mm, chunk + 1)
                k = slice(2 * chunk, 2 * chunk + 2)
                m0 = 4 * chunk
                dve.tensor_tensor(mod_sh[:, k], bank[7][:, m0:m0 + 2], cols_a[:, R_ADA + 2 * chunk:R_ADA + 2 * chunk + 2],
                                  ALU.add)
                dve.tensor_tensor(mod_sc[:, k], bank[7][:, m0 + 2:m0 + 4], b1[:, k], ALU.add).then_inc(mod_read, 1)
                dve.wait_ge(mod_read, chunk + 1)
                dve.tensor_tensor(mod_sc[:, k], mod_sc[:, k], cols_a[:, R_PRE + 2 * chunk:R_PRE + 2 * chunk + 2],
                                  ALU.mult).then_inc(mod_done, 1)

            modulate(0)
            dve.wait_ge(x_std, 1)
            fence(dve.reciprocal(rstd[:, :], rstd[:, :]))
            for s in range(ST):
                dve.tensor_scalar(x_sb[:, s, :], x_sb[:, s, :], rstd[:, s:s + 1], None, ALU.mult).then_inc(xn_done, 1)
            for k in range(1, KT, 2):
                dve.wait_ge(xT_mm, k + 1)
                dve.tensor_copy(xT[:, k, :], bank[k % 6][:, :]).then_inc(xT_dve, 1)
            fence(dve.memset(vec[:, S:VEC], NEG))
            dve.wait_ge(t5_mm, 1)
            dve.tensor_copy(vec[:, 0:S], bank[6][0:HN, :]).then_inc(vec_done, 1)
            for chunk in range(D // 256):
                make_h(chunk)
                if chunk + 1 < D // 256:
                    modulate(chunk + 1)
            lo_half(N_FIRST)
            dve.wait_ge(unit_used, N_FIRST)
            for m in range(1, 6, 2):
                dst = kvc[:, m, :] if m < 4 else ks[:, m - 4, :]
                dve.tensor_copy(dst, bank[m][:, :]).then_inc(first_dve, 1)

            def gate_chunk(i):
                chunk = D // 256 + i
                dve.wait_ge(mod_mm, chunk + 1)
                k = slice(4 * i, 4 * i + 4)
                dve.tensor_tensor(gate_col[:, k], bank[7][:, 4 * chunk:4 * chunk + 4],
                                  cols_a[:, R_ADA + 2 * KT + 4 * i:R_ADA + 2 * KT + 4 * i + 4], ALU.add).then_inc(mod_read, 1)
                dve.wait_ge(mod_read, chunk + 1)
                fence(dve.tensor_tensor(gate_col[:, k], gate_col[:, k], cols_a[:, R_POST + 4 * i:R_POST + 4 * i + 4],
                                        ALU.mult))

            def panel_out(a):
                b, s = a // ST, a % ST
                dve.tensor_copy(vals[:, s, PANEL[b][2]:PANEL[b][2] + PANEL[b][1]], bank[a % 7][:, 0:PANEL[b][1]]) \
                   .then_inc(val_dve, 1)

            u, done, chunks, read = N_FIRST + 1, N_FIRST, 0, 0
            for b, (_, n, _) in enumerate(PANEL):
                done += 8 if n > 280 else 4
                while u < done + 2:
                    lo_half(u)
                    u += 1
                    if (u - N_FIRST) % 4 == 0 and chunks < 4:
                        modulate(D // 256 + chunks)
                        chunks += 1
                    if (u - N_FIRST) % 4 == 3 and read < chunks and u - N_FIRST > 6:
                        gate_chunk(read)
                        read += 1
                dve.wait_ge(unit_used, done)
                for s in range(1, ST, 2):
                    panel_out(ST * b + s)
            while read < 4:
                gate_chunk(read)
                read += 1
            dve.wait_ge(val_act, 2 * len(PANEL))
            dve.wait_ge(val_dve, 2 * len(PANEL))
            dve.wait_ge(misc_in, 80)
            for s in range(ST):
                ins = dve.tensor_tensor(fl[:, s, :], vals[:, s, PF:PF + HF], bf[:, :], ALU.add)
            fence(ins)
            dve.scalar_tensor_tensor(out=fe[:, :, :], in0=fl[:, :, :], scalar=-1.0, in1=fl[:, :, :],
                                     op0=ALU.mult, op1=ALU.max).then_inc(f_abs, 1)
            dve.wait_ge(gate_exp, 1)
            reciprocal_of_one_plus(gate[:, :, :], gate[:, :, :])
            fence(dve.tensor_scalar(gate[:, 0, 0:3 * HN:3], gate[:, 0, 0:3 * HN:3], anym, None, ALU.mult))
            fence(dve.tensor_scalar(fl[:, :, :], fl[:, :, :], 0.0, None, ALU.min))
            dve.wait_ge(f_ln, 1)
            dve.tensor_tensor(fl[:, :, :], fl[:, :, :], fe[:, :, :], ALU.subtract).then_inc(logf_done, 1)

            def tile_out(t):
                kind, i = TILES[t]
                src = ACC[t % 2][:, :]
                if kind in ("zn", "zf", "za"):
                    dve.wait_ge(z_exp, z_order.index(t) + 1)
                    reciprocal_of_one_plus(e_sb[:, :], e_sb[:, :])
                    dst = yT[:, y_of(kind, i), :]
                    if kind == "za":
                        fence(dve.tensor_tensor(e_sb[:, :], e_sb[:, :], conv_z[:, :], ALU.mult))
                    dve.tensor_tensor(dst, src, e_sb[:, :], ALU.mult).then_inc(tile_dve, 1)
                elif kind == "gc":
                    dve.wait_ge(unit_used, HALF_AT[t, 1] + 1)
                    dve.wait_ge(*taken[index["u", i]])
                    y0 = CW - 1
                    dve.tensor_tensor(conv_y[:, y0:], src, u_sb[:, :], ALU.mult).then_inc(tile_dve, 1)
                    dve.wait_ge(*taken[t])
                    w = [cols_a[:, R_CONV + j * CT + i:R_CONV + j * CT + i + 1] for j in range(CW)]
                    fence(dve.tensor_scalar(conv_z[:, :], conv_y[:, 0:S], w[0], None, ALU.mult))
                    for j in range(1, CW):
                        fence(dve.scalar_tensor_tensor(out=conv_z[:, :], in0=conv_y[:, j:j + S], scalar=w[j],
                                                       in1=conv_z[:, :], op0=ALU.mult, op1=ALU.add))
                elif kind == "gb":
                    dve.wait_ge(unit_used, HALF_AT[t, 1] + 1)
                    dve.tensor_tensor(conv_z[:, :], src, conv_z[:, :], ALU.mult).then_inc(tile_dve, 1)
                    dve.wait_ge(*taken[t])

            def softmax_in(j):
                kind, h, _ = JOBS[j]
                dve.wait_ge(s_mm, j + 1)
                if j >= 1:
                    dve.wait_ge(t_mm, 2 * j)
                if kind == "fox":
                    dve.wait_ge(d_done, h + 1)
                else:
                    dve.wait_ge(bias_in[h % 2], 16 * (h // 2 + 1))
                for b in range(ST):
                    cs = slice(SO[b], SO[b] + SW[b])
                    bias = dbias[:, cs] if kind == "fox" else bias_t[:, h % 2, S - SW[b]:S]
                    ins = dve.tensor_tensor_reduce(prob[:, cs], SB[b][:, SBO[b]:SBO[b] + SW[b]], bias, 1.0, NEG,
                                                   ALU.add, ALU.max, mx[:, b:b + 1])
                fence(ins)
                if kind == "sel":
                    dve.wait_ge(bias_c_done, h + 1)
                    flat = pc[:, :, :].rearrange("p b n -> p (b n)")
                    fence(dve.tensor_tensor(flat, SC, bias_c[:, :, :].rearrange("p b n -> p (b n)"), ALU.add))
                dve.tensor_scalar(nmx[:, :], mx[:, :], -1.0, None, ALU.mult).then_inc(nmx_done, 1)
                if kind == "sel":
                    fence(dve.tensor_reduce(rr[:, :], pc[:, :, :], AX.X, ALU.max))
                    for b in range(ST):
                        ins = dve.tensor_scalar(pc[:, b, :], pc[:, b, :], rr[:, b:b + 1], None, ALU.subtract)
                    ins.then_inc(sc_sub, 1)

            def softmax_out(j):
                kind, h, _ = JOBS[j]
                dve.wait_ge(p_exp, j + 1)
                fence(dve.reciprocal(rr[:, :], ssum[:, :]))
                if kind != "fox":
                    g = 3 * h + {"sel": 1, "win": 2}[kind]
                    fence(dve.tensor_tensor(rr[:, :], rr[:, :], gate[:, :, g], ALU.mult))
                for b in range(ST):
                    cs = slice(SO[b], SO[b] + SW[b])
                    ins = dve.tensor_scalar(prob[:, cs], prob[:, cs], rr[:, b:b + 1], None, ALU.mult)
                ins.then_inc(p_done, 1)
                if kind == "sel":
                    dve.wait_ge(pc_exp, h + 1)
                    dve.wait_ge(p_done, j + 1)
                    fence(dve.tensor_reduce(rr[:, :], pc[:, :, :], AX.X, ALU.add))
                    fence(dve.reciprocal(rr[:, :], rr[:, :]))
                    fence(dve.tensor_tensor(rr[:, :], rr[:, :], gate[:, :, 3 * h], ALU.mult))
                    for b in range(ST):
                        ins = dve.tensor_scalar(pc[:, b, :], pc[:, b, :], rr[:, b:b + 1], None, ALU.mult)
                    ins.then_inc(pc_done, 1)

            for t in range(NT + 1):
                if t < NT:
                    lead = list(range(AT[t] + 2, min(AT[t + 1] + 2, NU)))
                    for u in lead[:len(lead) // 2]:
                        lo_half(u)
                if t == 2:
                    dve.wait_ge(cum_mm, 1)
                    dve.tensor_copy(cum[:, :, :], bank[7][:, 64:64 + ST * HF].rearrange("p (s h) -> p s h", s=ST)) \
                       .then_inc(cum_done, 1)
                if t >= 1:
                    tile_out(t - 1)
                if t == CMP_TILES:
                    dve.wait_ge(hid_exp, 1)
                    reciprocal_of_one_plus(hid[:, :, :], hid[:, :, :])
                    for w in range(2):
                        ins = dve.tensor_tensor(hid[:, w, :], bank[4 + w][0:2 * NC, 0:CMP_HID], hid[:, w, :], ALU.mult)
                    ins.then_inc(hid_done, 1)
                    dve.wait_ge(hidT_mm, 1)
                    for w in range(2):
                        src = (T0, T1)[w][:, 0:2 * P].rearrange("p (j n) -> p j n", j=2)[:, :, 0:2 * NC]
                        ins = dve.tensor_copy(hidT[:, w, :, :], src)
                    ins.then_inc(hidT_done, 1)
                if t == CMP_TILES + 1:
                    dve.wait_ge(kc_act, 1)
                    dve.tensor_copy(vcmp[:, :, :], bank[4][0:NC, P:P + KVG * HD].rearrange("p (g d) -> p g d", g=KVG)) \
                       .then_inc(kvcmp_done, 1)
                for j, (kind, g, at_t) in enumerate(JOBS):
                    if t == at_t + 3 and kind != "sel":
                        o = (j // 3) * 2 + (kind == "fox")
                        dve.wait_ge(o_mm, o + 1)
                        y = y_of("zf", g) if kind == "fox" else y_of("zn", g)
                        dve.wait_ge(*taken[index["zf" if kind == "fox" else "zn", g]])
                        dve.tensor_tensor(yT[:, y, :], OB[:, :], yT[:, y, :], ALU.mult).then_inc(o_done, 1)
                for j, (kind, g, at_t) in enumerate(JOBS):
                    if t == at_t + 2:
                        dve.wait_ge(t_mm, 2 * j + 1)
                        dve.tensor_copy(probT[:, TO[1]:TO[2]], T1[:, 0:TW[1]]).then_inc(pT_dve, 1)
                    if t == at_t + 1:
                        softmax_in(j)
                if t < NT:
                    for u in lead[len(lead) // 2:]:
                        lo_half(u)
                for j, (kind, g, at_t) in enumerate(JOBS):
                    if t == at_t + 1:
                        softmax_out(j)
                    if t == at_t + 2 and kind == "sel":
                        dve.wait_ge(t_mm, 2 * j + 2)
                        dve.tensor_copy(pcT[:, :], T1[0:NC, :]).then_inc(pcT_dve, 1)
            u = AT[NT] + 2
            for k, c_k in enumerate(OUT_ORDER):
                dve.wait_ge(yh_hi, k + 1)
                dve.tensor_tensor(h_lo[:, c_k, :], yT[:, c_k, :], h_hi[:, c_k, :].bitcast(F32), ALU.subtract) \
                   .then_inc(y_ready, 1)
                if k % 3 == 2 and u < AT[NT] + NSPLIT:
                    lo_half(u)
                    u += 1
            while u < AT[NT] + KT + 2:
                lo_half(u)
                u += 1
            for s in range(ST):
                dve.wait_ge(y_mm, 2 * s + 2) if s < ST - 1 else dve.wait_ge(unit_used, AT[NT] + KT)
                dve.tensor_copy(y_half[:, s, S:2 * S], YB[2 * s + 1][:, :]).then_inc(y_dve, 1)
            while u < NU:
                lo_half(u)
                u += 1
            for s in range(ST):
                for n in range(2):
                    if n == 0:
                        dve.wait_ge(y_sq, s + 1)
                        dve.tensor_reduce(tot[:, s:s + 1], sq[:, s, :], AX.X, ALU.add).then_inc(y_tot, 1)
                        if s >= 2:
                            dve.wait_ge(stored[s % 2], 32 * (s // 2))
                    cs = slice(D // 2 + n * S, D // 2 + (n + 1) * S)
                    ins = dve.tensor_tensor(fin[:, s % 2, cs], YB[2 * s + n][:, :], g_bc[:, cs], ALU.mult)
                fence(ins)
                dve.wait_ge(y_std, s + 1)
                fence(dve.reciprocal(rs3[:, s:s + 1], rs2[:, s:s + 1]))
                r = rs3[:, s:s + 1]
                dve.wait_ge(xa_in[s % 2], 16 * (s // 2 + 1))
                dve.wait_ge(yg_done, s + 1)
                dve.scalar_tensor_tensor(out=fin[:, s % 2, 0:D // 2], in0=y_half[:, s, :], scalar=r,
                                         in1=x_again[:, s % 2, 0:D // 2], op0=ALU.mult, op1=ALU.add).then_inc(fin_done, 1)
                dve.scalar_tensor_tensor(out=fin[:, s % 2, D // 2:], in0=fin[:, s % 2, D // 2:], scalar=r,
                                         in1=x_again[:, s % 2, D // 2:], op0=ALU.mult, op1=ALU.add).then_inc(fin_done, 1)

        @block.gpsimd
        def _(pool):
            seq = [0]

            def fence(ins):
                seq[0] += 1
                ins.then_inc(pool_seq, 1)
                pool.wait_ge(pool_seq, seq[0])

            for k in range(KT):
                pool.wait_ge(hi_done, k + 1)
                n = UNITS[k][2]
                hi, lo = split(k)
                pool.tensor_tensor(lo, w_raw[:, k % NRAW, 0:n], hi.bitcast(F32), ALU.subtract).then_inc(first_lo, 1)
                pool.wait_ge(h_rounded, k + 1)
                pool.tensor_tensor(h_lo[:, k, :], xmix[:, k % 2, :], h_hi[:, k, :].bitcast(F32), ALU.subtract) \
                    .then_inc(h_ready, 1)
            pool.wait_ge(first_act, 3)
            pool.wait_ge(first_dve, 3)
            fence(pool.memset(blk_hi[:, :, :, 2 * NC:].bitcast(F32), 0.0))
            fence(pool.memset(blk_lo[:, :, :, 2 * NC:].bitcast(F32), 0.0))
            for q in range(16):
                w, l0 = q // 8, q % 8 * 4
                a, r = divmod(l0, CMP_STRIDE)
                kv = kvc[:, 2 * w:2 * w + 2, :].rearrange("p g (n s) -> p s g n", s=CMP_STRIDE)
                b4 = blk[:, :, :].rearrange("p l (g n) -> p l g n", g=2)
                for i in range(4):
                    ins = pool.tensor_scalar(b4[:, i, :, :], kv[:, r + i, :, a:a + NC],
                                             pe_cols[:, w, l0 + i:l0 + i + 1], None, ALU.add)
                fence(ins)
                if q >= 2:
                    pool.wait_ge(unit_used, CMP_AT[q - 2] + 1)
                fence(pool.tensor_copy(blk_hi[:, q % 2, :, 0:2 * NC], blk[:, :, :]))
                pool.tensor_tensor(blk_lo[:, q % 2, :, 0:2 * NC], blk[:, :, :],
                                   blk_hi[:, q % 2, :, 0:2 * NC].bitcast(F32), ALU.subtract).then_inc(blk_done, 1)
                pool.wait_ge(blk_done, q + 1)
            for g in range(HN):
                pool.wait_ge(bias_in[g % 2], 16 * (g // 2 + 1))
                if g >= 1:
                    pool.wait_ge(nmx_done, 3 * (g - 1) + 1)
                fence(pool.memset(bias_c[:, :, :], NEG))
                for b in range(ST):
                    n = min(NC, (P // CMP_STRIDE) * (b + 1) - 1)
                    u0 = S - (b + 1) * P + CMP_LEN - 1
                    ins = pool.tensor_copy(bias_c[:, b, 0:n],
                                           bias_t[:, g % 2, u0:u0 + (n - 1) * CMP_STRIDE + 1:CMP_STRIDE])
                ins.then_inc(bias_c_done, 1)
                pool.wait_ge(d_act, g + 1)
                for b in range(ST):
                    o = SO[b] + b * P
                    ins = pool.affine_select(out=dbias[:, o:o + P], in_=dbias[:, o:o + P], compare_op=ALU.is_ge,
                                             fill=NEG, base=0, pattern=[[-1, P]], channel_multiplier=1)
                ins.then_inc(d_done, 1)
            pool.wait_ge(gb_done, 4)
            for s in range(ST):
                pool.wait_ge(yh_sq, s + 1)
                pool.tensor_tensor(y_half[:, s, :], y_half[:, s, :], g_bc[:, 0:D // 2], ALU.mult).then_inc(yg_done, 1)


def bias_buckets():
    half = BUCKETS // 2
    dist = np.arange(S - 1, -1, -1)
    far = np.maximum(dist, half).astype(np.float32)
    large = half + (np.log(far / np.float32(half)) / np.float32(np.log(MAX_DIST / half))
                    * np.float32(BUCKETS - half)).astype(np.int32)
    bucket = np.where(dist < half, dist, np.minimum(large, BUCKETS - 1))
    return (np.arange(BUCKETS)[:, None] == bucket[None, :]).astype(np.float32)


def shape_constants():
    i = np.arange(P)
    return np.concatenate([np.eye(P), i[:, None] <= i[None, :], np.ones((P, P)),
                           i[:, None] >= CMP_LEN - 1], axis=1).astype(np.float32)


_INS = ["x", "c", "w_ada", "b_ada", "pre_norm", "post_norm", "w_in", "b_forget", "conv_w", "cmp_pe_k",
        "cmp_w1_k", "cmp_w2_k", "cmp_pe_v", "cmp_w1_v", "cmp_w2_v", "w_out", "rel_bias"]


def kernel(**inputs):
    import concourse.bacc as bacc
    from concourse.bass_utils import run_bass_kernel_spmd

    nc = bacc.Bacc("TRN2", target_bir_lowering=False, num_devices=1, dynamic_dma_scratch_size=1024)
    arrays = {name: np.ascontiguousarray(inputs[name]) for name in _INS}
    arrays["consts"], arrays["onehot"] = shape_constants(), bias_buckets()
    args = [nc.dram_tensor(name, a.shape, mybir.dt.from_np(a.dtype), kind="ExternalInput").ap()
            for name, a in arrays.items()]
    out = nc.dram_tensor("out", [1, S, D], F32, kind="ExternalOutput").ap()
    layer_program(nc, *args, out)
    r = run_bass_kernel_spmd(nc, [arrays], core_ids=[0])
    return r.results[0]["out"]
```

```python
from contextlib import ExitStack

import numpy as np

import concourse.bass as bass
from concourse import mybir

F32 = mybir.dt.float32
F32R = mybir.dt.float32r
ALU = mybir.AluOpType
ACT = mybir.ActivationFunctionType
AX = mybir.AxisListType

P = 128
D = 2048
S = 512
KT = D // P
ST = S // P
HD = 128
D_CONV = D // 4
D_FOX = 3 * D // 8
D_NSA = D - D_CONV - D_FOX
HF = D_FOX // HD
HN = D_NSA // HD
KVG = 2
CT = D_CONV // P
CW = 3
CMP_LEN, CMP_STRIDE, CMP_HID = 32, 16, 256
NC = (S - CMP_LEN) // CMP_STRIDE + 1
CPAD = 32
BUCKETS, MAX_DIST = 32, 128
EPS = 1e-6
NEG = -1e30
SCALE = HD ** -0.5

U_A = 0
GB_A, GC_A, Z_A = D_CONV, 2 * D_CONV, 3 * D_CONV
Q_F = 4 * D_CONV
K_F, V_F = Q_F + D_FOX, Q_F + 2 * D_FOX
F_F = Q_F + 3 * D_FOX
Z_F = F_F + HF
Q_N = Z_F + D_FOX
KV = KVG * HD
KC, VC, KS, VS, KW, VW = (Q_N + D_NSA + i * KV for i in range(6))
G_N = VW + KV
Z_N = G_N + 3 * HN
N_IN = Z_N + D_NSA

R_C, R_PRE, R_ADA, R_CONV, R_POST = 0, KT, 2 * KT, 5 * KT, 5 * KT + CW * CT
R_ALL = R_POST + KT

PANEL = [(V_F, 512, 0), (V_F + 512, D_FOX + HF - 512, 512), (VS, KV, D_FOX + HF),
         (VW, KV + 3 * HN, D_FOX + HF + KV)]
PW = sum(n for _, n, _ in PANEL)
PF, PVS, PVW, PG = D_FOX, D_FOX + HF, D_FOX + HF + KV, D_FOX + HF + 2 * KV

SLOT = 1120
NRAW, NSPLIT, NADA = 4, 4, 4
VEC = S + P

SW = [(b + 1) * P for b in range(ST)]
SO = [sum(SW[:b]) for b in range(ST)]
SALL = sum(SW)
TW = [S - k * P for k in range(ST)]
TO = [sum(TW[:k]) for k in range(ST)]


def tiles_and_jobs():
    conv = [(kind, i) for i in range(CT) for kind in ("u", "gc", "gb", "za")]
    tiles = [("kw", 0), ("kw", 1), conv.pop(0), conv.pop(0)]
    jobs = []
    for g in range(HN):
        b = len(tiles)
        tiles += [("qn", g), ("zn", g), ("qf", g), ("kf", g), ("zf", g), conv.pop(0), conv.pop(0)]
        jobs += [("sel", g, b + 1), ("win", g, b + 3), ("fox", g, b + 5)]
    return tiles + conv, jobs


TILES, JOBS = tiles_and_jobs()
NT = len(TILES)
CMP_TILES, CMP_PER = 4, 4
EARLY = 4
LATE = 8
Y_FIRST = 4
OUT_ORDER = [k for k in range(KT) if k != CT - 1] + [CT - 1]
COL0 = {"kw": KW, "qn": Q_N, "zn": Z_N, "qf": Q_F, "kf": K_F, "zf": Z_F,
        "u": U_A, "gc": GC_A, "gb": GB_A, "za": Z_A}


def weight_units():
    units, first_at, half_at, cmp_at = [], [], {}, {}
    for k in range(KT):
        first_at.append(len(units))
        units.append(("first", (k,), KV * 3))
        e, odd = divmod(k - KT // 2, 2)
        if not odd and 0 <= e < EARLY:
            half_at[e, 0] = len(units)
            units.append(("tile", (e, 0), KT // 2 * P))
    n_first = len(units)
    for b, (_, n, _) in enumerate(PANEL):
        step = 2 if n > 280 else 4
        units += [("panel", (b, k, step), step * n) for k in range(0, KT, step)]
    at = []
    for t in range(NT):
        at.append(len(units))
        for h in range(2):
            if t < CMP_TILES:
                for i in range(CMP_PER // 2):
                    q = CMP_PER * t + CMP_PER // 2 * h + i
                    cmp_at[q] = len(units)
                    units.append(("cmp", (q,), 4 * CMP_HID))
            if (t, h) not in half_at:
                half_at[t, h] = len(units)
                units.append(("tile", (t, h), KT // 2 * P))
    at.append(len(units))
    units += [("out", (n, k), D // 2) for n in range(2) for k in OUT_ORDER]
    return units, n_first, first_at, at, half_at, cmp_at


UNITS, N_FIRST, FIRST_AT, AT, HALF_AT, CMP_AT = weight_units()
NU = len(UNITS)
FIRST_LATE = NU - LATE
N_PANEL = AT[0] - N_FIRST


def layer_program(nc, x, c, w_ada, b_ada, pre_norm, post_norm, w_in, b_forget, conv_w,
                  pe_k, w1_k, w2_k, pe_v, w1_v, w2_v, w_out, rel_bias, consts, onehot, out):
    ctx = ExitStack()
    with ctx:
        top = [ctx.enter_context(nc.sbuf_tensor("arena", [P, 56960], F32))]
        base = 1152
        place = {}

        def at(name, shape, dt, offset):
            place[name] = offset + 4 * int(np.prod(shape[1:]))
            assert place[name] <= base + 4 * 56960, (name, place[name])
            return nc.alloc_sbuf_tensor_at(name, shape, dt, offset=offset)

        def row(names, offset):
            made = []
            for name, shape, dt in names:
                made.append(at(name, shape, dt, offset))
                offset = -(-place[name] // 32) * 32
            return made, offset

        (h_hi, h_lo), o = row([("h_hi", [P, KT, S], F32R), ("h_lo", [P, KT, S], F32R)], base)
        xT = at("xT", [P, KT, S], F32, base + 4 * KT * S)
        (w_raw, w_hi, w_lo), o2 = row([("w_raw", [P, NRAW, SLOT], F32),
                                       ("w_hi", [P, NSPLIT, SLOT], F32R),
                                       ("w_lo", [P, NSPLIT, SLOT], F32R)], o)
        x_again = at("x_again", [P, 2, D], F32, o)
        fin = at("fin", [P, 2, D], F32, o + 4 * NRAW * SLOT)
        shared = o2
        (yT, vals, prob, probT, dbias), o3 = row(
            [("yT", [P, KT, S], F32), ("vals", [P, ST, PW], F32), ("prob", [P, SALL], F32),
             ("probT", [P, SALL], F32), ("dbias", [P, SALL], F32)], shared)
        ada = at("ada", [P, NADA, 4, S], F32, shared)
        x_sb = at("x_sb", [P, ST, D], F32, shared + 4 * KT * S)
        o_prob = shared + 4 * KT * S + 4 * ST * PW
        o_prob = -(-o_prob // 32) * 32
        (kvc, blk, blk_hi, blk_lo, hidT), oc = row(
            [("kvc", [P, 4, S], F32), ("blk", [P, 4, 2 * NC], F32),
             ("blk_hi", [P, 2, 4, 66], F32R), ("blk_lo", [P, 2, 4, 66], F32R),
             ("hidT", [P, 2, 2, 2 * NC], F32)], o_prob)
        assert oc <= o3
        late_hi = at("late_hi", [P, LATE, D // 2], F32R, shared)
        late_lo = at("late_lo", [P, LATE, D // 2], F32R, shared + 4 * LATE * D // 2)
        assert shared + 8 * LATE * D // 2 <= o3
        mid = o3
        (ks, kw, qn, qf, kf, bias_t, u_sb, conv_y, conv_z, e_sb, pcT, sq_out), o4 = row(
            [("ks", [P, KVG, CPAD + S], F32), ("kw", [P, KVG, S], F32), ("qn", [P, S], F32),
             ("qf", [P, S], F32), ("kf", [P, S], F32), ("bias_t", [P, 2, S], F32),
             ("u_sb", [P, S], F32), ("conv_y", [P, CW - 1 + S], F32), ("conv_z", [P, S], F32),
             ("e_sb", [P, S], F32), ("pcT", [NC, S], F32), ("sq_out", [P, S], F32)], mid)
        (g_bc, y_half), o5 = row([("g_bc", [P, D], F32), ("y_half", [P, ST, D // 2], F32)], mid)
        assert o5 <= o4
        acc = at("acc", [P, 2, S], F32, mid + 4 * KVG * (CPAD + 2 * S))
        hid = at("hid", [2 * NC, 2, CMP_HID], F32, -(-place["pcT"] // 32) * 32)
        oneh = at("oneh", [BUCKETS, S], F32, place["qf"] + 4 * S + 2 * 4 * S)
        (vec, rows_a, rows_b), _ = row([("vec", [HN, VEC], F32), ("rows_a", [R_ALL, P], F32),
                                        ("rows_b", [2 * CMP_LEN, P], F32)], -(-place["conv_y"] // 32) * 32)
        assert place["rows_b"] <= place["pcT"]
        xmix = at("xmix", [P, 2, S], F32, -(-place["qf"] // 32) * 32)
        (cst, rel, cols_a, pe_cols, c_act, c_tmp, mod_sc, mod_sh,
         stat, rstd, w2, eps_c, one_c, cum, fl, fe, gate, bf, ssum, nmx, mx, rr, bias_c, pc,
         vcmp, sq, tot, rs2, rs3, b1), o6 = row(
            [("cst", [P, 3 * P + 1], F32), ("rel", [BUCKETS, HN], F32),
             ("cols_a", [P, R_ALL], F32), ("pe_cols", [P, 2, CMP_LEN], F32),
             ("c_act", [P, KT], F32), ("c_tmp", [P, KT], F32), 
             ("mod_sc", [P, KT], F32), ("mod_sh", [P, KT], F32), ("stat", [P, ST], F32),
             ("rstd", [P, ST], F32), ("w2", [P, 2, 2, HD], F32),
             ("eps_c", [P, 1], F32), ("one_c", [P, 1], F32), ("cum", [P, ST, HF], F32),
             ("fl", [P, ST, HF], F32), ("fe", [P, ST, HF], F32), ("gate", [P, ST, 3 * HN], F32),
             ("bf", [P, HF], F32), ("ssum", [P, ST], F32), ("nmx", [P, ST], F32),
             ("mx", [P, ST], F32), ("rr", [P, ST], F32), ("bias_c", [P, ST, NC], F32),
             ("pc", [P, ST, NC], F32), 
             ("vcmp", [NC, KVG, HD], F32), ("sq", [P, ST, 3], F32), ("tot", [P, ST], F32),
             ("rs2", [P, ST], F32), ("rs3", [P, ST], F32), ("b1", [P, KT], F32)], o4)
        ident, tri, ones, anym = (cst[:, 0:P], cst[:, P:2 * P], cst[:, 2 * P:3 * P],
                                  cst[:, 3 * P:3 * P + 1])
        t5_dram = nc.dram_tensor("t5_rows", [HN, VEC], F32, kind="Internal").ap()
        gate_dram = nc.dram_tensor("gate_row", [1, D], F32, kind="Internal").ap()
        t5_wide = nc.dram_tensor("t5_wide", [HN, P, VEC], F32, kind="Internal").ap()

        bank = [ctx.enter_context(nc.psum_tensor(f"bank{i}", [P, S], F32)) for i in range(8)]
        ACC = [bank[2], bank[3]]
        SB = [bank[6], bank[6], bank[5], bank[4]]
        SBO = [CPAD, 2 * CPAD + SW[0], CPAD, 0]
        SC = [bank[6][:, 0:NC], bank[6][:, CPAD + SW[0]:CPAD + SW[0] + NC], bank[5][:, 0:NC],
              bank[6][:, 2 * CPAD + SW[0] + SW[1]:2 * CPAD + SW[0] + SW[1] + NC]]
        T0, T1, OB = bank[0], bank[1], bank[7]
        YB = [bank[i] for i in (1, 2, 7, 3, 4, 5, 6, 0)]

        def sem(name):
            return ctx.enter_context(nc.semaphore(name))

        rows_in, const_in, misc_in, t5_out = (sem(n) for n in ("rows_in", "const_in", "misc_in", "t5_out"))
        x_in = [sem(f"x_in{i}") for i in range(ST)]
        raw_in = [sem(f"raw_in{i}") for i in range(NRAW)]
        ada_in = [sem(f"ada_in{i}") for i in range(NADA)]
        bias_in = [sem(f"bias_in{i}") for i in range(2)]
        xa_in = [sem(f"xa_in{i}") for i in range(2)]
        stored = [sem(f"stored{i}") for i in range(2)]
        rows_T, t5_mm, xT_mm, mod_mm, unit_used = (
            sem(n) for n in ("rows_T", "t5_mm", "xT_mm", "mod_mm", "unit_used"))
        cum_mm, cumb_mm, s_mm, t_mm, o_mm = (
            sem(n) for n in ("cum_mm", "cumb_mm", "s_mm", "t_mm", "o_mm"))
        hidT_mm, kvcmp_mm, y_mm = (sem(n) for n in ("hidT_mm", "kvcmp_mm", "y_mm"))
        act_seq, hi_done, xT_act, first_act, val_act, tile_act = (
            sem(n) for n in ("act_seq", "hi_done", "xT_act", "first_act", "val_act", "tile_act"))
        c_exp, x_sq, x_std, gate_exp, f_exp, f_ln, z_exp, hid_exp = (
            sem(n) for n in ("c_exp", "x_sq", "x_std", "gate_exp", "f_exp", "f_ln", "z_exp", "hid_exp"))
        p_exp, pc_exp, pT_act, d_act, yh_hi, y_act, y_sq, y_std, kc_act = (
            sem(n) for n in ("p_exp", "pc_exp", "pT_act", "d_act", "yh_hi", "y_act", "y_sq", "y_std",
                             "kc_act"))
        dve_seq, lo_done, ada_used, acc_done, xn_done, xT_dve, first_dve, val_dve, tile_dve = (
            sem(n) for n in ("dve_seq", "lo_done", "ada_used", "acc_done", "xn_done", "xT_dve",
                             "first_dve", "val_dve", "tile_dve"))
        cols_done, c_done, vec_done, mod_read, h_ready, stat_v, f_abs, logf_done, cum_done = (
            sem(n) for n in ("cols_done", "c_done", "vec_done", "mod_read", "h_ready", "stat_v",
                             "f_abs", "logf_done", "cum_done"))
        nmx_done, sc_sub, p_done, pc_done, pT_dve, pcT_dve, o_done = (
            sem(n) for n in ("nmx_done", "sc_sub", "p_done", "pc_done", "pT_dve", "pcT_dve", "o_done"))
        hid_done, hidT_done, kvcmp_done, y_ready, y_dve, y_tot, fin_done = (
            sem(n) for n in ("hid_done", "hidT_done", "kvcmp_done", "y_ready", "y_dve", "y_tot",
                             "fin_done"))
        early_act, rstd_done, xn_act = sem("early_act"), sem("rstd_done"), sem("xn_act")
        g_in, g_done = sem("g_in"), sem("g_done")
        row_out = [sem(f"row_out{i}") for i in range(2)]
        mod_done, h_full, h_rounded, yh_sq = (sem(n) for n in ("mod_done", "h_full", "h_rounded", "yh_sq"))
        first_lo, yg_done = sem("first_lo"), sem("yg_done")
        pool_seq, blk_done, d_done, bias_c_done = (
            sem(n) for n in ("pool_seq", "blk_done", "d_done", "bias_c_done"))

        block = ctx.enter_context(nc.Block())

        def on_act(t):
            return TILES[t][0] in ("qn", "qf", "kf", "u") and t >= EARLY

        taken, n_act, n_dve = [], 0, 0
        for t in range(NT):
            if on_act(t):
                n_act += 1
                taken.append((tile_act, n_act))
            else:
                n_dve += 1
                taken.append((tile_dve, n_dve))
        index = {name: t for t, name in enumerate(TILES)}
        z_order = [t for t, (kind, _) in enumerate(TILES) if kind in ("zn", "zf", "za")]

        def y_of(kind, i):
            return {"za": i, "zf": CT + i, "zn": CT + HF + i}[kind]

        def partial(t):
            kind, i = TILES[t]
            return {"kw": kw[:, i % KVG, :], "u": u_sb[:, :], "gc": conv_y[:, CW - 1:]}[kind]

        def lo_of(u):
            return (first_lo, u + 1) if u < N_FIRST else (lo_done, u + 1 - N_FIRST)

        def split(u):
            n = UNITS[u][2]
            if u >= FIRST_LATE:
                return late_hi[:, u - FIRST_LATE, :], late_lo[:, u - FIRST_LATE, :]
            return w_hi[:, u % NSPLIT, 0:n], w_lo[:, u % NSPLIT, 0:n]

        @block.sync
        def _(sp):
            sp.dma_start(rows_a[R_C:R_C + KT, :], c.rearrange("o (k p) -> (o k) p", p=P)).then_inc(rows_in, 16)
            sp.dma_start(rows_a[R_PRE:R_PRE + KT, :], pre_norm.rearrange("o (k p) -> (o k) p", p=P)).then_inc(rows_in, 16)
            sp.dma_start(rows_a[R_ADA:R_ADA + 3 * KT, :], b_ada.rearrange("o (k p) -> (o k) p", p=P)).then_inc(rows_in, 16)
            sp.dma_start(rows_a[R_CONV:R_CONV + CW * CT, :], conv_w.rearrange("o j (k p) -> (o j k) p", p=P)).then_inc(rows_in, 16)
            sp.dma_start(rows_a[R_POST:R_POST + KT, :], post_norm.rearrange("o (k p) -> (o k) p", p=P)).then_inc(rows_in, 16)
            sp.dma_start(rows_b[0:CMP_LEN, :], pe_k[0]).then_inc(rows_in, 16)
            sp.dma_start(rows_b[CMP_LEN:2 * CMP_LEN, :], pe_v[0]).then_inc(rows_in, 16)
            sp.dma_start(cst[:, :], consts).then_inc(const_in, 16)
            for s in range(ST):
                sp.dma_start(x_sb[:, s, :], x[0, s * P:(s + 1) * P, :]).then_inc(x_in[s], 16)

            def ada_unit(n):
                chunk, q = n // 4, n % 4
                if n >= NADA:
                    sp.wait_ge(ada_used, n - NADA + 1)
                rows = w_ada[0, q * S:(q + 1) * S, :].rearrange("(k p) n -> p k n", p=P)
                if chunk < D // 256:
                    for half in range(2):
                        sp.dma_start(ada[:, n % NADA, :, half * 256:(half + 1) * 256],
                                     rows[:, :, half * D + chunk * 256:half * D + (chunk + 1) * 256]
                                     ).then_inc(ada_in[n % NADA], 16)
                else:
                    c0 = 2 * D + (chunk - D // 256) * S
                    sp.dma_start(ada[:, n % NADA, :, :], rows[:, :, c0:c0 + S]).then_inc(ada_in[n % NADA], 32)

            def weight_unit(u):
                kind, where, n = UNITS[u]
                if u >= NRAW:
                    sp.wait_ge(*lo_of(u - NRAW))
                dst = w_raw[:, u % NRAW, 0:n]
                if kind == "first":
                    src = w_in[0, where[0] * P:(where[0] + 1) * P, KC:KC + 3 * KV]
                elif kind == "panel":
                    b, k, step = where
                    c0, w, _ = PANEL[b]
                    dst = dst.rearrange("p (k n) -> p k n", k=step)
                    src = w_in[0, k * P:(k + step) * P, c0:c0 + w].rearrange("(k p) n -> p k n", p=P)
                elif kind == "tile":
                    (name, i), half = TILES[where[0]], where[1]
                    c0, n_k = COL0[name] + i * P, KT // 2
                    dst = dst.rearrange("p (k n) -> p k n", k=n_k)
                    src = w_in[0, half * n_k * P:(half + 1) * n_k * P, c0:c0 + P].rearrange(
                        "(k p) n -> p k n", p=P)
                elif kind == "cmp":
                    w1, q = (w1_k, w1_v)[where[0] // 8], where[0] % 8
                    dst = dst.rearrange("p (k n) -> p k n", k=4)
                    src = w1[0, q * S:(q + 1) * S, :].rearrange("(k p) n -> p k n", p=P)
                else:
                    half, k = where
                    src = w_out[0, k * P:(k + 1) * P, half * D // 2:(half + 1) * D // 2]
                sp.dma_start(dst, src).then_inc(raw_in[u % NRAW], 16)

            for chunk in range(D // 256):
                for q in range(4):
                    ada_unit(4 * chunk + q)
                if chunk == 0:
                    sp.dma_start(oneh[:, :], onehot).then_inc(misc_in, 16)
                    sp.dma_start(rel[:, :], rel_bias).then_inc(misc_in, 16)
                    sp.dma_start(bf[:, :], b_forget.broadcast_to([P, HF])).then_inc(misc_in, 16)
                    sp.dma_start(w2[:, 0, :, :], w2_k[0].rearrange("(k p) n -> p k n", p=P)).then_inc(misc_in, 16)
                    sp.dma_start(w2[:, 1, :, :], w2_v[0].rearrange("(k p) n -> p k n", p=P)).then_inc(misc_in, 16)
                for u in range(FIRST_AT[2 * chunk], (FIRST_AT + [N_FIRST] * 2)[2 * chunk + 2]):
                    weight_unit(u)
            sp.wait_ge(vec_done, 1)
            sp.dma_start(t5_dram, vec[:, :]).then_inc(t5_out, 16)
            for i in range(N_PANEL):
                weight_unit(N_FIRST + i)
                if i < 16:
                    ada_unit(4 * (D // 256) + i)
                if i == 2:
                    sp.wait_ge(t5_out, 16)
                    sp.dma_start(t5_wide, bass.AP(tensor=t5_dram.tensor, offset=0,
                                                  ap=[[VEC, HN], [0, P], [1, VEC]])).then_inc(t5_out, 16)
            sp.wait_ge(t5_out, 32)

            def bias_load(h):
                if h >= 2:
                    sp.wait_ge(nmx_done, 3 * (h - 2) + 2)
                    sp.wait_ge(bias_c_done, h - 1)
                src = bass.AP(tensor=t5_wide.tensor, offset=h * P * VEC + P - 1, ap=[[VEC - 1, P], [1, S]])
                sp.dma_start(bias_t[:, h % 2, :], src).then_inc(bias_in[h % 2], 16)

            bias_load(0)
            for t in range(NT):
                if (t + 2) % 7 == 0 and (t + 2) // 7 < HN:
                    bias_load((t + 2) // 7)
                for u in range(AT[t], AT[t + 1]):
                    weight_unit(u)
            for u in range(AT[NT], NU):
                weight_unit(u)
            sp.wait_ge(*lo_of(NU - 1))
            for s in range(2):
                sp.dma_start(x_again[:, s, :], x[0, s * P:(s + 1) * P, :]).then_inc(xa_in[s], 16)
            for s in range(ST):
                for half in range(2):
                    cs = slice(half * D // 2, (half + 1) * D // 2)
                    sp.wait_ge(fin_done, 2 * s + half + 1)
                    sp.dma_start(out[0, s * P:(s + 1) * P, cs], fin[:, s % 2, cs]).then_inc(stored[s % 2], 16)
                if s + 2 < ST:
                    sp.dma_start(x_again[:, s % 2, :], x[0, (s + 2) * P:(s + 3) * P, :]).then_inc(xa_in[s % 2], 16)
            for i in range(2):
                sp.wait_ge(stored[i], 32 * (ST // 2))

        @block.tensor
        def _(pe):
            def exact(dst, a_hi, a_lo, b_hi, b_lo, first, last):
                pe.matmul(dst, a_hi, b_hi, start=first, stop=False)
                pe.matmul(dst, a_hi, b_lo, start=False, stop=False)
                return pe.matmul(dst, a_lo, b_hi, start=False, stop=last)

            pe.wait_ge(const_in, 16)
            pe.wait_ge(rows_in, 112)
            pe.transpose(bank[7][:, 0:R_ALL], rows_a[:, :], ident[0:R_ALL, 0:R_ALL])
            pe.transpose(bank[7][:, P:P + 2 * CMP_LEN], rows_b[:, :],
                         ident[0:2 * CMP_LEN, 0:2 * CMP_LEN]).then_inc(rows_T, 1)
            def modulation(chunk):
                pe.wait_ge(acc_done, chunk + 1)
                pe.wait_ge(cols_done, 1)
                if chunk >= 1:
                    pe.wait_ge(mod_read, chunk)
                for j in range(4):
                    mm = pe.matmul(bank[7][:, 4 * chunk + j:4 * chunk + j + 1],
                                   acc[:, chunk % 2, j * P:(j + 1) * P], ones[:, 0:1], start=True, stop=True)
                mm.then_inc(mod_mm, 1)

            def gate_row(chunk):
                pe.wait_ge(acc_done, chunk + 1)
                pe.wait_ge(mod_read, chunk)
                pe.matmul(bank[7][0:1, :], ones[:, 0:1], acc[:, chunk % 2, :], start=True, stop=True).then_inc(mod_mm, 1)

            pe.wait_ge(xn_done, ST // 2)
            pe.wait_ge(xn_act, ST // 2)
            for k in range(KT):
                if k >= 6:
                    pe.wait_ge(xT_act, k - 5)
                for s in range(ST):
                    mm = pe.transpose(bank[k % 6][:, s * P:(s + 1) * P], x_sb[:, s, k * P:(k + 1) * P], ident)
                mm.then_inc(xT_mm, 1)
            pe.wait_ge(misc_in, 80)
            pe.matmul(bank[6][0:HN, 0:S], rel[:, :], oneh[:, :], start=True, stop=True).then_inc(t5_mm, 1)

            modulation(0)
            for k in range(KT):
                pe.wait_ge(h_ready, k + 1)
                u = FIRST_AT[k]
                pe.wait_ge(*lo_of(u))
                if k == 0:
                    pe.wait_ge(xT_act, KT)
                hi, lo = split(u)
                for m in range(6):
                    cs = slice(m * P, (m + 1) * P)
                    mm = exact(bank[m][:, :], hi[:, cs], lo[:, cs], h_hi[:, k, :], h_lo[:, k, :],
                               k == 0, k == KT - 1)
                mm.then_inc(unit_used, 1)
                if k % 2 == 0 and k // 2 + 1 < D // 256:
                    modulation(k // 2 + 1)
                e = next((t for t in range(EARLY) if HALF_AT[t, 0] == u + 1), None)
                if e is not None:
                    pe.wait_ge(*lo_of(u + 1))
                    if e == 0:
                        pe.wait_ge(vec_done, 1)
                    else:
                        pe.wait_ge(early_act, e)
                    hi, lo = split(u + 1)
                    for i in range(KT // 2):
                        cs = slice(i * P, (i + 1) * P)
                        mm = exact(bank[6][:, :], hi[:, cs], lo[:, cs], h_hi[:, i, :], h_lo[:, i, :],
                                   i == 0, i == KT // 2 - 1)
                    mm.then_inc(unit_used, 1)
            u = N_FIRST
            gate_chunk = D // 256
            for b, (_, n, _) in enumerate(PANEL):
                step = 2 if n > 280 else 4
                for k0 in range(0, KT, step):
                    pe.wait_ge(*lo_of(u))
                    hi, lo = split(u)
                    for k in range(k0, k0 + step):
                        ws = slice((k - k0) * n, (k - k0 + 1) * n)
                        for s in range(ST):
                            a = ST * b + s
                            if k == 0:
                                if a < 6:
                                    if a % 2 == 0:
                                        pe.wait_ge(first_act, a // 2 + 1)
                                    else:
                                        pe.wait_ge(first_dve, a // 2 + 1)
                                elif a == 6:
                                    pe.wait_ge(early_act, EARLY)
                                elif (a - 7) % 2 == 0:
                                    pe.wait_ge(val_act, (a - 7) // 2 + 1)
                                else:
                                    pe.wait_ge(val_dve, (a - 7) // 2 + 1)
                            ps = slice(s * P, (s + 1) * P)
                            mm = exact(bank[a % 7][:, 0:n], h_hi[:, k, ps], h_lo[:, k, ps], hi[:, ws], lo[:, ws],
                                       k == 0, k == KT - 1)
                    mm.then_inc(unit_used, 1)
                    u += 1
                    if (u - N_FIRST) % 4 == 1 and u - N_FIRST > 4 and gate_chunk < D // 256 + 4:
                        gate_row(gate_chunk)
                        gate_chunk += 1

            def compress(q):
                u = CMP_AT[q]
                pe.wait_ge(*lo_of(u))
                pe.wait_ge(blk_done, q + 1)
                hi, lo = split(u)
                for i in range(4):
                    cs = slice(i * CMP_HID, (i + 1) * CMP_HID)
                    mm = exact(bank[4 + q // 8][0:66, 0:CMP_HID], blk_hi[:, q % 2, i, :], blk_lo[:, q % 2, i, :],
                               hi[:, cs], lo[:, cs], q % 8 == 0 and i == 0, q % 8 == 7 and i == 3)
                mm.then_inc(unit_used, 1)

            def hidden_T():
                pe.wait_ge(hid_done, 1)
                for w in range(2):
                    for j in range(2):
                        mm = pe.transpose((T0, T1)[w][:, j * P:j * P + 2 * NC], hid[:, w, j * P:(j + 1) * P],
                                          ident[0:2 * NC, 0:2 * NC])
                mm.then_inc(hidT_mm, 1)

            def compressed_kv():
                pe.wait_ge(hidT_done, 1)
                for j in range(2):
                    pe.matmul(bank[4][:, 0:2 * NC], w2[:, 0, j, :], hidT[:, 0, j, :], start=(j == 0), stop=(j == 1))
                for g in range(KVG):
                    for j in range(2):
                        mm = pe.matmul(bank[4][0:NC, P + g * HD:P + (g + 1) * HD],
                                       hidT[:, 1, j, g * NC:(g + 1) * NC], w2[:, 1, j, :],
                                       start=(j == 0), stop=(j == 1))
                mm.then_inc(kvcmp_mm, 1)

            def cum_rows(g):
                pe.wait_ge(nmx_done, 3 * g + 1)
                pe.wait_ge(cum_done, 1)
                for s in range(ST):
                    mm = pe.matmul(bank[4][:, s * P:(s + 1) * P], cum[:, s, g:g + 1].to_broadcast([P, P]), ident,
                                   start=True, stop=True)
                mm.then_inc(cumb_mm, 1)

            def scores(j):
                kind, h, _ = JOBS[j]
                if j >= 1:
                    pe.wait_ge(nmx_done, j)
                if kind == "sel":
                    pe.wait_ge(*taken[index["qn", h]])
                    q, key = qn, ks[:, h // 3, CPAD:]
                    pe.wait_ge(kvcmp_done, 1)
                    pe.wait_ge(kc_act, 1)
                elif kind == "win":
                    pe.wait_ge(d_act, h + 1)
                    q, key = qn, kw[:, h // 3, :]
                else:
                    pe.wait_ge(*taken[index["kf", h]])
                    q, key = qf, kf[:, :]
                if kind == "sel":
                    both = ks[:, h // 3, :]
                    for b in range(ST - 1):
                        pe.matmul(SB[b][:, SBO[b] - CPAD:SBO[b] + SW[b]], q[:, b * P:(b + 1) * P],
                                  both[:, 0:CPAD + SW[b]], start=True, stop=True)
                    pe.matmul(SC[3], q[:, 3 * P:], both[:, 0:NC], start=True, stop=True)
                for b in range(ST - 1 if kind == "sel" else 0, ST):
                    mm = pe.matmul(SB[b][:, SBO[b]:SBO[b] + SW[b]], q[:, b * P:(b + 1) * P], key[:, 0:SW[b]],
                                   start=True, stop=True)
                mm.then_inc(s_mm, 1)

            def transposes(j, part):
                kind = JOBS[j][0]
                if part == 0:
                    pe.wait_ge(p_done, j + 1)
                    pe.wait_ge(hidT_done, 1)
                    if j >= 1:
                        pe.wait_ge(pT_act, 2 * j)
                        pe.wait_ge(pT_dve, j)
                        pe.wait_ge(pcT_dve, (j + 2) // 3)
                    for k in range(2):
                        for b in range(k, ST):
                            mm = pe.transpose((T0, T1)[k][:, (b - k) * P:(b - k + 1) * P],
                                              prob[:, SO[b] + k * P:SO[b] + (k + 1) * P], ident)
                else:
                    pe.wait_ge(pT_act, 2 * j + 1)
                    for k in range(2, ST):
                        for b in range(k, ST):
                            o = TO[k] - TO[2] + (b - k) * P
                            mm = pe.transpose(T0[:, o:o + P], prob[:, SO[b] + k * P:SO[b] + (k + 1) * P], ident)
                    if kind == "sel":
                        pe.wait_ge(pT_dve, j + 1)
                        pe.wait_ge(pc_done, j // 3 + 1)
                        for b in range(ST):
                            mm = pe.transpose(T1[0:NC, b * P:(b + 1) * P], pc[:, b, :], ident)
                mm.then_inc(t_mm, 1)

            def weighted_values(j):
                kind, h, _ = JOBS[j]
                if kind != "win" and (j // 3) * 2 + (kind == "fox") >= 1:
                    pe.wait_ge(o_done, (j // 3) * 2 + (kind == "fox"))
                pe.wait_ge(pT_act, 2 * j + 2)
                pe.wait_ge(pT_dve, j + 1)
                v0 = {"sel": PVS + (h // 3) * HD, "win": PVW + (h // 3) * HD, "fox": h * HD}[kind]
                for k in range(ST):
                    mm = pe.matmul(OB[:, k * P:], vals[:, k, v0:v0 + HD], probT[:, TO[k]:TO[k] + TW[k]],
                                   start=(k == 0 and kind != "win"), stop=(k == ST - 1 and kind != "sel"))
                if kind == "sel":
                    pe.wait_ge(pcT_dve, j // 3 + 1)
                    pe.matmul(OB[:, :], vcmp[:, h // 3, :], pcT[:, :], start=False, stop=False)
                else:
                    mm.then_inc(o_mm, 1)

            def cumulative():
                pe.wait_ge(logf_done, 1)
                flat = fl[:, :, :].rearrange("p s h -> p (s h)")
                pe.matmul(bank[7][:, 64:64 + ST * HF], tri, flat, start=True, stop=True)
                mm = pe.matmul(bank[7][:, 96:96 + ST * HF], ones, flat, start=True, stop=True)
                mm.then_inc(cum_mm, 1)

            for t in range(NT):
                if t == 0:
                    pe.wait_ge(val_dve, 5)
                    pe.wait_ge(val_act, 6)
                elif t >= 2:
                    pe.wait_ge(*taken[t - 2])
                for half in range(2):
                    if t < CMP_TILES:
                        if t == 0 and half == 0:
                            pe.wait_ge(val_act, 6)
                            pe.wait_ge(val_dve, 6)
                            pe.wait_ge(val_act, 7)
                        for i in range(CMP_PER // 2):
                            compress(CMP_PER * t + CMP_PER // 2 * half + i)
                    if t >= EARLY or half == 1:
                        u = HALF_AT[t, half]
                        pe.wait_ge(*lo_of(u))
                        hi, lo = split(u)
                        for i in range(KT // 2):
                            k, cs = half * KT // 2 + i, slice(i * P, (i + 1) * P)
                            mm = exact(ACC[t % 2][:, :], hi[:, cs], lo[:, cs], h_hi[:, k, :], h_lo[:, k, :],
                                       k == (0 if t >= EARLY else KT // 2), k == KT - 1)
                        mm.then_inc(unit_used, 1)
                    if half == 0:
                        if t == CMP_TILES:
                            hidden_T()
                        for j, (_, _, at_t) in enumerate(JOBS):
                            if t == at_t + 2:
                                transposes(j, 1)
                if t == 1:
                    cumulative()
                if t == CMP_TILES:
                    compressed_kv()
                for j, (_, g, at_t) in enumerate(JOBS):
                    if t == at_t + 2:
                        weighted_values(j)
                for j, (kind, g, at_t) in enumerate(JOBS):
                    if t == at_t + 1:
                        transposes(j, 0)
                        if kind == "sel":
                            cum_rows(g)
                for j, (_, g, at_t) in enumerate(JOBS):
                    if t == at_t:
                        scores(j)

            pe.wait_ge(pT_dve, len(JOBS))
            pe.wait_ge(pT_act, 2 * len(JOBS))
            pe.wait_ge(nmx_done, len(JOBS))
            pe.wait_ge(*taken[NT - 2])
            pe.wait_ge(o_done, 2 * HN)

            def out_step(half, i, s, u):
                hi, lo = split(u)
                k = OUT_ORDER[i]
                ps = slice(s * P, (s + 1) * P)
                for n in range(2):
                    ws = slice(n * S, (n + 1) * S)
                    if half == 0 and i == 0 and YB[2 * s + n] is ACC[(NT - 1) % 2]:
                        pe.wait_ge(*taken[NT - 1])
                    if half == 1 and i == 0:
                        pe.wait_ge((y_act, y_dve)[n], s + 1)
                    mm = exact(YB[2 * s + n][:, :], h_hi[:, k, ps], h_lo[:, k, ps], hi[:, ws], lo[:, ws],
                               i == 0, i == KT - 1)
                    if half == 0 and i == KT - 1 and (s, n) != (ST - 1, 1):
                        mm.then_inc(y_mm, 1)
                return mm

            for half in range(2):
                for i in range(KT if half == 0 else KT - LATE):
                    u = AT[NT] + half * KT + i
                    pe.wait_ge(*lo_of(u))
                    pe.wait_ge(y_ready, i + 1)
                    for s in range(ST):
                        mm = out_step(half, i, s, u)
                    mm.then_inc(unit_used, 1)
            for s in range(ST):
                for i in range(KT - LATE, KT):
                    pe.wait_ge(*lo_of(AT[NT] + KT + i))
                    mm = out_step(1, i, s, AT[NT] + KT + i)
                mm.then_inc(y_mm, 1)

        @block.scalar
        def _(act):
            seq = [0]

            def fence(ins):
                seq[0] += 1
                ins.then_inc(act_seq, 1)
                act.wait_ge(act_seq, seq[0])

            def hi_half(u):
                act.wait_ge(raw_in[u % NRAW], 16 * (u // NRAW + 1))
                if NSPLIT <= u < FIRST_LATE:
                    act.wait_ge(unit_used, u - NSPLIT + 1)
                act.activation(split(u)[0], w_raw[:, u % NRAW, 0:UNITS[u][2]], ACT.Copy).then_inc(hi_done, 1)

            act.wait_ge(cols_done, 1)
            act.activation(c_tmp[:, :], cols_a[:, R_C:R_C + KT], ACT.Exp, scale=-1.0).then_inc(c_exp, 1)
            act.wait_ge(c_exp, 1)
            act.preload_act_table(ACT.Sqrt)
            act.wait_ge(stat_v, 1)
            for s in range(ST):
                act.wait_ge(x_in[s], 16)
                act.activation(xT[:, 4 * s:4 * s + 4, :].rearrange("p k n -> p (k n)"), x_sb[:, s, :], ACT.Square,
                               accum_out=stat[:, s:s + 1]).then_inc(x_sq, 1)
            act.wait_ge(x_sq, ST)
            act.activation(rstd[:, :], stat[:, :], ACT.Sqrt, scale=1.0 / D, bias=eps_c[:, :]).then_inc(x_std, 1)
            act.wait_ge(rstd_done, 1)
            for s in range(ST // 2, ST):
                act.activation(x_sb[:, s, :], x_sb[:, s, :], ACT.Copy, scale=rstd[:, s:s + 1]).then_inc(xn_act, 1)
            for k in range(KT):
                act.wait_ge(xT_mm, k + 1)
                act.activation(xT[:, k, :], bank[k % 6][:, :], ACT.Copy).then_inc(xT_act, 1)

            def early_out(e):
                act.wait_ge(unit_used, HALF_AT[e, 0] + 1)
                act.activation(partial(e), bank[6][:, :], ACT.Copy).then_inc(early_act, 1)

            act.wait_ge(xT_act, KT)
            for chunk in range(D // 256):
                e = chunk - D // 512 - 1
                for u in range(FIRST_AT[2 * chunk], FIRST_AT[2 * chunk + 1]):
                    hi_half(u)
                if e < 0:
                    hi_half(FIRST_AT[2 * chunk + 1])
                act.wait_ge(mod_done, chunk + 1)
                for k in (2 * chunk, 2 * chunk + 1):
                    if k >= 2:
                        act.wait_ge(h_ready, k - 1)
                    act.activation(xmix[:, k % 2, :], xT[:, k, :], ACT.Identity, scale=mod_sc[:, k:k + 1],
                                   bias=mod_sh[:, k:k + 1]).then_inc(h_full, 1)
                    act.wait_ge(h_full, k + 1)
                    act.activation(h_hi[:, k, :], xmix[:, k % 2, :], ACT.Copy).then_inc(h_rounded, 1)
                if e >= 0:
                    early_out(e)
                    hi_half(FIRST_AT[2 * chunk + 1])
            early_out(EARLY - 1)
            hi_half(N_FIRST)
            act.wait_ge(unit_used, N_FIRST)
            for m in range(0, 6, 2):
                dst = kvc[:, m, :] if m < 4 else ks[:, m - 4, CPAD:]
                act.activation(dst, bank[m][:, :], ACT.Copy).then_inc(first_act, 1)

            def panel_out(a):
                b, s = a // ST, a % ST
                act.activation(vals[:, s, PANEL[b][2]:PANEL[b][2] + PANEL[b][1]], bank[a % 7][:, 0:PANEL[b][1]],
                               ACT.Copy).then_inc(val_act, 1)

            u, done = N_FIRST + 1, N_FIRST
            for b, (_, n, _) in enumerate(PANEL):
                done += 8 if n > 280 else 4
                while u < done + 2:
                    hi_half(u)
                    u += 1
                act.wait_ge(unit_used, done)
                for s in range(0, ST, 2):
                    panel_out(ST * b + s)
            act.wait_ge(val_act, 2 * len(PANEL))
            act.wait_ge(val_dve, 2 * len(PANEL))
            act.activation(gate[:, :, :], vals[:, :, PG:PG + 3 * HN], ACT.Exp, scale=-1.0).then_inc(gate_exp, 1)
            act.wait_ge(f_abs, 1)
            act.activation(fe[:, :, :], fe[:, :, :], ACT.Exp, scale=-1.0).then_inc(f_exp, 1)
            act.wait_ge(f_exp, 1)
            act.activation(fe[:, :, :], fe[:, :, :], ACT.Ln, bias=one_c[:, :]).then_inc(f_ln, 1)

            def tile_out(t):
                kind, i = TILES[t]
                if not on_act(t) and kind not in ("zn", "zf", "za"):
                    return
                act.wait_ge(unit_used, HALF_AT[t, 1] + 1)
                src = ACC[t % 2][:, :]
                if kind == "qn":
                    if i >= 1:
                        act.wait_ge(s_mm, 3 * (i - 1) + 2)
                    ins = act.activation(qn[:, :], src, ACT.Copy, scale=SCALE)
                elif kind == "qf":
                    if i >= 1:
                        act.wait_ge(s_mm, 3 * i)
                    ins = act.activation(qf[:, :], src, ACT.Copy, scale=SCALE)
                elif kind == "kf":
                    if i >= 1:
                        act.wait_ge(s_mm, 3 * i)
                    ins = act.activation(kf[:, :], src, ACT.Copy)
                elif kind == "u":
                    act.wait_ge(*taken[index["gc", i - 1]])
                    ins = act.activation(u_sb[:, :], src, ACT.Copy)
                else:
                    z = z_order.index(t)
                    if z >= 1:
                        act.wait_ge(*taken[z_order[z - 1]])
                    act.activation(e_sb[:, :], src, ACT.Exp, scale=-1.0).then_inc(z_exp, 1)
                    return
                ins.then_inc(tile_act, 1)

            def y_hi(i):
                act.activation(h_hi[:, OUT_ORDER[i], :], yT[:, OUT_ORDER[i], :], ACT.Copy).then_inc(yh_hi, 1)

            for t in range(NT + 1):
                if t < NT:
                    lead = list(range(AT[t] + 2, min(AT[t + 1] + 2, NU)))
                    for u in lead[:len(lead) // 2]:
                        hi_half(u)
                if t >= 1:
                    tile_out(t - 1)
                if t == CMP_TILES:
                    act.wait_ge(unit_used, AT[CMP_TILES])
                    for w in range(2):
                        ins = act.activation(hid[:, w, :], bank[4 + w][0:2 * NC, 0:CMP_HID], ACT.Exp, scale=-1.0)
                    ins.then_inc(hid_exp, 1)
                if t == CMP_TILES + 1:
                    act.wait_ge(kvcmp_mm, 1)
                    act.activation(ks[:, :, 0:NC], bank[4][:, 0:2 * NC].rearrange("p (g n) -> p g n", g=KVG),
                                   ACT.Copy).then_inc(kc_act, 1)
                for j, (kind, g, at_t) in enumerate(JOBS):
                    if t == at_t + 2:
                        act.wait_ge(t_mm, 2 * j + 1)
                        if j >= 1:
                            act.wait_ge(o_mm, (j // 3) * 2 + (kind == "fox")) if kind != "win" else act.wait_ge(
                                t_mm, 2 * j + 1)
                        act.activation(probT[:, TO[0]:TO[1]], T0[:, :], ACT.Copy).then_inc(pT_act, 1)
                        if kind == "sel":
                            act.wait_ge(cumb_mm, g + 1)
                            if g >= 1:
                                act.wait_ge(nmx_done, 3 * g)
                            for b in range(ST):
                                ins = act.activation(dbias[:, SO[b]:SO[b] + SW[b]], bank[4][:, 0:SW[b]], ACT.Identity,
                                                     scale=-1.0, bias=cum[:, b, g:g + 1])
                            ins.then_inc(d_act, 1)
                    if t == at_t + 1:
                        act.wait_ge(nmx_done, j + 1)
                        for b in range(ST):
                            cs = slice(SO[b], SO[b] + SW[b])
                            ins = act.activation(prob[:, cs], prob[:, cs], ACT.Exp, bias=nmx[:, b:b + 1],
                                                 accum_out=ssum[:, b:b + 1])
                        ins.then_inc(p_exp, 1)
                        if kind == "sel":
                            act.wait_ge(sc_sub, g + 1)
                            act.activation(pc[:, :, :], pc[:, :, :], ACT.Exp).then_inc(pc_exp, 1)
                if t < NT:
                    for u in lead[len(lead) // 2:]:
                        hi_half(u)
                for j, (_, g, at_t) in enumerate(JOBS):
                    if t == at_t + 2:
                        act.wait_ge(t_mm, 2 * j + 2)
                        act.activation(probT[:, TO[2]:SALL], T0[:, 0:SALL - TO[2]], ACT.Copy).then_inc(pT_act, 1)
                if t == NT - 1:
                    act.wait_ge(unit_used, HALF_AT[t, 0] + 1)
                    act.wait_ge(o_done, 2 * HN)
                    for i in range(Y_FIRST):
                        y_hi(i)
            u = AT[NT] + 2
            act.wait_ge(unit_used, AT[NT])
            for i in range(Y_FIRST, KT):
                if OUT_ORDER[i] == CT - 1:
                    act.wait_ge(*taken[index["za", CT - 1]])
                y_hi(i)
                if i == Y_FIRST + 1:
                    for slot in range(2):
                        act.wait_ge(row_out[slot], 32)
                    act.dma_start(g_bc[:, :], gate_dram.broadcast_to([P, D])).then_inc(g_in, 16)
                if i % 3 == 2 and u < AT[NT] + NSPLIT:
                    hi_half(u)
                    u += 1
            act.dma_start(y_half[:, 0:2, :].rearrange("p s n -> p (s n)"),
                          b_ada[:, 2 * D:3 * D].broadcast_to([P, D])).then_inc(g_in, 16)
            act.dma_start(y_half[:, 2:4, :].rearrange("p s n -> p (s n)"),
                          post_norm.broadcast_to([P, D])).then_inc(g_in, 16)
            while u < AT[NT] + KT + 2:
                hi_half(u)
                u += 1
            act.wait_ge(g_done, 1)
            for s in range(ST):
                act.wait_ge(y_mm, 2 * s + 1)
                act.activation(y_half[:, s, 0:S], YB[2 * s][:, :], ACT.Copy).then_inc(y_act, 1)
            while u < FIRST_LATE:
                hi_half(u)
                u += 1
            act.wait_ge(y_ready, KT)
            while u < NU:
                hi_half(u)
                u += 1
            act.wait_ge(unit_used, FIRST_LATE)
            act.wait_ge(*lo_of(NU - 1))
            for s in range(ST):
                act.wait_ge(y_dve, s + 1)
                act.wait_ge(y_act, s + 1)
                act.activation(fin[:, 1, 0:D // 2], y_half[:, s, :], ACT.Square,
                               accum_out=sq[:, s, 0:1]).then_inc(yh_sq, 1)
                act.wait_ge(yh_sq, s + 1)
            act.preload_act_table(ACT.Sqrt)
            for s in range(ST):
                act.wait_ge(y_mm, 2 * ST - 1 + s + 1)
                fence(act.activation(sq_out[:, :], YB[2 * s][:, :], ACT.Square, accum_out=sq[:, s, 1:2]))
                act.activation(sq_out[:, :], YB[2 * s + 1][:, :], ACT.Square, accum_out=sq[:, s, 2:3]).then_inc(y_sq, 1)
                act.wait_ge(y_tot, s + 1)
                act.activation(rs2[:, s:s + 1], tot[:, s:s + 1], ACT.Sqrt, scale=1.0 / D, bias=eps_c[:, :]).then_inc(y_std, 1)

        @block.vector
        def _(dve):
            seq = [0]

            def fence(ins):
                seq[0] += 1
                ins.then_inc(dve_seq, 1)
                dve.wait_ge(dve_seq, seq[0])

            def lo_half(u):
                n = UNITS[u][2]
                hi, lo = split(u)
                dve.wait_ge(hi_done, u + 1)
                dve.tensor_tensor(lo, w_raw[:, u % NRAW, 0:n], hi.bitcast(F32), ALU.subtract).then_inc(lo_done, 1)

            def reciprocal_of_one_plus(dst, src):
                fence(dve.tensor_scalar(dst, src, 1.0, None, ALU.add))
                fence(dve.reciprocal(dst, dst))

            dve.memset(eps_c[:, :], EPS)
            dve.memset(conv_y[:, 0:CW - 1], 0.0)
            dve.memset(ks[:, :, NC:CPAD], 0.0)
            dve.memset(one_c[:, :], 1.0).then_inc(stat_v, 1)
            dve.wait_ge(rows_T, 1)
            fence(dve.tensor_copy(cols_a[:, :], bank[7][:, 0:R_ALL]))
            dve.tensor_copy(pe_cols[:, :, :], bank[7][:, P:P + 2 * CMP_LEN].rearrange("p (w l) -> p w l", w=2)) \
               .then_inc(cols_done, 1)
            dve.wait_ge(c_exp, 1)
            reciprocal_of_one_plus(c_tmp[:, :], c_tmp[:, :])
            fence(dve.tensor_tensor(c_act[:, :], cols_a[:, R_C:R_C + KT], c_tmp[:, :], ALU.mult))
            fence(dve.tensor_scalar(b1[:, :], cols_a[:, R_ADA + KT:R_ADA + 2 * KT], 1.0, None, ALU.add))

            def modulate(chunk):
                if chunk >= 2:
                    dve.wait_ge(mod_mm, chunk - 1)
                dst = acc[:, chunk % 2, :]
                for k in range(KT):
                    n = 4 * chunk + k // 4
                    if k % 4 == 0:
                        dve.wait_ge(ada_in[n % NADA], 32 * (n // NADA + 1))
                    src = ada[:, n % NADA, k % 4, :]
                    if k == 0:
                        ins = dve.tensor_scalar(dst, src, c_act[:, 0:1], None, ALU.mult)
                    else:
                        ins = dve.scalar_tensor_tensor(out=dst, in0=src, scalar=c_act[:, k:k + 1], in1=dst,
                                                       op0=ALU.mult, op1=ALU.add)
                    if k == KT - 1:
                        ins.then_inc(acc_done, 1)
                        dve.wait_ge(acc_done, chunk + 1)
                        dve.sem_inc(ada_used, 1)
                    elif k % 4 == 3:
                        ins.then_inc(ada_used, 1)
                        dve.wait_ge(ada_used, n + 1)
                    else:
                        fence(ins)

            def make_h(chunk):
                dve.wait_ge(mod_mm, chunk + 1)
                k = slice(2 * chunk, 2 * chunk + 2)
                m0 = 4 * chunk
                dve.tensor_tensor(mod_sh[:, k], bank[7][:, m0:m0 + 2], cols_a[:, R_ADA + 2 * chunk:R_ADA + 2 * chunk + 2],
                                  ALU.add)
                dve.tensor_tensor(mod_sc[:, k], bank[7][:, m0 + 2:m0 + 4], b1[:, k], ALU.add).then_inc(mod_read, 1)
                dve.wait_ge(mod_read, chunk + 1)
                dve.tensor_tensor(mod_sc[:, k], mod_sc[:, k], cols_a[:, R_PRE + 2 * chunk:R_PRE + 2 * chunk + 2],
                                  ALU.mult).then_inc(mod_done, 1)

            dve.wait_ge(x_std, 1)
            dve.reciprocal(rstd[:, :], rstd[:, :]).then_inc(rstd_done, 1)
            dve.wait_ge(rstd_done, 1)
            for s in range(ST // 2):
                dve.tensor_scalar(x_sb[:, s, :], x_sb[:, s, :], rstd[:, s:s + 1], None, ALU.mult).then_inc(xn_done, 1)
            modulate(0)
            fence(dve.memset(vec[:, S:VEC], NEG))
            dve.wait_ge(t5_mm, 1)
            dve.tensor_copy(vec[:, 0:S], bank[6][0:HN, :]).then_inc(vec_done, 1)
            for chunk in range(D // 256):
                make_h(chunk)
                if chunk + 1 < D // 256:
                    modulate(chunk + 1)
            lo_half(N_FIRST)
            dve.wait_ge(unit_used, N_FIRST)
            for m in range(1, 6, 2):
                dst = kvc[:, m, :] if m < 4 else ks[:, m - 4, CPAD:]
                dve.tensor_copy(dst, bank[m][:, :]).then_inc(first_dve, 1)

            def gate_chunk(i):
                chunk = D // 256 + i
                dve.wait_ge(mod_mm, chunk + 1)
                if i >= 2:
                    dve.wait_ge(row_out[i % 2], 16)
                dve.tensor_copy((pcT, sq_out)[i % 2][0:1, :], bank[7][0:1, :]).then_inc(mod_read, 1)

            def panel_out(a):
                b, s = a // ST, a % ST
                dve.tensor_copy(vals[:, s, PANEL[b][2]:PANEL[b][2] + PANEL[b][1]], bank[a % 7][:, 0:PANEL[b][1]]) \
                   .then_inc(val_dve, 1)

            u, done, chunks, read = N_FIRST + 1, N_FIRST, 0, 0
            for b, (_, n, _) in enumerate(PANEL):
                done += 8 if n > 280 else 4
                while u < done + 2:
                    lo_half(u)
                    u += 1
                    if (u - N_FIRST) % 4 == 0 and chunks < 4:
                        modulate(D // 256 + chunks)
                        chunks += 1
                    if (u - N_FIRST) % 4 == 3 and read < chunks and u - N_FIRST > 6:
                        gate_chunk(read)
                        read += 1
                dve.wait_ge(unit_used, done)
                for s in range(1, ST, 2):
                    panel_out(ST * b + s)
            while read < 4:
                gate_chunk(read)
                read += 1
            dve.wait_ge(val_act, 2 * len(PANEL))
            dve.wait_ge(val_dve, 2 * len(PANEL))
            dve.wait_ge(misc_in, 80)
            for s in range(ST):
                ins = dve.tensor_tensor(fl[:, s, :], vals[:, s, PF:PF + HF], bf[:, :], ALU.add)
            fence(ins)
            dve.scalar_tensor_tensor(out=fe[:, :, :], in0=fl[:, :, :], scalar=-1.0, in1=fl[:, :, :],
                                     op0=ALU.mult, op1=ALU.max).then_inc(f_abs, 1)
            dve.wait_ge(gate_exp, 1)
            reciprocal_of_one_plus(gate[:, :, :], gate[:, :, :])
            fence(dve.tensor_scalar(gate[:, 0, 0:3 * HN:3], gate[:, 0, 0:3 * HN:3], anym, None, ALU.mult))
            fence(dve.tensor_scalar(fl[:, :, :], fl[:, :, :], 0.0, None, ALU.min))
            dve.wait_ge(f_ln, 1)
            dve.tensor_tensor(fl[:, :, :], fl[:, :, :], fe[:, :, :], ALU.subtract).then_inc(logf_done, 1)

            def tile_out(t):
                kind, i = TILES[t]
                src = ACC[t % 2][:, :]
                if kind in ("zn", "zf", "za"):
                    dve.wait_ge(z_exp, z_order.index(t) + 1)
                    reciprocal_of_one_plus(e_sb[:, :], e_sb[:, :])
                    dst = yT[:, y_of(kind, i), :]
                    if kind == "za":
                        fence(dve.tensor_tensor(e_sb[:, :], e_sb[:, :], conv_z[:, :], ALU.mult))
                    dve.tensor_tensor(dst, src, e_sb[:, :], ALU.mult).then_inc(tile_dve, 1)
                elif kind in ("kw", "u") and t < EARLY:
                    dve.wait_ge(unit_used, HALF_AT[t, 1] + 1)
                    dve.tensor_tensor(partial(t), src, partial(t), ALU.add).then_inc(tile_dve, 1)
                    dve.wait_ge(*taken[t])
                elif kind == "gc":
                    dve.wait_ge(unit_used, HALF_AT[t, 1] + 1)
                    dve.wait_ge(*taken[index["u", i]])
                    y0 = CW - 1
                    if t < EARLY:
                        fence(dve.tensor_tensor(partial(t), src, partial(t), ALU.add))
                        src = conv_y[:, y0:]
                    dve.tensor_tensor(conv_y[:, y0:], src, u_sb[:, :], ALU.mult).then_inc(tile_dve, 1)
                    dve.wait_ge(*taken[t])
                    w = [cols_a[:, R_CONV + j * CT + i:R_CONV + j * CT + i + 1] for j in range(CW)]
                    fence(dve.tensor_scalar(conv_z[:, :], conv_y[:, 0:S], w[0], None, ALU.mult))
                    for j in range(1, CW):
                        fence(dve.scalar_tensor_tensor(out=conv_z[:, :], in0=conv_y[:, j:j + S], scalar=w[j],
                                                       in1=conv_z[:, :], op0=ALU.mult, op1=ALU.add))
                elif kind == "gb":
                    dve.wait_ge(unit_used, HALF_AT[t, 1] + 1)
                    dve.tensor_tensor(conv_z[:, :], src, conv_z[:, :], ALU.mult).then_inc(tile_dve, 1)
                    dve.wait_ge(*taken[t])

            def softmax_in(j):
                kind, h, _ = JOBS[j]
                dve.wait_ge(s_mm, j + 1)
                if j >= 1:
                    dve.wait_ge(t_mm, 2 * j)
                if kind == "fox":
                    dve.wait_ge(d_done, h + 1)
                else:
                    dve.wait_ge(bias_in[h % 2], 16 * (h // 2 + 1))
                for b in range(ST):
                    cs = slice(SO[b], SO[b] + SW[b])
                    bias = dbias[:, cs] if kind == "fox" else bias_t[:, h % 2, S - SW[b]:S]
                    ins = dve.tensor_tensor_reduce(prob[:, cs], SB[b][:, SBO[b]:SBO[b] + SW[b]], bias, 1.0, NEG,
                                                   ALU.add, ALU.max, mx[:, b:b + 1])
                fence(ins)
                if kind == "sel":
                    dve.wait_ge(bias_c_done, h + 1)
                    for b in range(ST):
                        ins = dve.tensor_tensor(pc[:, b, :], SC[b], bias_c[:, b, :], ALU.add)
                    fence(ins)
                dve.tensor_scalar(nmx[:, :], mx[:, :], -1.0, None, ALU.mult).then_inc(nmx_done, 1)
                if kind == "sel":
                    fence(dve.tensor_reduce(rr[:, :], pc[:, :, :], AX.X, ALU.max))
                    for b in range(ST):
                        ins = dve.tensor_scalar(pc[:, b, :], pc[:, b, :], rr[:, b:b + 1], None, ALU.subtract)
                    ins.then_inc(sc_sub, 1)

            def softmax_out(j):
                kind, h, _ = JOBS[j]
                dve.wait_ge(p_exp, j + 1)
                fence(dve.reciprocal(rr[:, :], ssum[:, :]))
                if kind != "fox":
                    g = 3 * h + {"sel": 1, "win": 2}[kind]
                    fence(dve.tensor_tensor(rr[:, :], rr[:, :], gate[:, :, g], ALU.mult))
                for b in range(ST):
                    cs = slice(SO[b], SO[b] + SW[b])
                    ins = dve.tensor_scalar(prob[:, cs], prob[:, cs], rr[:, b:b + 1], None, ALU.mult)
                ins.then_inc(p_done, 1)
                if kind == "sel":
                    dve.wait_ge(pc_exp, h + 1)
                    dve.wait_ge(p_done, j + 1)
                    fence(dve.tensor_reduce(rr[:, :], pc[:, :, :], AX.X, ALU.add))
                    fence(dve.reciprocal(rr[:, :], rr[:, :]))
                    fence(dve.tensor_tensor(rr[:, :], rr[:, :], gate[:, :, 3 * h], ALU.mult))
                    for b in range(ST):
                        ins = dve.tensor_scalar(pc[:, b, :], pc[:, b, :], rr[:, b:b + 1], None, ALU.mult)
                    ins.then_inc(pc_done, 1)

            def y_lo(i):
                k = OUT_ORDER[i]
                dve.wait_ge(yh_hi, i + 1)
                dve.tensor_tensor(h_lo[:, k, :], yT[:, k, :], h_hi[:, k, :].bitcast(F32), ALU.subtract).then_inc(y_ready, 1)

            for t in range(NT + 1):
                if t < NT:
                    lead = list(range(AT[t] + 2, min(AT[t + 1] + 2, NU)))
                    for u in lead[:len(lead) // 2]:
                        lo_half(u)
                if t == 2:
                    dve.wait_ge(cum_mm, 1)
                    dve.tensor_copy(cum[:, :, :], bank[7][:, 64:64 + ST * HF].rearrange("p (s h) -> p s h", s=ST))
                    fence(dve.tensor_copy(fe[:, :, :], bank[7][:, 96:96 + ST * HF].rearrange("p (s h) -> p s h", s=ST)))
                    for s in range(1, ST):
                        if s >= 2:
                            fence(dve.tensor_tensor(fe[:, s - 1, :], fe[:, s - 1, :], fe[:, s - 2, :], ALU.add))
                        ins = dve.tensor_tensor(cum[:, s, :], cum[:, s, :], fe[:, s - 1, :], ALU.add)
                    ins.then_inc(cum_done, 1)
                if t >= 1:
                    tile_out(t - 1)
                if t == CMP_TILES:
                    dve.wait_ge(hid_exp, 1)
                    reciprocal_of_one_plus(hid[:, :, :], hid[:, :, :])
                    for w in range(2):
                        ins = dve.tensor_tensor(hid[:, w, :], bank[4 + w][0:2 * NC, 0:CMP_HID], hid[:, w, :], ALU.mult)
                    ins.then_inc(hid_done, 1)
                    dve.wait_ge(hidT_mm, 1)
                    for w in range(2):
                        src = (T0, T1)[w][:, 0:2 * P].rearrange("p (j n) -> p j n", j=2)[:, :, 0:2 * NC]
                        ins = dve.tensor_copy(hidT[:, w, :, :], src)
                    ins.then_inc(hidT_done, 1)
                if t == CMP_TILES + 1:
                    dve.wait_ge(kc_act, 1)
                    dve.tensor_copy(vcmp[:, :, :], bank[4][0:NC, P:P + KVG * HD].rearrange("p (g d) -> p g d", g=KVG)) \
                       .then_inc(kvcmp_done, 1)
                for j, (kind, g, at_t) in enumerate(JOBS):
                    if t == at_t + 3 and kind != "sel":
                        o = (j // 3) * 2 + (kind == "fox")
                        dve.wait_ge(o_mm, o + 1)
                        y = y_of("zf", g) if kind == "fox" else y_of("zn", g)
                        dve.wait_ge(*taken[index["zf" if kind == "fox" else "zn", g]])
                        dve.tensor_tensor(yT[:, y, :], OB[:, :], yT[:, y, :], ALU.mult).then_inc(o_done, 1)
                for j, (kind, g, at_t) in enumerate(JOBS):
                    if t == at_t + 2:
                        dve.wait_ge(t_mm, 2 * j + 1)
                        dve.tensor_copy(probT[:, TO[1]:TO[2]], T1[:, 0:TW[1]]).then_inc(pT_dve, 1)
                    if t == at_t + 1:
                        softmax_in(j)
                if t < NT:
                    for u in lead[len(lead) // 2:]:
                        lo_half(u)
                for j, (kind, g, at_t) in enumerate(JOBS):
                    if t == at_t + 1:
                        softmax_out(j)
                    if t == at_t + 2 and kind == "sel":
                        dve.wait_ge(t_mm, 2 * j + 2)
                        dve.tensor_copy(pcT[:, :], T1[0:NC, :]).then_inc(pcT_dve, 1)
                if t == NT - 1:
                    for i in range(Y_FIRST):
                        y_lo(i)
            u = AT[NT] + 2
            for i in range(Y_FIRST, KT):
                y_lo(i)
                if i % 3 == 2 and u < AT[NT] + NSPLIT:
                    lo_half(u)
                    u += 1
            while u < AT[NT] + KT + 2:
                lo_half(u)
                u += 1
            dve.wait_ge(g_done, 1)
            for s in range(ST):
                dve.wait_ge(y_mm, 2 * s + 2) if s < ST - 1 else dve.wait_ge(unit_used, AT[NT] + KT)
                dve.tensor_copy(y_half[:, s, S:2 * S], YB[2 * s + 1][:, :]).then_inc(y_dve, 1)
            while u < NU:
                lo_half(u)
                u += 1
            for s in range(ST):
                for n in range(2):
                    if n == 0:
                        dve.wait_ge(y_sq, s + 1)
                        dve.tensor_reduce(tot[:, s:s + 1], sq[:, s, :], AX.X, ALU.add).then_inc(y_tot, 1)
                        if s >= 2:
                            dve.wait_ge(stored[s % 2], 32 * (s // 2))
                    cs = slice(D // 2 + n * S, D // 2 + (n + 1) * S)
                    dve.wait_ge(g_done, 1)
                    ins = dve.tensor_tensor(fin[:, s % 2, cs], YB[2 * s + n][:, :], g_bc[:, cs], ALU.mult)
                fence(ins)
                dve.wait_ge(y_std, s + 1)
                fence(dve.reciprocal(rs3[:, s:s + 1], rs2[:, s:s + 1]))
                r = rs3[:, s:s + 1]
                dve.wait_ge(xa_in[s % 2], 16 * (s // 2 + 1))
                dve.wait_ge(yg_done, s + 1)
                dve.scalar_tensor_tensor(out=fin[:, s % 2, 0:D // 2], in0=y_half[:, s, :], scalar=r,
                                         in1=x_again[:, s % 2, 0:D // 2], op0=ALU.mult, op1=ALU.add).then_inc(fin_done, 1)
                dve.scalar_tensor_tensor(out=fin[:, s % 2, D // 2:], in0=fin[:, s % 2, D // 2:], scalar=r,
                                         in1=x_again[:, s % 2, D // 2:], op0=ALU.mult, op1=ALU.add).then_inc(fin_done, 1)

        @block.gpsimd
        def _(pool):
            seq = [0]

            def fence(ins):
                seq[0] += 1
                ins.then_inc(pool_seq, 1)
                pool.wait_ge(pool_seq, seq[0])

            def lo_half(u):
                pool.wait_ge(hi_done, u + 1)
                hi, lo = split(u)
                pool.tensor_tensor(lo, w_raw[:, u % NRAW, 0:UNITS[u][2]], hi.bitcast(F32),
                                   ALU.subtract).then_inc(first_lo, 1)

            for k in range(KT):
                late = k % 2 == 1 and k // 2 > D // 512
                if not late:
                    lo_half(FIRST_AT[k])
                pool.wait_ge(h_rounded, k + 1)
                pool.tensor_tensor(h_lo[:, k, :], xmix[:, k % 2, :], h_hi[:, k, :].bitcast(F32), ALU.subtract) \
                    .then_inc(h_ready, 1)
                if late:
                    lo_half(FIRST_AT[k])
                elif FIRST_AT[k] + 1 < (FIRST_AT + [N_FIRST])[k + 1]:
                    lo_half(FIRST_AT[k] + 1)
            pool.wait_ge(first_act, 3)
            pool.wait_ge(first_dve, 3)
            fence(pool.memset(blk_hi[:, :, :, 2 * NC:].bitcast(F32), 0.0))
            fence(pool.memset(blk_lo[:, :, :, 2 * NC:].bitcast(F32), 0.0))
            for q in range(16):
                if q == 2:
                    for i in range(4):
                        pool.wait_ge(mod_read, D // 256 + i + 1)
                        pool.dma_start(gate_dram[:, i * S:(i + 1) * S], (pcT, sq_out)[i % 2][0:1, :]) \
                            .then_inc(row_out[i % 2], 16)
                    for slot in range(2):
                        pool.wait_ge(row_out[slot], 32)
                w, l0 = q // 8, q % 8 * 4
                a, r = divmod(l0, CMP_STRIDE)
                kv = kvc[:, 2 * w:2 * w + 2, :].rearrange("p g (n s) -> p s g n", s=CMP_STRIDE)
                fence(pool.tensor_tensor(
                    blk[:, :, :].rearrange("p l (g n) -> p l g n", g=2), kv[:, r:r + 4, :, a:a + NC],
                    pe_cols[:, w, l0:l0 + 4].rearrange("p (l g n) -> p l g n", g=1, n=1).to_broadcast([P, 4, 2, NC]),
                    ALU.add))
                if q >= 2:
                    pool.wait_ge(unit_used, CMP_AT[q - 2] + 1)
                fence(pool.tensor_copy(blk_hi[:, q % 2, :, 0:2 * NC], blk[:, :, :]))
                pool.tensor_tensor(blk_lo[:, q % 2, :, 0:2 * NC], blk[:, :, :],
                                   blk_hi[:, q % 2, :, 0:2 * NC].bitcast(F32), ALU.subtract).then_inc(blk_done, 1)
                pool.wait_ge(blk_done, q + 1)
            for g in range(HN):
                pool.wait_ge(bias_in[g % 2], 16 * (g // 2 + 1))
                if g >= 1:
                    pool.wait_ge(nmx_done, 3 * (g - 1) + 1)
                fence(pool.memset(bias_c[:, :, :], NEG))
                for b in range(ST):
                    n = min(NC, (P // CMP_STRIDE) * (b + 1) - 1)
                    u0 = S - (b + 1) * P + CMP_LEN - 1
                    ins = pool.tensor_copy(bias_c[:, b, 0:n],
                                           bias_t[:, g % 2, u0:u0 + (n - 1) * CMP_STRIDE + 1:CMP_STRIDE])
                ins.then_inc(bias_c_done, 1)
                pool.wait_ge(d_act, g + 1)
                for b in range(ST):
                    o = SO[b] + b * P
                    ins = pool.affine_select(out=dbias[:, o:o + P], in_=dbias[:, o:o + P], compare_op=ALU.is_ge,
                                             fill=NEG, base=0, pattern=[[-1, P]], channel_multiplier=1)
                ins.then_inc(d_done, 1)
            pool.wait_ge(g_in, 48)
            fence(pool.tensor_tensor(g_bc[:, :], g_bc[:, :], y_half[:, 0:2, :].rearrange("p s n -> p (s n)"), ALU.add))
            pool.tensor_tensor(g_bc[:, :], g_bc[:, :], y_half[:, 2:4, :].rearrange("p s n -> p (s n)"),
                               ALU.mult).then_inc(g_done, 1)
            pool.wait_ge(g_done, 1)
            for s in range(ST):
                pool.wait_ge(yh_sq, s + 1)
                pool.tensor_tensor(y_half[:, s, :], y_half[:, s, :], g_bc[:, 0:D // 2], ALU.mult).then_inc(yg_done, 1)


def bias_buckets():
    half = BUCKETS // 2
    dist = np.arange(S - 1, -1, -1)
    far = np.maximum(dist, half).astype(np.float32)
    large = half + (np.log(far / np.float32(half)) / np.float32(np.log(MAX_DIST / half))
                    * np.float32(BUCKETS - half)).astype(np.int32)
    bucket = np.where(dist < half, dist, np.minimum(large, BUCKETS - 1))
    return (np.arange(BUCKETS)[:, None] == bucket[None, :]).astype(np.float32)


def shape_constants():
    i = np.arange(P)
    return np.concatenate([np.eye(P), i[:, None] <= i[None, :], np.ones((P, P)),
                           i[:, None] >= CMP_LEN - 1], axis=1).astype(np.float32)


_INS = ["x", "c", "w_ada", "b_ada", "pre_norm", "post_norm", "w_in", "b_forget", "conv_w", "cmp_pe_k",
        "cmp_w1_k", "cmp_w2_k", "cmp_pe_v", "cmp_w1_v", "cmp_w2_v", "w_out", "rel_bias"]


def kernel(**inputs):
    import concourse.bacc as bacc
    from concourse.bass_utils import run_bass_kernel_spmd

    nc = bacc.Bacc("TRN2", target_bir_lowering=False, num_devices=1, dynamic_dma_scratch_size=1024)
    arrays = {name: np.ascontiguousarray(inputs[name]) for name in _INS}
    arrays["consts"], arrays["onehot"] = shape_constants(), bias_buckets()
    args = [nc.dram_tensor(name, a.shape, mybir.dt.from_np(a.dtype), kind="ExternalInput").ap()
            for name, a in arrays.items()]
    out = nc.dram_tensor("out", [1, S, D], F32, kind="ExternalOutput").ap()
    layer_program(nc, *args, out)
    r = run_bass_kernel_spmd(nc, [arrays], core_ids=[0])
    return r.results[0]["out"]
```

```python
from contextlib import ExitStack

import numpy as np

import concourse.bass as bass
from concourse import mybir

F32 = mybir.dt.float32
F32R = mybir.dt.float32r
ALU = mybir.AluOpType
ACT = mybir.ActivationFunctionType
AX = mybir.AxisListType

P = 128
D = 2048
S = 512
KT = D // P
ST = S // P
HD = 128
D_CONV = D // 4
D_FOX = 3 * D // 8
D_NSA = D - D_CONV - D_FOX
HF = D_FOX // HD
HN = D_NSA // HD
KVG = 2
CT = D_CONV // P
CW = 3
CMP_LEN, CMP_STRIDE, CMP_HID = 32, 16, 256
NC = (S - CMP_LEN) // CMP_STRIDE + 1
CPAD = 32
BUCKETS, MAX_DIST = 32, 128
EPS = 1e-6
NEG = -1e30
SCALE = HD ** -0.5

U_A = 0
GB_A, GC_A, Z_A = D_CONV, 2 * D_CONV, 3 * D_CONV
Q_F = 4 * D_CONV
K_F, V_F = Q_F + D_FOX, Q_F + 2 * D_FOX
F_F = Q_F + 3 * D_FOX
Z_F = F_F + HF
Q_N = Z_F + D_FOX
KV = KVG * HD
KC, VC, KS, VS, KW, VW = (Q_N + D_NSA + i * KV for i in range(6))
G_N = VW + KV
Z_N = G_N + 3 * HN
N_IN = Z_N + D_NSA

R_C, R_PRE, R_ADA, R_CONV = 0, KT, 2 * KT, 5 * KT
R_ALL = R_CONV + CW * CT

PANEL = [(V_F, 512, 0), (V_F + 512, D_FOX + HF - 512, 512), (VS, KV, D_FOX + HF),
         (VW, KV + 3 * HN, D_FOX + HF + KV)]
PW = sum(n for _, n, _ in PANEL)
PF, PVS, PVW, PG = D_FOX, D_FOX + HF, D_FOX + HF + KV, D_FOX + HF + 2 * KV

SLOT = 1120
NRAW, NSPLIT, NADA = 4, 4, 4
STORES = [2] * (ST - 1) + [4]
VEC = S + P

SW = [(b + 1) * P for b in range(ST)]
SO = [sum(SW[:b]) for b in range(ST)]
SALL = sum(SW)
TW = [S - k * P for k in range(ST)]
TO = [sum(TW[:k]) for k in range(ST)]


def tiles_and_jobs():
    conv = [(kind, i) for i in range(CT) for kind in ("u", "gc", "gb", "za")]
    tiles = [("kw", 0), ("kw", 1), conv.pop(0), conv.pop(0)]
    jobs = []
    for g in range(HN):
        b = len(tiles)
        tiles += [("qn", g), ("qf", g), ("zn", g), ("kf", g), ("zf", g), conv.pop(0), conv.pop(0)]
        jobs += [("sel", g, b + 1), ("win", g, b + 3), ("fox", g, b + 5)]
    return tiles + conv, jobs


TILES, JOBS = tiles_and_jobs()
NT = len(TILES)
CMP_TILES, CMP_PER = 4, 4
EARLY = 4
AHEAD = 3
HEAD_TILES = 7
LATE = 8
Y_FIRST = 4
OUT_ORDER = [k for k in range(KT) if k != CT - 1] + [CT - 1]
COL0 = {"kw": KW, "qn": Q_N, "zn": Z_N, "qf": Q_F, "kf": K_F, "zf": Z_F,
        "u": U_A, "gc": GC_A, "gb": GB_A, "za": Z_A}


EARLY_PARTS = {1: [(0, 0, 3)], 2: [(1, 0, 5)], 3: [(2, 0, 7)], 4: [(3, 0, 4), (3, 4, 4)],
               5: [(0, 3, 4), (0, 7, 4)], 6: [(1, 5, 4), (1, 9, 4)]}
ROUND_TWO = 5


def weight_units():
    units, first_at, early_at, parts, cmp_at = [], [], {}, [], {}
    for k in range(KT):
        first_at.append(len(units))
        units.append(("first", (k,), KV * 3))
        for part in EARLY_PARTS.get(k // 2, []) if k % 2 == 0 else []:
            early_at[part] = len(units)
            units.append(("tile", part, part[2] * P))
    n_first = len(units)
    for b, (_, n, _) in enumerate(PANEL):
        step = 2 if n > 280 else 4
        units += [("panel", (b, k, step), step * n) for k in range(0, KT, step)]
    at = []
    for t in range(NT):
        at.append(len(units))
        k0 = sum(n for tile, _, n in early_at if tile == t)
        mid = (k0 + KT) // 2 + k0 % 2
        parts.append([])
        for h, (k, n) in enumerate(((k0, mid - k0), (mid, KT - mid))):
            if t < CMP_TILES:
                for i in range(CMP_PER // 2):
                    q = CMP_PER * t + CMP_PER // 2 * h + i
                    cmp_at[q] = len(units)
                    units.append(("cmp", (q,), 4 * CMP_HID))
            parts[t].append((k, n, len(units)))
            units.append(("tile", (t, k, n), n * P))
    at.append(len(units))
    units += [("out", (n, k), D // 2) for n in range(2) for k in OUT_ORDER]
    return units, n_first, first_at, early_at, at, parts, cmp_at


UNITS, N_FIRST, FIRST_AT, EARLY_AT, AT, PARTS, CMP_AT = weight_units()
EARLY_END = {chunk: EARLY_AT[parts[-1]] + 1 for chunk, parts in EARLY_PARTS.items()}
NU = len(UNITS)
FIRST_LATE = NU - LATE
N_PANEL = AT[0] - N_FIRST


def layer_program(nc, x, c, w_ada, b_ada, pre_norm, post_norm, w_in, b_forget, conv_w,
                  pe_k, w1_k, w2_k, pe_v, w1_v, w2_v, w_out, rel_bias, consts, onehot, out):
    ctx = ExitStack()
    with ctx:
        top = [ctx.enter_context(nc.sbuf_tensor("arena", [P, 56960], F32))]
        base = 1152
        place = {}

        def at(name, shape, dt, offset):
            place[name] = offset + 4 * int(np.prod(shape[1:]))
            assert place[name] <= base + 4 * 56960, (name, place[name])
            return nc.alloc_sbuf_tensor_at(name, shape, dt, offset=offset)

        def row(names, offset):
            made = []
            for name, shape, dt in names:
                made.append(at(name, shape, dt, offset))
                offset = -(-place[name] // 32) * 32
            return made, offset

        (h_hi, h_lo), o = row([("h_hi", [P, KT, S], F32R), ("h_lo", [P, KT, S], F32R)], base)
        xT = at("xT", [P, KT, S], F32, base + 4 * KT * S)
        (w_raw, w_hi, w_lo), o2 = row([("w_raw", [P, NRAW, SLOT], F32),
                                       ("w_hi", [P, NSPLIT, SLOT], F32R),
                                       ("w_lo", [P, NSPLIT, SLOT], F32R)], o)
        x_again = at("x_again", [P, 2, D], F32, o)
        fin = at("fin", [P, 2, D], F32, o + 4 * NRAW * SLOT)
        shared = o2
        (yT, vals, prob, probT, dbias), o3 = row(
            [("yT", [P, KT, S], F32), ("vals", [P, ST, PW], F32), ("prob", [P, SALL], F32),
             ("probT", [P, SALL], F32), ("dbias", [P, SALL], F32)], shared)
        ada = at("ada", [P, NADA, 4, S], F32, shared)
        x_sb = at("x_sb", [P, ST, D], F32, shared + 4 * KT * S)
        o_prob = shared + 4 * KT * S + 4 * ST * PW
        o_prob = -(-o_prob // 32) * 32
        (kvc, blk, blk_hi, blk_lo, hidT), oc = row(
            [("kvc", [P, 4, S], F32), ("blk", [P, 4, 2 * NC], F32),
             ("blk_hi", [P, 2, 4, 66], F32R), ("blk_lo", [P, 2, 4, 66], F32R),
             ("hidT", [P, 2, 2, 2 * NC], F32)], o_prob)
        assert oc <= o3
        late_hi = at("late_hi", [P, LATE, D // 2], F32R, shared)
        late_lo = at("late_lo", [P, LATE, D // 2], F32R, shared + 4 * LATE * D // 2)
        assert shared + 8 * LATE * D // 2 <= o3
        mid = o3
        (ks, kw, qn, qf, kf, bias_t, u_sb, conv_y, conv_z, e_sb, pcT, sq_out), o4 = row(
            [("ks", [P, KVG, CPAD + S], F32), ("kw", [P, KVG, S], F32), ("qn", [P, S], F32),
             ("qf", [P, S], F32), ("kf", [P, S], F32), ("bias_t", [P, 2, S], F32),
             ("u_sb", [P, S], F32), ("conv_y", [P, CW - 1 + S], F32), ("conv_z", [P, S], F32),
             ("e_sb", [P, S], F32), ("pcT", [NC, S], F32), ("sq_out", [P, S], F32)], mid)
        (g_bc, y_half), o5 = row([("g_bc", [P, D], F32), ("y_half", [P, ST, D // 2], F32)], mid)
        assert o5 <= o4
        acc = at("acc", [P, 2, S], F32, mid + 4 * KVG * (CPAD + 2 * S))
        hid = at("hid", [2 * NC, 2, CMP_HID], F32, -(-place["pcT"] // 32) * 32)
        oneh = at("oneh", [BUCKETS, S], F32, place["qf"] + 4 * S + 2 * 4 * S)
        (vec, rows_a, rows_b), _ = row([("vec", [HN, VEC], F32), ("rows_a", [R_ALL, P], F32),
                                        ("rows_b", [2 * CMP_LEN, P], F32)], -(-place["conv_y"] // 32) * 32)
        assert place["rows_b"] <= place["pcT"]
        cum_T = at("cum_T", [HF * ST, P], F32, -(-place["qf"] // 32) * 32)
        xmix = at("xmix", [P, 2, S], F32, -(-place["qf"] // 32) * 32)
        (cst, rel, cols_a, pe_cols, c_act, c_tmp, mod_sc, mod_sh,
         stat, rstd, w2, eps_c, one_c, cum, fl, fe, gate, bf, ssum, nmx, mx, rr, bias_c, pc,
         vcmp, sq, tot, rs2, rs3, b1), o6 = row(
            [("cst", [P, 3 * P + 1], F32), ("rel", [BUCKETS, HN], F32),
             ("cols_a", [P, R_ALL], F32), ("pe_cols", [P, 2, CMP_LEN], F32),
             ("c_act", [P, KT], F32), ("c_tmp", [P, KT], F32),
             ("mod_sc", [P, KT], F32), ("mod_sh", [P, KT], F32), ("stat", [P, ST], F32),
             ("rstd", [P, ST], F32), ("w2", [P, 2, 2, HD], F32),
             ("eps_c", [P, 1], F32), ("one_c", [P, 1], F32), ("cum", [P, ST, HF], F32),
             ("fl", [P, ST, HF], F32), ("fe", [P, ST, HF], F32), ("gate", [P, ST, 3 * HN], F32),
             ("bf", [P, HF], F32), ("ssum", [P, ST], F32), ("nmx", [P, ST], F32),
             ("mx", [P, ST], F32), ("rr", [P, ST], F32), ("bias_c", [P, ST, NC], F32),
             ("pc", [P, ST, NC], F32),
             ("vcmp", [NC, KVG, HD], F32), ("sq", [P, ST, 3], F32), ("tot", [P, ST], F32),
             ("rs2", [P, ST], F32), ("rs3", [P, ST], F32), ("b1", [P, KT], F32)], o4)
        ident, tri, ones, anym = (cst[:, 0:P], cst[:, P:2 * P], cst[:, 2 * P:3 * P],
                                  cst[:, 3 * P:3 * P + 1])
        t5_dram = nc.dram_tensor("t5_rows", [HN, VEC], F32, kind="Internal").ap()
        cum_dram = nc.dram_tensor("cum_rows", [ST * HF, P], F32, kind="Internal").ap()
        gate_dram = nc.dram_tensor("gate_row", [1, D], F32, kind="Internal").ap()
        t5_wide = nc.dram_tensor("t5_wide", [HN, P, VEC], F32, kind="Internal").ap()

        bank = [ctx.enter_context(nc.psum_tensor(f"bank{i}", [P, S], F32)) for i in range(8)]
        ACC = [bank[2], bank[3]]
        SB = [bank[6], bank[6], bank[5], bank[4]]
        SBO = [CPAD, 2 * CPAD + SW[0], CPAD, 0]
        SC = [bank[6][:, 0:NC], bank[6][:, CPAD + SW[0]:CPAD + SW[0] + NC], bank[5][:, 0:NC],
              bank[6][:, 2 * CPAD + SW[0] + SW[1]:2 * CPAD + SW[0] + SW[1] + NC]]
        T0, T1, OB = bank[0], bank[1], bank[7]
        YB = [bank[i] for i in (1, 2, 7, 0, 4, 5, 6, 3)]

        def sem(name):
            return ctx.enter_context(nc.semaphore(name))

        rows_in, const_in, misc_in, t5_out = (sem(n) for n in ("rows_in", "const_in", "misc_in", "t5_out"))
        x_in = [sem(f"x_in{i}") for i in range(ST)]
        raw_in = [sem(f"raw_in{i}") for i in range(NRAW)]
        ada_in = [sem(f"ada_in{i}") for i in range(NADA)]
        bias_in = [sem(f"bias_in{i}") for i in range(2)]
        xa_in = [sem(f"xa_in{i}") for i in range(2)]
        stored = [sem(f"stored{i}") for i in range(2)]
        rows_T, t5_mm, xT_mm, mod_mm, unit_used = (
            sem(n) for n in ("rows_T", "t5_mm", "xT_mm", "mod_mm", "unit_used"))
        cum_mm, cumT_mm, s_mm, t_mm, o_mm = (
            sem(n) for n in ("cum_mm", "cumT_mm", "s_mm", "t_mm", "o_mm"))
        hidT_mm, kvcmp_mm, y_mm = (sem(n) for n in ("hidT_mm", "kvcmp_mm", "y_mm"))
        act_seq, hi_done, xT_act, first_act, val_act, tile_act = (
            sem(n) for n in ("act_seq", "hi_done", "xT_act", "first_act", "val_act", "tile_act"))
        c_exp, x_sq, x_std, gate_exp, f_exp, f_ln, z_exp, hid_exp = (
            sem(n) for n in ("c_exp", "x_sq", "x_std", "gate_exp", "f_exp", "f_ln", "z_exp", "hid_exp"))
        p_exp, pc_exp, pT_act, d_act, yh_hi, y_act, y_sq, y_std, kc_act = (
            sem(n) for n in ("p_exp", "pc_exp", "pT_act", "d_act", "yh_hi", "y_act", "y_sq", "y_std",
                             "kc_act"))
        dve_seq, lo_done, ada_used, acc_done, xn_done, first_dve, val_dve, tile_dve = (
            sem(n) for n in ("dve_seq", "lo_done", "ada_used", "acc_done", "xn_done",
                             "first_dve", "val_dve", "tile_dve"))
        cols_done, vec_done, mod_read, h_ready, stat_v, f_abs, logf_done, cum_done, cumT_done = (
            sem(n) for n in ("cols_done", "vec_done", "mod_read", "h_ready", "stat_v",
                             "f_abs", "logf_done", "cum_done", "cumT_done"))
        nmx_done, sc_sub, p_done, pc_done, pT_dve, pcT_dve, o_done = (
            sem(n) for n in ("nmx_done", "sc_sub", "p_done", "pc_done", "pT_dve", "pcT_dve", "o_done"))
        hid_done, hidT_done, kvcmp_done, y_ready, y_dve, y_tot, fin_done = (
            sem(n) for n in ("hid_done", "hidT_done", "kvcmp_done", "y_ready", "y_dve", "y_tot",
                             "fin_done"))
        early_act, early_dve, rstd_done, xn_act, y_sq_a = (sem(n) for n in ("early_act", "early_dve", "rstd_done", "xn_act", "y_sq_a"))
        g_in, g_done = sem("g_in"), sem("g_done")
        cum_out, cum_in = sem("cum_out"), sem("cum_in")
        row_out = [sem(f"row_out{i}") for i in range(2)]
        mod_done, h_full, h_rounded, yh_sq = (sem(n) for n in ("mod_done", "h_full", "h_rounded", "yh_sq"))
        first_lo, yg_done = sem("first_lo"), sem("yg_done")
        pool_seq, blk_done, d_done, bias_c_done = (
            sem(n) for n in ("pool_seq", "blk_done", "d_done", "bias_c_done"))

        block = ctx.enter_context(nc.Block())

        def on_act(t):
            return TILES[t][0] in ("qn", "qf", "kf", "u") and t >= EARLY

        taken, n_act, n_dve = [], 0, 0
        for t in range(NT):
            if on_act(t):
                n_act += 1
                taken.append((tile_act, n_act))
            else:
                n_dve += 1
                taken.append((tile_dve, n_dve))
        index = {name: t for t, name in enumerate(TILES)}
        z_order = [t for t, (kind, _) in enumerate(TILES) if kind in ("zn", "zf", "za")]

        def y_of(kind, i):
            return {"za": i, "zf": CT + i, "zn": CT + HF + i}[kind]

        def partial(t):
            kind, i = TILES[t]
            return {"kw": kw[:, i % KVG, :], "u": u_sb[:, :], "gc": conv_y[:, CW - 1:]}[kind]

        def late_from(chunk):
            if chunk < D // 512:
                return FIRST_AT[2 * chunk + 1] + 1
            return FIRST_AT[2 * chunk + 1]

        def lo_of(u):
            return (first_lo, u + 1) if u < N_FIRST else (lo_done, u + 1 - N_FIRST)

        def split(u):
            n = UNITS[u][2]
            if u >= FIRST_LATE:
                return late_hi[:, u - FIRST_LATE, :], late_lo[:, u - FIRST_LATE, :]
            return w_hi[:, u % NSPLIT, 0:n], w_lo[:, u % NSPLIT, 0:n]

        @block.sync
        def _(sp):
            sp.dma_start(x_sb[:, 0, :], x[0, 0:P, :]).then_inc(x_in[0], 16)
            sp.dma_start(rows_a[R_C:R_C + KT, :], c.rearrange("o (k p) -> (o k) p", p=P)).then_inc(rows_in, 16)
            sp.dma_start(rows_a[R_PRE:R_PRE + KT, :], pre_norm.rearrange("o (k p) -> (o k) p", p=P)).then_inc(rows_in, 16)
            sp.dma_start(rows_a[R_ADA:R_ADA + 3 * KT, :], b_ada.rearrange("o (k p) -> (o k) p", p=P)).then_inc(rows_in, 16)
            sp.dma_start(rows_a[R_CONV:R_CONV + CW * CT, :], conv_w.rearrange("o j (k p) -> (o j k) p", p=P)).then_inc(rows_in, 16)
            sp.dma_start(rows_b[0:CMP_LEN, :], pe_k[0]).then_inc(rows_in, 16)
            sp.dma_start(rows_b[CMP_LEN:2 * CMP_LEN, :], pe_v[0]).then_inc(rows_in, 16)
            sp.dma_start(cst[:, :], consts).then_inc(const_in, 16)
            for s in range(1, ST):
                sp.dma_start(x_sb[:, s, :], x[0, s * P:(s + 1) * P, :]).then_inc(x_in[s], 16)

            def ada_unit(n):
                chunk, q = n // 4, n % 4
                if n >= NADA:
                    sp.wait_ge(ada_used, n - NADA + 1)
                rows = w_ada[0, q * S:(q + 1) * S, :].rearrange("(k p) n -> p k n", p=P)
                if chunk < D // 256:
                    for half in range(2):
                        sp.dma_start(ada[:, n % NADA, :, half * 256:(half + 1) * 256],
                                     rows[:, :, half * D + chunk * 256:half * D + (chunk + 1) * 256]
                                     ).then_inc(ada_in[n % NADA], 16)
                else:
                    c0 = 2 * D + (chunk - D // 256) * S
                    sp.dma_start(ada[:, n % NADA, :, :], rows[:, :, c0:c0 + S]).then_inc(ada_in[n % NADA], 32)

            def weight_unit(u):
                kind, where, n = UNITS[u]
                if u >= NRAW:
                    sp.wait_ge(*lo_of(u - NRAW))
                dst = w_raw[:, u % NRAW, 0:n]
                if kind == "first":
                    src = w_in[0, where[0] * P:(where[0] + 1) * P, KC:KC + 3 * KV]
                elif kind == "panel":
                    b, k, step = where
                    c0, w, _ = PANEL[b]
                    dst = dst.rearrange("p (k n) -> p k n", k=step)
                    src = w_in[0, k * P:(k + step) * P, c0:c0 + w].rearrange("(k p) n -> p k n", p=P)
                elif kind == "tile":
                    (name, i), k0, n_k = TILES[where[0]], where[1], where[2]
                    c0 = COL0[name] + i * P
                    dst = dst.rearrange("p (k n) -> p k n", k=n_k)
                    src = w_in[0, k0 * P:(k0 + n_k) * P, c0:c0 + P].rearrange("(k p) n -> p k n", p=P)
                elif kind == "cmp":
                    w1, q = (w1_k, w1_v)[where[0] // 8], where[0] % 8
                    dst = dst.rearrange("p (k n) -> p k n", k=4)
                    src = w1[0, q * S:(q + 1) * S, :].rearrange("(k p) n -> p k n", p=P)
                else:
                    half, k = where
                    src = w_out[0, k * P:(k + 1) * P, half * D // 2:(half + 1) * D // 2]
                sp.dma_start(dst, src).then_inc(raw_in[u % NRAW], 16)

            for chunk in range(D // 256):
                for q in range(4):
                    ada_unit(4 * chunk + q)
                if chunk == 0:
                    sp.dma_start(oneh[:, :], onehot).then_inc(misc_in, 16)
                    sp.dma_start(rel[:, :], rel_bias).then_inc(misc_in, 16)
                    sp.dma_start(bf[:, :], b_forget.broadcast_to([P, HF])).then_inc(misc_in, 16)
                    sp.dma_start(w2[:, 0, :, :], w2_k[0].rearrange("(k p) n -> p k n", p=P)).then_inc(misc_in, 16)
                    sp.dma_start(w2[:, 1, :, :], w2_v[0].rearrange("(k p) n -> p k n", p=P)).then_inc(misc_in, 16)
                for u in range(FIRST_AT[2 * chunk], (FIRST_AT + [N_FIRST] * 2)[2 * chunk + 2]):
                    weight_unit(u)
            sp.wait_ge(vec_done, 1)
            sp.dma_start(t5_dram, vec[:, :]).then_inc(t5_out, 16)
            for i in range(N_PANEL):
                weight_unit(N_FIRST + i)
                if i < 16:
                    ada_unit(4 * (D // 256) + i)
                if i == 2:
                    sp.wait_ge(t5_out, 16)
                    sp.dma_start(t5_wide, bass.AP(tensor=t5_dram.tensor, offset=0,
                                                  ap=[[VEC, HN], [0, P], [1, VEC]])).then_inc(t5_out, 16)
            sp.wait_ge(t5_out, 32)

            def bias_load(h):
                if h >= 2:
                    sp.wait_ge(nmx_done, 3 * (h - 2) + 2)
                    sp.wait_ge(bias_c_done, h - 1)
                src = bass.AP(tensor=t5_wide.tensor, offset=h * P * VEC + P - 1, ap=[[VEC - 1, P], [1, S]])
                sp.dma_start(bias_t[:, h % 2, :], src).then_inc(bias_in[h % 2], 16)

            def cum_load(g):
                if g == 0:
                    sp.wait_ge(cum_out, 16)
                    sp.wait_ge(hidT_mm, 1)
                else:
                    sp.wait_ge(d_act, g)
                src = bass.AP(tensor=cum_dram.tensor, offset=g * P, ap=[[0, P], [HF * P, ST], [1, P]])
                sp.dma_start(sq_out[:, :].rearrange("p (s k) -> p s k", s=ST), src).then_inc(cum_in, 16)

            bias_load(0)
            for t in range(NT):
                if t == CMP_TILES + 1:
                    sp.wait_ge(cumT_done, 1)
                    sp.dma_start(cum_dram, cum_T[:, :]).then_inc(cum_out, 16)
                if t == HEAD_TILES:
                    cum_load(0)
                if t % HEAD_TILES == HEAD_TILES - 1 and HEAD_TILES < t < HEAD_TILES * HF:
                    cum_load(t // HEAD_TILES)
                if (t + 2) % HEAD_TILES == 0 and (t + 2) // HEAD_TILES < HN:
                    bias_load((t + 2) // HEAD_TILES)
                for u in range(AT[t], AT[t + 1]):
                    weight_unit(u)
            for u in range(AT[NT], NU):
                weight_unit(u)
            sp.wait_ge(*lo_of(NU - 1))
            for s in range(2):
                sp.dma_start(x_again[:, s, :], x[0, s * P:(s + 1) * P, :]).then_inc(xa_in[s], 16)
            for s in range(ST):
                for i in range(STORES[s]):
                    cs = slice(i * D // STORES[s], (i + 1) * D // STORES[s])
                    sp.wait_ge(fin_done, sum(STORES[:s]) + i + 1)
                    sp.dma_start(out[0, s * P:(s + 1) * P, cs], fin[:, s % 2, cs]).then_inc(stored[s % 2], 16)
                if s + 2 < ST:
                    sp.dma_start(x_again[:, s % 2, :], x[0, (s + 2) * P:(s + 3) * P, :]).then_inc(xa_in[s % 2], 16)
            for i in range(2):
                sp.wait_ge(stored[i], 16 * sum(STORES[i::2]))

        @block.tensor
        def _(pe):
            def exact(dst, a_hi, a_lo, b_hi, b_lo, first, last):
                pe.matmul(dst, a_hi, b_hi, start=first, stop=False)
                pe.matmul(dst, a_hi, b_lo, start=False, stop=False)
                return pe.matmul(dst, a_lo, b_hi, start=False, stop=last)

            pe.wait_ge(const_in, 16)
            pe.wait_ge(rows_in, 96)
            pe.transpose(bank[7][:, 0:R_ALL], rows_a[:, :], ident[0:R_ALL, 0:R_ALL])
            pe.transpose(bank[7][:, P:P + 2 * CMP_LEN], rows_b[:, :],
                         ident[0:2 * CMP_LEN, 0:2 * CMP_LEN]).then_inc(rows_T, 1)
            def modulation(chunk):
                pe.wait_ge(acc_done, chunk + 1)
                pe.wait_ge(cols_done, 1)
                if chunk >= 1:
                    pe.wait_ge(mod_read, chunk)
                for j in range(4):
                    mm = pe.matmul(bank[7][:, 4 * chunk + j:4 * chunk + j + 1],
                                   acc[:, chunk % 2, j * P:(j + 1) * P], ones[:, 0:1], start=True, stop=True)
                mm.then_inc(mod_mm, 1)

            def gate_row(chunk):
                pe.wait_ge(acc_done, chunk + 1)
                pe.wait_ge(mod_read, chunk)
                pe.matmul(bank[7][0:1, :], ones[:, 0:1], acc[:, chunk % 2, :], start=True, stop=True).then_inc(mod_mm, 1)

            pe.wait_ge(xn_done, ST // 2)
            pe.wait_ge(xn_act, ST // 2)
            for k in range(KT):
                if k >= 6:
                    pe.wait_ge(xT_act, k - 5)
                for s in range(ST):
                    mm = pe.transpose(bank[k % 6][:, s * P:(s + 1) * P], x_sb[:, s, k * P:(k + 1) * P], ident)
                mm.then_inc(xT_mm, 1)
            pe.wait_ge(misc_in, 80)
            pe.matmul(bank[6][0:HN, 0:S], rel[:, :], oneh[:, :], start=True, stop=True).then_inc(t5_mm, 1)

            def early_parts(chunk):
                if chunk == 1:
                    pe.wait_ge(vec_done, 1)
                elif chunk <= ROUND_TWO:
                    pe.wait_ge(early_act, chunk - 1)
                else:
                    pe.wait_ge(early_dve, chunk - ROUND_TWO)
                parts = EARLY_PARTS[chunk]
                for part in parts:
                    t, k0, n_k = part
                    pe.wait_ge(*lo_of(EARLY_AT[part]))
                    hi, lo = split(EARLY_AT[part])
                    for i in range(n_k):
                        cs = slice(i * P, (i + 1) * P)
                        mm = exact(bank[6][:, :], hi[:, cs], lo[:, cs], h_hi[:, k0 + i, :], h_lo[:, k0 + i, :],
                                   part is parts[0] and i == 0, part is parts[-1] and i == n_k - 1)
                    mm.then_inc(unit_used, 1)

            modulation(0)
            for k in range(KT):
                pe.wait_ge(h_ready, k + 1)
                u = FIRST_AT[k]
                pe.wait_ge(*lo_of(u))
                if k == 0:
                    pe.wait_ge(xT_act, KT)
                hi, lo = split(u)
                for m in range(6):
                    cs = slice(m * P, (m + 1) * P)
                    mm = exact(bank[m][:, :], hi[:, cs], lo[:, cs], h_hi[:, k, :], h_lo[:, k, :],
                               k == 0, k == KT - 1)
                mm.then_inc(unit_used, 1)
                if k % 2 == 0:
                    if k // 2 in EARLY_PARTS:
                        early_parts(k // 2)
                    if k // 2 + 1 < D // 256:
                        modulation(k // 2 + 1)
            u = N_FIRST
            gate_chunk = D // 256
            for b, (_, n, _) in enumerate(PANEL):
                step = 2 if n > 280 else 4
                for k0 in range(0, KT, step):
                    pe.wait_ge(*lo_of(u))
                    hi, lo = split(u)
                    for k in range(k0, k0 + step):
                        ws = slice((k - k0) * n, (k - k0 + 1) * n)
                        for s in range(ST):
                            a = ST * b + s
                            if k == 0:
                                if a < 6:
                                    if a % 2 == 0:
                                        pe.wait_ge(first_act, a // 2 + 1)
                                    else:
                                        pe.wait_ge(first_dve, a // 2 + 1)
                                elif a == 6:
                                    pe.wait_ge(early_dve, len(EARLY_PARTS) - EARLY)
                                elif (a - 7) % 2 == 0:
                                    pe.wait_ge(val_act, (a - 7) // 2 + 1)
                                else:
                                    pe.wait_ge(val_dve, (a - 7) // 2 + 1)
                            ps = slice(s * P, (s + 1) * P)
                            mm = exact(bank[a % 7][:, 0:n], h_hi[:, k, ps], h_lo[:, k, ps], hi[:, ws], lo[:, ws],
                                       k == 0, k == KT - 1)
                    mm.then_inc(unit_used, 1)
                    u += 1
                    if (u - N_FIRST) % 4 == 1 and u - N_FIRST > 4 and gate_chunk < D // 256 + 4:
                        gate_row(gate_chunk)
                        gate_chunk += 1

            def compress(q):
                u = CMP_AT[q]
                pe.wait_ge(*lo_of(u))
                pe.wait_ge(blk_done, q + 1)
                hi, lo = split(u)
                for i in range(4):
                    cs = slice(i * CMP_HID, (i + 1) * CMP_HID)
                    mm = exact(bank[4 + q // 8][0:66, 0:CMP_HID], blk_hi[:, q % 2, i, :], blk_lo[:, q % 2, i, :],
                               hi[:, cs], lo[:, cs], q % 8 == 0 and i == 0, q % 8 == 7 and i == 3)
                mm.then_inc(unit_used, 1)

            def hidden_T():
                pe.wait_ge(hid_done, 1)
                for w in range(2):
                    for j in range(2):
                        mm = pe.transpose((T0, T1)[w][:, j * P:j * P + 2 * NC], hid[:, w, j * P:(j + 1) * P],
                                          ident[0:2 * NC, 0:2 * NC])
                mm.then_inc(hidT_mm, 1)

            def compressed_kv():
                pe.wait_ge(hidT_done, 1)
                for j in range(2):
                    pe.matmul(bank[4][:, 0:2 * NC], w2[:, 0, j, :], hidT[:, 0, j, :], start=(j == 0), stop=(j == 1))
                for g in range(KVG):
                    for j in range(2):
                        mm = pe.matmul(bank[4][0:NC, P + g * HD:P + (g + 1) * HD],
                                       hidT[:, 1, j, g * NC:(g + 1) * NC], w2[:, 1, j, :],
                                       start=(j == 0), stop=(j == 1))
                mm.then_inc(kvcmp_mm, 1)

            def scores(j):
                kind, h, _ = JOBS[j]
                if j >= 1:
                    pe.wait_ge(nmx_done, j)
                if kind == "sel":
                    pe.wait_ge(*taken[index["qn", h]])
                    q, key = qn, ks[:, h // 3, CPAD:]
                    pe.wait_ge(kvcmp_done, 1)
                    pe.wait_ge(kc_act, 1)
                elif kind == "win":
                    q, key = qn, kw[:, h // 3, :]
                else:
                    pe.wait_ge(*taken[index["kf", h]])
                    q, key = qf, kf[:, :]
                if kind == "sel":
                    both = ks[:, h // 3, :]
                    for b in range(ST - 1):
                        pe.matmul(SB[b][:, SBO[b] - CPAD:SBO[b] + SW[b]], q[:, b * P:(b + 1) * P],
                                  both[:, 0:CPAD + SW[b]], start=True, stop=True)
                    pe.matmul(SC[3], q[:, 3 * P:], both[:, 0:NC], start=True, stop=True)
                for b in range(ST - 1 if kind == "sel" else 0, ST):
                    mm = pe.matmul(SB[b][:, SBO[b]:SBO[b] + SW[b]], q[:, b * P:(b + 1) * P], key[:, 0:SW[b]],
                                   start=True, stop=True)
                mm.then_inc(s_mm, 1)

            def transposes(j, part):
                kind = JOBS[j][0]
                if part == 0:
                    pe.wait_ge(p_done, j + 1)
                    pe.wait_ge(hidT_done, 1)
                    if j >= 1:
                        pe.wait_ge(pT_act, 2 * j)
                        pe.wait_ge(pT_dve, j)
                        pe.wait_ge(pcT_dve, (j + 2) // 3)
                    for k in range(2):
                        for b in range(k, ST):
                            mm = pe.transpose((T0, T1)[k][:, (b - k) * P:(b - k + 1) * P],
                                              prob[:, SO[b] + k * P:SO[b] + (k + 1) * P], ident)
                else:
                    pe.wait_ge(pT_act, 2 * j + 1)
                    for k in range(2, ST):
                        for b in range(k, ST):
                            o = TO[k] - TO[2] + (b - k) * P
                            mm = pe.transpose(T0[:, o:o + P], prob[:, SO[b] + k * P:SO[b] + (k + 1) * P], ident)
                    if kind == "sel":
                        pe.wait_ge(pT_dve, j + 1)
                        pe.wait_ge(pc_done, j // 3 + 1)
                        for b in range(ST):
                            mm = pe.transpose(T1[0:NC, b * P:(b + 1) * P], pc[:, b, :], ident)
                mm.then_inc(t_mm, 1)

            def weighted_values(j):
                kind, h, _ = JOBS[j]
                if kind != "win" and (j // 3) * 2 + (kind == "fox") >= 1:
                    pe.wait_ge(o_done, (j // 3) * 2 + (kind == "fox"))
                pe.wait_ge(pT_act, 2 * j + 2)
                pe.wait_ge(pT_dve, j + 1)
                v0 = {"sel": PVS + (h // 3) * HD, "win": PVW + (h // 3) * HD, "fox": h * HD}[kind]
                for k in range(ST):
                    mm = pe.matmul(OB[:, k * P:], vals[:, k, v0:v0 + HD], probT[:, TO[k]:TO[k] + TW[k]],
                                   start=(k == 0 and kind != "win"), stop=(k == ST - 1 and kind != "sel"))
                if kind == "sel":
                    pe.wait_ge(pcT_dve, j // 3 + 1)
                    pe.matmul(OB[:, :], vcmp[:, h // 3, :], pcT[:, :], start=False, stop=False)
                else:
                    mm.then_inc(o_mm, 1)

            def cumulative():
                pe.wait_ge(logf_done, 1)
                flat = fl[:, :, :].rearrange("p s h -> p (s h)")
                pe.matmul(bank[7][:, 64:64 + ST * HF], tri, flat, start=True, stop=True)
                mm = pe.matmul(bank[7][:, 96:96 + ST * HF], ones, flat, start=True, stop=True)
                mm.then_inc(cum_mm, 1)

            def cumulative_T():
                pe.wait_ge(cum_done, 1)
                pe.transpose(bank[7][0:HF * ST, P:2 * P], cum[:, :, :].rearrange("p s h -> p (s h)"),
                             ident).then_inc(cumT_mm, 1)

            for t in range(NT):
                if t == 0:
                    pe.wait_ge(val_dve, 5)
                    pe.wait_ge(val_act, 6)
                elif t >= 2:
                    pe.wait_ge(*taken[t - 2])
                for half in range(2):
                    if t < CMP_TILES:
                        if t == 0 and half == 0:
                            pe.wait_ge(val_dve, 6)
                        if t == CMP_TILES // 2 and half == 0:
                            pe.wait_ge(val_act, 7)
                        for i in range(CMP_PER // 2):
                            compress(CMP_PER * t + CMP_PER // 2 * half + i)
                    k0, n_k, u = PARTS[t][half]
                    pe.wait_ge(*lo_of(u))
                    hi, lo = split(u)
                    for i in range(n_k):
                        k, cs = k0 + i, slice(i * P, (i + 1) * P)
                        mm = exact(ACC[t % 2][:, :], hi[:, cs], lo[:, cs], h_hi[:, k, :], h_lo[:, k, :],
                                   half == 0 and i == 0, k == KT - 1)
                    mm.then_inc(unit_used, 1)
                    if half == 0:
                        if t == CMP_TILES + 1:
                            compressed_kv()
                        for j, (_, _, at_t) in enumerate(JOBS):
                            if t == at_t + 2:
                                transposes(j, 1)
                if t == 1:
                    cumulative()
                if t == 2:
                    cumulative_T()
                if t == CMP_TILES:
                    hidden_T()
                for j, (_, g, at_t) in enumerate(JOBS):
                    if t == at_t + 2:
                        weighted_values(j)
                for j, (kind, g, at_t) in enumerate(JOBS):
                    if t == at_t + 1:
                        transposes(j, 0)
                for j, (_, g, at_t) in enumerate(JOBS):
                    if t == at_t:
                        scores(j)

            pe.wait_ge(pT_dve, len(JOBS))
            pe.wait_ge(pT_act, 2 * len(JOBS))
            pe.wait_ge(nmx_done, len(JOBS))
            pe.wait_ge(*taken[NT - 2])
            pe.wait_ge(o_done, 2 * HN)

            def out_step(half, i, s, u, cols=range(2)):
                hi, lo = split(u)
                k = OUT_ORDER[i]
                ps = slice(s * P, (s + 1) * P)
                for n in cols:
                    ws = slice(n * S, (n + 1) * S)
                    if half == 0 and i == 0 and YB[2 * s + n] is ACC[(NT - 1) % 2]:
                        pe.wait_ge(*taken[NT - 1])
                    if half == 1 and i == 0:
                        pe.wait_ge((y_act, y_dve)[n], s + 1)
                    mm = exact(YB[2 * s + n][:, :], h_hi[:, k, ps], h_lo[:, k, ps], hi[:, ws], lo[:, ws],
                               i == 0, i == KT - 1)
                    if half == 0 and i == KT - 1 and (s, n) != (ST - 1, 1):
                        mm.then_inc(y_mm, 1)
                return mm

            for half in range(2):
                for i in range(KT if half == 0 else KT - LATE):
                    u = AT[NT] + half * KT + i
                    pe.wait_ge(*lo_of(u))
                    pe.wait_ge(y_ready, i + 1)
                    for s in range(ST):
                        mm = out_step(half, i, s, u)
                    mm.then_inc(unit_used, 1)
            for s in range(ST):
                for cols in ([0, 1],) if s < ST - 1 else ([0], [1]):
                    for i in range(KT - LATE, KT):
                        pe.wait_ge(*lo_of(AT[NT] + KT + i))
                        mm = out_step(1, i, s, AT[NT] + KT + i, cols)
                    mm.then_inc(y_mm, 1)

        @block.scalar
        def _(act):
            seq = [0]

            def fence(ins):
                seq[0] += 1
                ins.then_inc(act_seq, 1)
                act.wait_ge(act_seq, seq[0])

            def hi_half(u):
                act.wait_ge(raw_in[u % NRAW], 16 * (u // NRAW + 1))
                if NSPLIT <= u < FIRST_LATE:
                    act.wait_ge(unit_used, u - NSPLIT + 1)
                act.activation(split(u)[0], w_raw[:, u % NRAW, 0:UNITS[u][2]], ACT.Copy).then_inc(hi_done, 1)

            act.wait_ge(cols_done, 1)
            act.activation(c_tmp[:, :], cols_a[:, R_C:R_C + KT], ACT.Exp, scale=-1.0).then_inc(c_exp, 1)
            act.wait_ge(c_exp, 1)
            act.preload_act_table(ACT.Sqrt)
            act.wait_ge(stat_v, 1)
            for s in range(ST):
                act.wait_ge(x_in[s], 16)
                act.activation(xT[:, 4 * s:4 * s + 4, :].rearrange("p k n -> p (k n)"), x_sb[:, s, :], ACT.Square,
                               accum_out=stat[:, s:s + 1]).then_inc(x_sq, 1)
            act.wait_ge(x_sq, ST)
            act.activation(rstd[:, :], stat[:, :], ACT.Sqrt, scale=1.0 / D, bias=eps_c[:, :]).then_inc(x_std, 1)
            act.wait_ge(rstd_done, 1)
            for s in range(ST // 2, ST):
                act.activation(x_sb[:, s, :], x_sb[:, s, :], ACT.Copy, scale=rstd[:, s:s + 1]).then_inc(xn_act, 1)
            for k in range(KT):
                act.wait_ge(xT_mm, k + 1)
                act.activation(xT[:, k, :], bank[k % 6][:, :], ACT.Copy).then_inc(xT_act, 1)

            act.wait_ge(xT_act, KT)
            for chunk in range(D // 256):
                lead = late_from(chunk)
                for u in range(FIRST_AT[2 * chunk], lead):
                    hi_half(u)
                act.wait_ge(mod_done, chunk + 1)
                for k in (2 * chunk, 2 * chunk + 1):
                    if k >= 2:
                        act.wait_ge(h_ready, k - 1)
                    act.activation(xmix[:, k % 2, :], xT[:, k, :], ACT.Identity, scale=mod_sc[:, k:k + 1],
                                   bias=mod_sh[:, k:k + 1]).then_inc(h_full, 1)
                    act.wait_ge(h_full, k + 1)
                    act.activation(h_hi[:, k, :], xmix[:, k % 2, :], ACT.Copy).then_inc(h_rounded, 1)
                if 2 <= chunk <= ROUND_TWO:
                    act.wait_ge(unit_used, EARLY_END[chunk - 1])
                    act.activation(partial(EARLY_PARTS[chunk - 1][0][0]), bank[6][:, :], ACT.Copy) \
                       .then_inc(early_act, 1)
                for u in range(lead, FIRST_AT[2 * chunk + 1] + 1):
                    hi_half(u)
            hi_half(N_FIRST)
            act.wait_ge(unit_used, N_FIRST)
            for m in range(0, 6, 2):
                dst = kvc[:, m, :] if m < 4 else ks[:, m - 4, CPAD:]
                act.activation(dst, bank[m][:, :], ACT.Copy).then_inc(first_act, 1)

            def panel_out(a):
                b, s = a // ST, a % ST
                act.activation(vals[:, s, PANEL[b][2]:PANEL[b][2] + PANEL[b][1]], bank[a % 7][:, 0:PANEL[b][1]],
                               ACT.Copy).then_inc(val_act, 1)

            u, done = N_FIRST + 1, N_FIRST
            for b, (_, n, _) in enumerate(PANEL):
                done += 8 if n > 280 else 4
                while u < done + (AHEAD if b == len(PANEL) - 1 else 2):
                    hi_half(u)
                    u += 1
                act.wait_ge(unit_used, done)
                for s in range(0, ST, 2):
                    panel_out(ST * b + s)
            hi_half(u)
            act.wait_ge(val_act, 2 * len(PANEL))
            act.wait_ge(val_dve, 2 * len(PANEL))
            act.activation(gate[:, :, :], vals[:, :, PG:PG + 3 * HN], ACT.Exp, scale=-1.0).then_inc(gate_exp, 1)
            act.wait_ge(f_abs, 1)
            act.activation(fe[:, :, :], fe[:, :, :], ACT.Exp, scale=-1.0).then_inc(f_exp, 1)
            act.wait_ge(f_exp, 1)
            act.activation(fe[:, :, :], fe[:, :, :], ACT.Ln, bias=one_c[:, :]).then_inc(f_ln, 1)

            def tile_out(t):
                kind, i = TILES[t]
                if not on_act(t) and kind not in ("zn", "zf", "za"):
                    return
                act.wait_ge(unit_used, PARTS[t][1][2] + 1)
                src = ACC[t % 2][:, :]
                if kind == "qn":
                    if i >= 1:
                        act.wait_ge(s_mm, 3 * (i - 1) + 2)
                    ins = act.activation(qn[:, :], src, ACT.Copy, scale=SCALE)
                elif kind == "qf":
                    if i >= 1:
                        act.wait_ge(s_mm, 3 * i)
                    ins = act.activation(qf[:, :], src, ACT.Copy, scale=SCALE)
                elif kind == "kf":
                    if i >= 1:
                        act.wait_ge(s_mm, 3 * i)
                    else:
                        act.wait_ge(cum_out, 16)
                    ins = act.activation(kf[:, :], src, ACT.Copy)
                elif kind == "u":
                    act.wait_ge(*taken[index["gc", i - 1]])
                    ins = act.activation(u_sb[:, :], src, ACT.Copy)
                else:
                    z = z_order.index(t)
                    if z >= 1:
                        act.wait_ge(*taken[z_order[z - 1]])
                    act.activation(e_sb[:, :], src, ACT.Exp, scale=-1.0).then_inc(z_exp, 1)
                    return
                ins.then_inc(tile_act, 1)

            def y_hi(i):
                act.activation(h_hi[:, OUT_ORDER[i], :], yT[:, OUT_ORDER[i], :], ACT.Copy).then_inc(yh_hi, 1)

            for t in range(NT + 1):
                if t < NT:
                    lead = list(range(AT[t] + AHEAD + (t == 0), min(AT[t + 1] + AHEAD, NU)))
                    for u in lead[:len(lead) // 2]:
                        hi_half(u)
                if t >= 1:
                    tile_out(t - 1)
                if t == CMP_TILES:
                    act.wait_ge(unit_used, AT[CMP_TILES])
                    for w in range(2):
                        ins = act.activation(hid[:, w, :], bank[4 + w][0:2 * NC, 0:CMP_HID], ACT.Exp, scale=-1.0)
                    ins.then_inc(hid_exp, 1)
                if t == CMP_TILES + 1:
                    act.wait_ge(kvcmp_mm, 1)
                    act.activation(ks[:, :, 0:NC], bank[4][:, 0:2 * NC].rearrange("p (g n) -> p g n", g=KVG),
                                   ACT.Copy).then_inc(kc_act, 1)
                for j, (kind, g, at_t) in enumerate(JOBS):
                    if t == at_t + 2:
                        act.wait_ge(t_mm, 2 * j + 1)
                        if j >= 1:
                            act.wait_ge(o_mm, (j // 3) * 2 + (kind == "fox")) if kind != "win" else act.wait_ge(
                                t_mm, 2 * j + 1)
                        act.activation(probT[:, TO[0]:TO[1]], T0[:, :], ACT.Copy).then_inc(pT_act, 1)
                        if kind == "sel":
                            act.wait_ge(cum_in, 16 * (g + 1))
                            if g >= 1:
                                act.wait_ge(nmx_done, 3 * g)
                            for b in range(ST):
                                ins = act.activation(dbias[:, SO[b]:SO[b] + SW[b]], sq_out[:, 0:SW[b]], ACT.Identity,
                                                     scale=-1.0, bias=cum[:, b, g:g + 1])
                            ins.then_inc(d_act, 1)
                    if t == at_t + 1:
                        act.wait_ge(nmx_done, j + 1)
                        for b in range(ST):
                            cs = slice(SO[b], SO[b] + SW[b])
                            ins = act.activation(prob[:, cs], prob[:, cs], ACT.Exp, bias=nmx[:, b:b + 1],
                                                 accum_out=ssum[:, b:b + 1])
                        ins.then_inc(p_exp, 1)
                        if kind == "sel":
                            act.wait_ge(sc_sub, g + 1)
                            act.activation(pc[:, :, :], pc[:, :, :], ACT.Exp).then_inc(pc_exp, 1)
                if t < NT:
                    for u in lead[len(lead) // 2:]:
                        hi_half(u)
                for j, (_, g, at_t) in enumerate(JOBS):
                    if t == at_t + 2:
                        act.wait_ge(t_mm, 2 * j + 2)
                        act.activation(probT[:, TO[2]:SALL], T0[:, 0:SALL - TO[2]], ACT.Copy).then_inc(pT_act, 1)
                if t == NT - 1:
                    act.wait_ge(unit_used, PARTS[t][0][2] + 1)
                    act.wait_ge(o_done, 2 * HN)
                    for i in range(Y_FIRST):
                        y_hi(i)
            u = AT[NT] + AHEAD
            act.wait_ge(unit_used, AT[NT])
            for i in range(Y_FIRST, KT):
                if OUT_ORDER[i] == CT - 1:
                    act.wait_ge(*taken[index["za", CT - 1]])
                y_hi(i)
                if i == Y_FIRST + 1:
                    for slot in range(2):
                        act.wait_ge(row_out[slot], 32)
                    act.dma_start(g_bc[:, :], gate_dram.broadcast_to([P, D])).then_inc(g_in, 16)
                if i % 3 == 2 and u < AT[NT] + NSPLIT:
                    hi_half(u)
                    u += 1
            act.dma_start(y_half[:, 0:2, :].rearrange("p s n -> p (s n)"),
                          b_ada[:, 2 * D:3 * D].broadcast_to([P, D])).then_inc(g_in, 16)
            act.dma_start(y_half[:, 2:4, :].rearrange("p s n -> p (s n)"),
                          post_norm.broadcast_to([P, D])).then_inc(g_in, 16)
            while u < AT[NT] + KT + 2:
                hi_half(u)
                u += 1
            act.wait_ge(g_done, 1)
            for s in range(ST):
                act.wait_ge(y_mm, 2 * s + 1)
                act.activation(y_half[:, s, 0:S], YB[2 * s][:, :], ACT.Copy).then_inc(y_act, 1)
            while u < FIRST_LATE:
                hi_half(u)
                u += 1
            act.wait_ge(y_ready, KT)
            while u < NU:
                hi_half(u)
                u += 1
            act.wait_ge(unit_used, FIRST_LATE)
            act.wait_ge(*lo_of(NU - 1))
            for s in range(ST):
                act.wait_ge(y_dve, s + 1)
                act.wait_ge(y_act, s + 1)
                act.activation(fin[:, 1, 0:D // 2], y_half[:, s, :], ACT.Square,
                               accum_out=sq[:, s, 0:1]).then_inc(yh_sq, 1)
                act.wait_ge(yh_sq, s + 1)
            act.preload_act_table(ACT.Sqrt)
            for s in range(ST):
                act.wait_ge(y_mm, 2 * ST - 1 + s + 1)
                act.activation(sq_out[:, :], YB[2 * s][:, :], ACT.Square, accum_out=sq[:, s, 1:2]).then_inc(y_sq_a, 1)
                act.wait_ge(y_sq_a, s + 1)
                if s == ST - 1:
                    act.wait_ge(y_mm, 2 * ST - 1 + s + 2)
                act.activation(sq_out[:, :], YB[2 * s + 1][:, :], ACT.Square, accum_out=sq[:, s, 2:3]).then_inc(y_sq, 1)
                act.wait_ge(y_tot, s + 1)
                act.activation(rs2[:, s:s + 1], tot[:, s:s + 1], ACT.Sqrt, scale=1.0 / D, bias=eps_c[:, :]).then_inc(y_std, 1)

        @block.vector
        def _(dve):
            seq = [0]

            def fence(ins):
                seq[0] += 1
                ins.then_inc(dve_seq, 1)
                dve.wait_ge(dve_seq, seq[0])

            def lo_half(u):
                n = UNITS[u][2]
                hi, lo = split(u)
                dve.wait_ge(hi_done, u + 1)
                dve.tensor_tensor(lo, w_raw[:, u % NRAW, 0:n], hi.bitcast(F32), ALU.subtract).then_inc(lo_done, 1)

            def reciprocal_of_one_plus(dst, src):
                fence(dve.tensor_scalar(dst, src, 1.0, None, ALU.add))
                fence(dve.reciprocal(dst, dst))

            dve.memset(eps_c[:, :], EPS)
            dve.memset(conv_y[:, 0:CW - 1], 0.0)
            dve.memset(ks[:, :, NC:CPAD], 0.0)
            dve.memset(one_c[:, :], 1.0).then_inc(stat_v, 1)
            dve.wait_ge(rows_T, 1)
            fence(dve.tensor_copy(cols_a[:, :], bank[7][:, 0:R_ALL]))
            dve.tensor_copy(pe_cols[:, :, :], bank[7][:, P:P + 2 * CMP_LEN].rearrange("p (w l) -> p w l", w=2)) \
               .then_inc(cols_done, 1)
            dve.wait_ge(c_exp, 1)
            reciprocal_of_one_plus(c_tmp[:, :], c_tmp[:, :])
            fence(dve.tensor_tensor(c_act[:, :], cols_a[:, R_C:R_C + KT], c_tmp[:, :], ALU.mult))
            fence(dve.tensor_scalar(b1[:, :], cols_a[:, R_ADA + KT:R_ADA + 2 * KT], 1.0, None, ALU.add))

            def modulate(chunk):
                if chunk >= 2:
                    dve.wait_ge(mod_mm, chunk - 1)
                dst = acc[:, chunk % 2, :]
                for k in range(KT):
                    n = 4 * chunk + k // 4
                    if k % 4 == 0:
                        dve.wait_ge(ada_in[n % NADA], 32 * (n // NADA + 1))
                    src = ada[:, n % NADA, k % 4, :]
                    if k == 0:
                        ins = dve.tensor_scalar(dst, src, c_act[:, 0:1], None, ALU.mult)
                    else:
                        ins = dve.scalar_tensor_tensor(out=dst, in0=src, scalar=c_act[:, k:k + 1], in1=dst,
                                                       op0=ALU.mult, op1=ALU.add)
                    if k == KT - 1:
                        ins.then_inc(acc_done, 1)
                        dve.wait_ge(acc_done, chunk + 1)
                        dve.sem_inc(ada_used, 1)
                    elif k % 4 == 3:
                        ins.then_inc(ada_used, 1)
                        dve.wait_ge(ada_used, n + 1)
                    else:
                        fence(ins)

            def make_h(chunk):
                dve.wait_ge(mod_mm, chunk + 1)
                k = slice(2 * chunk, 2 * chunk + 2)
                m0 = 4 * chunk
                dve.tensor_tensor(mod_sh[:, k], bank[7][:, m0:m0 + 2], cols_a[:, R_ADA + 2 * chunk:R_ADA + 2 * chunk + 2],
                                  ALU.add)
                dve.tensor_tensor(mod_sc[:, k], bank[7][:, m0 + 2:m0 + 4], b1[:, k], ALU.add).then_inc(mod_read, 1)
                dve.wait_ge(mod_read, chunk + 1)
                dve.tensor_tensor(mod_sc[:, k], mod_sc[:, k], cols_a[:, R_PRE + 2 * chunk:R_PRE + 2 * chunk + 2],
                                  ALU.mult).then_inc(mod_done, 1)

            dve.wait_ge(x_std, 1)
            dve.reciprocal(rstd[:, :], rstd[:, :]).then_inc(rstd_done, 1)
            dve.wait_ge(rstd_done, 1)
            for s in range(ST // 2):
                dve.tensor_scalar(x_sb[:, s, :], x_sb[:, s, :], rstd[:, s:s + 1], None, ALU.mult).then_inc(xn_done, 1)
            modulate(0)
            fence(dve.memset(vec[:, S:VEC], NEG))
            dve.wait_ge(t5_mm, 1)
            dve.tensor_copy(vec[:, 0:S], bank[6][0:HN, :]).then_inc(vec_done, 1)
            for chunk in range(D // 256):
                make_h(chunk)
                if chunk > ROUND_TWO and chunk - 1 in EARLY_PARTS:
                    part = partial(EARLY_PARTS[chunk - 1][0][0])
                    dve.wait_ge(unit_used, EARLY_END[chunk - 1])
                    dve.tensor_tensor(part, bank[6][:, :], part, ALU.add).then_inc(early_dve, 1)
                if chunk + 1 < D // 256:
                    modulate(chunk + 1)
            lo_half(N_FIRST)
            dve.wait_ge(unit_used, N_FIRST)
            for m in range(1, 6, 2):
                dst = kvc[:, m, :] if m < 4 else ks[:, m - 4, CPAD:]
                dve.tensor_copy(dst, bank[m][:, :]).then_inc(first_dve, 1)

            def gate_chunk(i):
                chunk = D // 256 + i
                dve.wait_ge(mod_mm, chunk + 1)
                if i >= 2:
                    dve.wait_ge(row_out[i % 2], 16)
                dve.tensor_copy((pcT, sq_out)[i % 2][0:1, :], bank[7][0:1, :]).then_inc(mod_read, 1)

            def panel_out(a):
                b, s = a // ST, a % ST
                dve.tensor_copy(vals[:, s, PANEL[b][2]:PANEL[b][2] + PANEL[b][1]], bank[a % 7][:, 0:PANEL[b][1]]) \
                   .then_inc(val_dve, 1)

            u, done, chunks, read = N_FIRST + 1, N_FIRST, 0, 0
            for b, (_, n, _) in enumerate(PANEL):
                done += 8 if n > 280 else 4
                while u < done + (AHEAD if b == len(PANEL) - 1 else 2):
                    lo_half(u)
                    u += 1
                    if (u - N_FIRST) % 4 == 0 and chunks < 4:
                        modulate(D // 256 + chunks)
                        chunks += 1
                    if (u - N_FIRST) % 4 == 3 and read < chunks and u - N_FIRST > 6:
                        gate_chunk(read)
                        read += 1
                dve.wait_ge(unit_used, done)
                for s in range(1, ST, 2):
                    panel_out(ST * b + s)
            while read < 4:
                gate_chunk(read)
                read += 1
            lo_half(u)
            dve.wait_ge(val_act, 2 * len(PANEL))
            dve.wait_ge(val_dve, 2 * len(PANEL))
            dve.wait_ge(misc_in, 80)
            for s in range(ST):
                ins = dve.tensor_tensor(fl[:, s, :], vals[:, s, PF:PF + HF], bf[:, :], ALU.add)
            fence(ins)
            dve.scalar_tensor_tensor(out=fe[:, :, :], in0=fl[:, :, :], scalar=-1.0, in1=fl[:, :, :],
                                     op0=ALU.mult, op1=ALU.max).then_inc(f_abs, 1)
            dve.wait_ge(gate_exp, 1)
            reciprocal_of_one_plus(gate[:, :, :], gate[:, :, :])
            fence(dve.tensor_scalar(gate[:, 0, 0:3 * HN:3], gate[:, 0, 0:3 * HN:3], anym, None, ALU.mult))
            fence(dve.tensor_scalar(fl[:, :, :], fl[:, :, :], 0.0, None, ALU.min))
            dve.wait_ge(f_ln, 1)
            dve.tensor_tensor(fl[:, :, :], fl[:, :, :], fe[:, :, :], ALU.subtract).then_inc(logf_done, 1)

            def tile_out(t):
                kind, i = TILES[t]
                src = ACC[t % 2][:, :]
                if kind in ("zn", "zf", "za"):
                    dve.wait_ge(z_exp, z_order.index(t) + 1)
                    reciprocal_of_one_plus(e_sb[:, :], e_sb[:, :])
                    dst = yT[:, y_of(kind, i), :]
                    if kind == "za":
                        fence(dve.tensor_tensor(e_sb[:, :], e_sb[:, :], conv_z[:, :], ALU.mult))
                    dve.tensor_tensor(dst, src, e_sb[:, :], ALU.mult).then_inc(tile_dve, 1)
                elif kind in ("kw", "u") and t < EARLY:
                    dve.wait_ge(unit_used, PARTS[t][1][2] + 1)
                    dve.tensor_tensor(partial(t), src, partial(t), ALU.add).then_inc(tile_dve, 1)
                    dve.wait_ge(*taken[t])
                elif kind == "gc":
                    dve.wait_ge(unit_used, PARTS[t][1][2] + 1)
                    dve.wait_ge(*taken[index["u", i]])
                    y0 = CW - 1
                    if t < EARLY:
                        fence(dve.tensor_tensor(partial(t), src, partial(t), ALU.add))
                        src = conv_y[:, y0:]
                    dve.tensor_tensor(conv_y[:, y0:], src, u_sb[:, :], ALU.mult).then_inc(tile_dve, 1)
                    dve.wait_ge(*taken[t])
                    w = [cols_a[:, R_CONV + j * CT + i:R_CONV + j * CT + i + 1] for j in range(CW)]
                    fence(dve.tensor_scalar(conv_z[:, :], conv_y[:, 0:S], w[0], None, ALU.mult))
                    for j in range(1, CW):
                        fence(dve.scalar_tensor_tensor(out=conv_z[:, :], in0=conv_y[:, j:j + S], scalar=w[j],
                                                       in1=conv_z[:, :], op0=ALU.mult, op1=ALU.add))
                elif kind == "gb":
                    dve.wait_ge(unit_used, PARTS[t][1][2] + 1)
                    dve.tensor_tensor(conv_z[:, :], src, conv_z[:, :], ALU.mult).then_inc(tile_dve, 1)
                    dve.wait_ge(*taken[t])

            def softmax_in(j):
                kind, h, _ = JOBS[j]
                dve.wait_ge(s_mm, j + 1)
                if j >= 1:
                    dve.wait_ge(t_mm, 2 * j)
                if kind == "fox":
                    dve.wait_ge(d_done, h + 1)
                else:
                    dve.wait_ge(bias_in[h % 2], 16 * (h // 2 + 1))
                for b in range(ST):
                    cs = slice(SO[b], SO[b] + SW[b])
                    bias = dbias[:, cs] if kind == "fox" else bias_t[:, h % 2, S - SW[b]:S]
                    ins = dve.tensor_tensor_reduce(prob[:, cs], SB[b][:, SBO[b]:SBO[b] + SW[b]], bias, 1.0, NEG,
                                                   ALU.add, ALU.max, mx[:, b:b + 1])
                fence(ins)
                if kind == "sel":
                    dve.wait_ge(bias_c_done, h + 1)
                    for b in range(ST):
                        ins = dve.tensor_tensor(pc[:, b, :], SC[b], bias_c[:, b, :], ALU.add)
                    fence(ins)
                dve.tensor_scalar(nmx[:, :], mx[:, :], -1.0, None, ALU.mult).then_inc(nmx_done, 1)
                if kind == "sel":
                    fence(dve.tensor_reduce(rr[:, :], pc[:, :, :], AX.X, ALU.max))
                    for b in range(ST):
                        ins = dve.tensor_scalar(pc[:, b, :], pc[:, b, :], rr[:, b:b + 1], None, ALU.subtract)
                    ins.then_inc(sc_sub, 1)

            def softmax_out(j):
                kind, h, _ = JOBS[j]
                dve.wait_ge(p_exp, j + 1)
                fence(dve.reciprocal(rr[:, :], ssum[:, :]))
                if kind != "fox":
                    g = 3 * h + {"sel": 1, "win": 2}[kind]
                    fence(dve.tensor_tensor(rr[:, :], rr[:, :], gate[:, :, g], ALU.mult))
                for b in range(ST):
                    cs = slice(SO[b], SO[b] + SW[b])
                    ins = dve.tensor_scalar(prob[:, cs], prob[:, cs], rr[:, b:b + 1], None, ALU.mult)
                ins.then_inc(p_done, 1)
                if kind == "sel":
                    dve.wait_ge(pc_exp, h + 1)
                    dve.wait_ge(p_done, j + 1)
                    fence(dve.tensor_reduce(rr[:, :], pc[:, :, :], AX.X, ALU.add))
                    fence(dve.reciprocal(rr[:, :], rr[:, :]))
                    fence(dve.tensor_tensor(rr[:, :], rr[:, :], gate[:, :, 3 * h], ALU.mult))
                    for b in range(ST):
                        ins = dve.tensor_scalar(pc[:, b, :], pc[:, b, :], rr[:, b:b + 1], None, ALU.mult)
                    ins.then_inc(pc_done, 1)

            def y_lo(i):
                k = OUT_ORDER[i]
                dve.wait_ge(yh_hi, i + 1)
                dve.tensor_tensor(h_lo[:, k, :], yT[:, k, :], h_hi[:, k, :].bitcast(F32), ALU.subtract).then_inc(y_ready, 1)

            for t in range(NT + 1):
                if t < NT:
                    lead = list(range(AT[t] + AHEAD + (t == 0), min(AT[t + 1] + AHEAD, NU)))
                    for u in lead[:len(lead) // 2]:
                        lo_half(u)
                if t == 2:
                    dve.wait_ge(cum_mm, 1)
                    dve.tensor_copy(cum[:, :, :], bank[7][:, 64:64 + ST * HF].rearrange("p (s h) -> p s h", s=ST))
                    fence(dve.tensor_copy(fe[:, :, :], bank[7][:, 96:96 + ST * HF].rearrange("p (s h) -> p s h", s=ST)))
                    for s in range(1, ST):
                        if s >= 2:
                            fence(dve.tensor_tensor(fe[:, s - 1, :], fe[:, s - 1, :], fe[:, s - 2, :], ALU.add))
                        ins = dve.tensor_tensor(cum[:, s, :], cum[:, s, :], fe[:, s - 1, :], ALU.add)
                    ins.then_inc(cum_done, 1)
                if t == 3:
                    dve.wait_ge(cumT_mm, 1)
                    dve.tensor_copy(cum_T[:, :], bank[7][0:HF * ST, P:2 * P]).then_inc(cumT_done, 1)
                if t == CMP_TILES:
                    dve.wait_ge(hid_exp, 1)
                    reciprocal_of_one_plus(hid[:, :, :], hid[:, :, :])
                    for w in range(2):
                        ins = dve.tensor_tensor(hid[:, w, :], bank[4 + w][0:2 * NC, 0:CMP_HID], hid[:, w, :], ALU.mult)
                    ins.then_inc(hid_done, 1)
                for j, (_, _, at_t) in enumerate(JOBS):
                    if t == at_t + 2:
                        dve.wait_ge(t_mm, 2 * j + 1)
                        dve.tensor_copy(probT[:, TO[1]:TO[2]], T1[:, 0:TW[1]]).then_inc(pT_dve, 1)
                if t >= 1:
                    tile_out(t - 1)
                if t == CMP_TILES + 1:
                    dve.wait_ge(kc_act, 1)
                    dve.tensor_copy(vcmp[:, :, :], bank[4][0:NC, P:P + KVG * HD].rearrange("p (g d) -> p g d", g=KVG)) \
                       .then_inc(kvcmp_done, 1)
                for j, (kind, g, at_t) in enumerate(JOBS):
                    if t == at_t + 3 and kind != "sel":
                        o = (j // 3) * 2 + (kind == "fox")
                        dve.wait_ge(o_mm, o + 1)
                        y = y_of("zf", g) if kind == "fox" else y_of("zn", g)
                        dve.wait_ge(*taken[index["zf" if kind == "fox" else "zn", g]])
                        dve.tensor_tensor(yT[:, y, :], OB[:, :], yT[:, y, :], ALU.mult).then_inc(o_done, 1)
                for j, (kind, g, at_t) in enumerate(JOBS):
                    if t == at_t + 1:
                        softmax_in(j)
                if t < NT:
                    for u in lead[len(lead) // 2:]:
                        lo_half(u)
                for j, (kind, g, at_t) in enumerate(JOBS):
                    if t == at_t + 1:
                        softmax_out(j)
                    if t == at_t + 2 and kind == "sel":
                        dve.wait_ge(t_mm, 2 * j + 2)
                        dve.tensor_copy(pcT[:, :], T1[0:NC, :]).then_inc(pcT_dve, 1)
                if t == CMP_TILES:
                    dve.wait_ge(hidT_mm, 1)
                    for w in range(2):
                        src = (T0, T1)[w][:, 0:2 * P].rearrange("p (j n) -> p j n", j=2)[:, :, 0:2 * NC]
                        ins = dve.tensor_copy(hidT[:, w, :, :], src)
                    ins.then_inc(hidT_done, 1)
                if t == NT - 1:
                    for i in range(Y_FIRST):
                        y_lo(i)
            u = AT[NT] + AHEAD
            for i in range(Y_FIRST, KT):
                y_lo(i)
                if i % 3 == 2 and u < AT[NT] + NSPLIT:
                    lo_half(u)
                    u += 1
            while u < AT[NT] + KT + 2:
                lo_half(u)
                u += 1
            dve.wait_ge(g_done, 1)
            for s in range(ST):
                dve.wait_ge(y_mm, 2 * s + 2) if s < ST - 1 else dve.wait_ge(unit_used, AT[NT] + KT)
                dve.tensor_copy(y_half[:, s, S:2 * S], YB[2 * s + 1][:, :]).then_inc(y_dve, 1)
            while u < NU:
                lo_half(u)
                u += 1
            for s in range(ST):
                if s >= 2:
                    dve.wait_ge(stored[s % 2], 32 * (s // 2))
                for n in range(2):
                    if n == 0:
                        dve.wait_ge(y_sq_a, s + 1)
                    else:
                        dve.wait_ge(y_sq, s + 1)
                        dve.tensor_reduce(tot[:, s:s + 1], sq[:, s, :], AX.X, ALU.add).then_inc(y_tot, 1)
                    cs = slice(D // 2 + n * S, D // 2 + (n + 1) * S)
                    ins = dve.tensor_tensor(fin[:, s % 2, cs], YB[2 * s + n][:, :], g_bc[:, cs], ALU.mult)
                fence(ins)
                dve.wait_ge(y_std, s + 1)
                fence(dve.reciprocal(rs3[:, s:s + 1], rs2[:, s:s + 1]))
                r = rs3[:, s:s + 1]
                dve.wait_ge(xa_in[s % 2], 16 * (s // 2 + 1))
                dve.wait_ge(yg_done, s + 1)
                for i in range(STORES[s]):
                    n = D // STORES[s]
                    cs = slice(i * n, (i + 1) * n)
                    src = y_half[:, s, cs] if i < STORES[s] // 2 else fin[:, s % 2, cs]
                    dve.scalar_tensor_tensor(out=fin[:, s % 2, cs], in0=src, scalar=r, in1=x_again[:, s % 2, cs],
                                             op0=ALU.mult, op1=ALU.add).then_inc(fin_done, 1)

        @block.gpsimd
        def _(pool):
            seq = [0]

            def fence(ins):
                seq[0] += 1
                ins.then_inc(pool_seq, 1)
                pool.wait_ge(pool_seq, seq[0])

            def lo_half(u):
                pool.wait_ge(hi_done, u + 1)
                hi, lo = split(u)
                pool.tensor_tensor(lo, w_raw[:, u % NRAW, 0:UNITS[u][2]], hi.bitcast(F32),
                                   ALU.subtract).then_inc(first_lo, 1)

            for k in range(KT):
                if k % 2 == 0:
                    lo_half(FIRST_AT[k])
                    units = range(FIRST_AT[k] + 1, late_from(k // 2))
                elif late_from(k // 2) <= FIRST_AT[k]:
                    units = range(late_from(k // 2), FIRST_AT[k] + 1)
                else:
                    units = []
                pool.wait_ge(h_rounded, k + 1)
                pool.tensor_tensor(h_lo[:, k, :], xmix[:, k % 2, :], h_hi[:, k, :].bitcast(F32), ALU.subtract) \
                    .then_inc(h_ready, 1)
                for u in units:
                    lo_half(u)
            pool.wait_ge(first_act, 3)
            pool.wait_ge(first_dve, 3)
            fence(pool.memset(blk_hi[:, :, :, 2 * NC:].bitcast(F32), 0.0))
            fence(pool.memset(blk_lo[:, :, :, 2 * NC:].bitcast(F32), 0.0))
            for q in range(16):
                if q == 2:
                    for i in range(4):
                        pool.wait_ge(mod_read, D // 256 + i + 1)
                        pool.dma_start(gate_dram[:, i * S:(i + 1) * S], (pcT, sq_out)[i % 2][0:1, :]) \
                            .then_inc(row_out[i % 2], 16)
                    for slot in range(2):
                        pool.wait_ge(row_out[slot], 32)
                w, l0 = q // 8, q % 8 * 4
                a, r = divmod(l0, CMP_STRIDE)
                kv = kvc[:, 2 * w:2 * w + 2, :].rearrange("p g (n s) -> p s g n", s=CMP_STRIDE)
                pos = pe_cols[:, w, l0:l0 + 4].rearrange("p (l g n) -> p l g n", g=1, n=1).to_broadcast([P, 4, 2, NC])
                pool.tensor_tensor(blk[:, :, :].rearrange("p l (g n) -> p l g n", g=2), kv[:, r:r + 4, :, a:a + NC],
                                   pos, ALU.add)
                if q >= 2:
                    pool.wait_ge(unit_used, CMP_AT[q - 2] + 1)
                fence(pool.tensor_tensor(blk_hi[:, q % 2, :, 0:2 * NC].rearrange("p l (g n) -> p l g n", g=2),
                                         kv[:, r:r + 4, :, a:a + NC], pos, ALU.add))
                pool.tensor_tensor(blk_lo[:, q % 2, :, 0:2 * NC], blk[:, :, :],
                                   blk_hi[:, q % 2, :, 0:2 * NC].bitcast(F32), ALU.subtract).then_inc(blk_done, 1)
                pool.wait_ge(blk_done, q + 1)
            for g in range(HN):
                pool.wait_ge(bias_in[g % 2], 16 * (g // 2 + 1))
                if g >= 1:
                    pool.wait_ge(nmx_done, 3 * (g - 1) + 1)
                fence(pool.memset(bias_c[:, :, :], NEG))
                for b in range(ST):
                    n = min(NC, (P // CMP_STRIDE) * (b + 1) - 1)
                    u0 = S - (b + 1) * P + CMP_LEN - 1
                    ins = pool.tensor_copy(bias_c[:, b, 0:n],
                                           bias_t[:, g % 2, u0:u0 + (n - 1) * CMP_STRIDE + 1:CMP_STRIDE])
                ins.then_inc(bias_c_done, 1)
                pool.wait_ge(d_act, g + 1)
                for b in range(ST):
                    o = SO[b] + b * P
                    ins = pool.affine_select(out=dbias[:, o:o + P], in_=dbias[:, o:o + P], compare_op=ALU.is_ge,
                                             fill=NEG, base=0, pattern=[[-1, P]], channel_multiplier=1)
                ins.then_inc(d_done, 1)
            pool.wait_ge(g_in, 48)
            fence(pool.tensor_tensor(g_bc[:, :], g_bc[:, :], y_half[:, 0:2, :].rearrange("p s n -> p (s n)"), ALU.add))
            pool.tensor_tensor(g_bc[:, :], g_bc[:, :], y_half[:, 2:4, :].rearrange("p s n -> p (s n)"),
                               ALU.mult).then_inc(g_done, 1)
            pool.wait_ge(g_done, 1)
            for s in range(ST):
                pool.wait_ge(yh_sq, s + 1)
                pool.tensor_tensor(y_half[:, s, :], y_half[:, s, :], g_bc[:, 0:D // 2], ALU.mult).then_inc(yg_done, 1)


def bias_buckets():
    half = BUCKETS // 2
    dist = np.arange(S - 1, -1, -1)
    far = np.maximum(dist, half).astype(np.float32)
    large = half + (np.log(far / np.float32(half)) / np.float32(np.log(MAX_DIST / half))
                    * np.float32(BUCKETS - half)).astype(np.int32)
    bucket = np.where(dist < half, dist, np.minimum(large, BUCKETS - 1))
    return (np.arange(BUCKETS)[:, None] == bucket[None, :]).astype(np.float32)


def shape_constants():
    i = np.arange(P)
    return np.concatenate([np.eye(P), i[:, None] <= i[None, :], np.ones((P, P)),
                           i[:, None] >= CMP_LEN - 1], axis=1).astype(np.float32)


_INS = ["x", "c", "w_ada", "b_ada", "pre_norm", "post_norm", "w_in", "b_forget", "conv_w", "cmp_pe_k",
        "cmp_w1_k", "cmp_w2_k", "cmp_pe_v", "cmp_w1_v", "cmp_w2_v", "w_out", "rel_bias"]


def kernel(**inputs):
    import concourse.bacc as bacc
    from concourse.bass_utils import run_bass_kernel_spmd

    nc = bacc.Bacc("TRN2", target_bir_lowering=False, num_devices=1, dynamic_dma_scratch_size=1024)
    arrays = {name: np.ascontiguousarray(inputs[name]) for name in _INS}
    arrays["consts"], arrays["onehot"] = shape_constants(), bias_buckets()
    args = [nc.dram_tensor(name, a.shape, mybir.dt.from_np(a.dtype), kind="ExternalInput").ap()
            for name, a in arrays.items()]
    out = nc.dram_tensor("out", [1, S, D], F32, kind="ExternalOutput").ap()
    layer_program(nc, *args, out)
    r = run_bass_kernel_spmd(nc, [arrays], core_ids=[0])
    return r.results[0]["out"]
```
